# Optimizing a Trainium2 kernel written in Bass

```python
import jax, jax.numpy as jnp
from jax import lax
import numpy as np

D_MODEL = 1024
BATCH = 1
SEQ = 512
DEPTH = 1

CHUNK = 64
D_MIX = D_MODEL
LRU_WIDTH = D_MIX // 4
LRU_HEADS = 4
LRU_HEAD_DIM = LRU_WIDTH // LRU_HEADS
CONV_WIDTH = 4
LRU_C = 8.0
FOX_WIDTH = D_MIX // 2
FOX_HEAD_DIM = 64
FOX_HEADS = FOX_WIDTH // FOX_HEAD_DIM
Q_BLOCK = 128
RWKV_WIDTH = D_MIX - LRU_WIDTH - FOX_WIDTH
RWKV_HEAD_DIM = 64
RWKV_HEADS = RWKV_WIDTH // RWKV_HEAD_DIM
DECAY_RANK = 32
AAA_RANK = 32
GATE_RANK = 64
N_GROUPS = 4
EXPERTS_PER_GROUP = 4
N_EXPERTS = N_GROUPS * EXPERTS_PER_GROUP
TOP_K = 2
D_EXPERT = 256
NORM_EPS = 1e-6
GN_EPS = 64e-5
LRU_COLS = 2 * LRU_WIDTH
FOX_COLS = 3 * FOX_WIDTH + FOX_HEADS
RWKV_COLS = 3 * RWKV_WIDTH + DECAY_RANK + AAA_RANK + GATE_RANK
D_IN = LRU_COLS + FOX_COLS + RWKV_COLS


def rms_norm(x, g, eps=NORM_EPS):
    xf = x.astype(jnp.float32)
    y = xf * lax.rsqrt(jnp.mean(xf * xf, axis=-1, keepdims=True) + eps)
    return (y * g.astype(jnp.float32)).astype(x.dtype)

def rglru_group(x_in, gate_in, conv_w, conv_b, wa, ba, wx, bx, lam, norm_g):
    f32 = jnp.float32
    B, S, W = x_in.shape
    xp = jnp.pad(x_in, ((0, 0), (CONV_WIDTH - 1, 0), (0, 0)))
    xc = conv_b + sum(xp[:, j:j + S] * conv_w[j] for j in range(CONV_WIDTH))
    xh = xc.reshape(B, S, LRU_HEADS, LRU_HEAD_DIM)
    r = jax.nn.sigmoid((jnp.einsum('bshi,hij->bshj', xh, wa).reshape(B, S, W) + ba).astype(f32))
    i = jax.nn.sigmoid((jnp.einsum('bshi,hij->bshj', xh, wx).reshape(B, S, W) + bx).astype(f32))
    log_a = -LRU_C * r * jax.nn.softplus(-lam.astype(f32))
    a = jnp.exp(log_a)
    b = jnp.sqrt(-jnp.expm1(2.0 * log_a)) * (i * xc.astype(f32))

    def combine(left, right):
        a1, b1 = left
        a2, b2 = right
        return a1 * a2, a2 * b1 + b2

    _, h = lax.associative_scan(combine, (a, b), axis=1)
    y = jax.nn.gelu(gate_in.astype(f32)) * h
    return rms_norm(y.astype(x_in.dtype), norm_g)

def fox_group(q, k, v, f_logit, fb, qn_g, kn_g, norm_g):
    f32 = jnp.float32
    B, S, _ = q.shape
    H, Dh = FOX_HEADS, FOX_HEAD_DIM
    qh = rms_norm(q.reshape(B, S, H, Dh), qn_g).transpose(0, 2, 1, 3)
    kh = rms_norm(k.reshape(B, S, H, Dh), kn_g).transpose(0, 2, 1, 3)
    vh = v.reshape(B, S, H, Dh).transpose(0, 2, 1, 3)
    log_f = jax.nn.log_sigmoid((f_logit + fb).astype(f32))
    c = jnp.cumsum(log_f, axis=1).transpose(0, 2, 1)
    nb = S // Q_BLOCK
    q_blocks = qh.reshape(B, H, nb, Q_BLOCK, Dh).transpose(2, 0, 1, 3, 4)
    c_blocks = c.reshape(B, H, nb, Q_BLOCK).transpose(2, 0, 1, 3)
    starts = jnp.arange(nb, dtype=jnp.int32) * Q_BLOCK
    k_pos = jnp.arange(S, dtype=jnp.int32)
    scale = FOX_HEAD_DIM ** -0.5

    def block(args):
        qb, cb, s0 = args
        s = jnp.einsum('bhqd,bhkd->bhqk', qb, kh).astype(f32) * scale
        s = s + cb[..., None] - c[:, :, None, :]
        q_pos = s0 + jnp.arange(Q_BLOCK, dtype=jnp.int32)
        mask = k_pos[None, :] <= q_pos[:, None]
        p = jax.nn.softmax(jnp.where(mask, s, -jnp.inf), axis=-1)
        return jnp.einsum('bhqk,bhkd->bhqd', p.astype(vh.dtype), vh)

    o = lax.map(block, (q_blocks, c_blocks, starts))
    o = o.transpose(1, 0, 3, 2, 4).reshape(B, S, FOX_WIDTH)
    return rms_norm(o.astype(q.dtype), norm_g)

def rwkv7_group(p, mu, w0, w2, a0, a2, g2, k_k, k_a, r_k, ln_g, ln_b):
    f32 = jnp.float32
    B, S, _ = p.shape
    H, N = RWKV_HEADS, RWKV_HEAD_DIM
    prev = jnp.pad(p, ((0, 0), (1, 0), (0, 0)))[:, :-1]
    p = p + (prev - p) * mu
    o1 = RWKV_WIDTH
    o2 = 2 * RWKV_WIDTH
    o3 = 3 * RWKV_WIDTH
    o4 = o3 + DECAY_RANK
    o5 = o4 + AAA_RANK
    r, k, v, wd, ad, gd = jnp.split(p, [o1, o2, o3, o4, o5], axis=-1)
    r = r.astype(f32)
    k = k.astype(f32)
    v = v.astype(f32)
    w = -jax.nn.softplus(-(w0 + jnp.tanh(wd) @ w2).astype(f32)) - 0.5
    decay = jnp.exp(-jnp.exp(w))
    a = jax.nn.sigmoid((a0 + ad @ a2).astype(f32))
    g = (jax.nn.sigmoid(gd) @ g2).astype(f32)

    def heads(t):
        return t.reshape(B, S, H, N)

    kk = heads(k * k_k)
    kk = kk / jnp.maximum(jnp.sqrt(jnp.sum(kk * kk, axis=-1, keepdims=True)), 1e-12)
    k = k * (1.0 + (a - 1.0) * k_a)
    rh, wh, kh, vh, ah = heads(r), heads(decay), heads(k), heads(v), heads(a)
    n_chunks = S // CHUNK

    def to_chunks(t):
        return t.transpose(1, 0, 2, 3).reshape(n_chunks, CHUNK, B, H, N)

    xs = (to_chunks(rh), to_chunks(wh), to_chunks(kh), to_chunks(vh), to_chunks(kk), to_chunks(kk * ah))

    def frame_step(state, inp):
        r_t, w_t, k_t, v_t, kk_t, b_t = inp
        sa = jnp.einsum('bhvk,bhk->bhv', state, -kk_t)
        state = (state * w_t[:, :, None, :] + sa[..., None] * b_t[:, :, None, :]
                 + v_t[..., None] * k_t[:, :, None, :])
        return state, jnp.einsum('bhvk,bhk->bhv', state, r_t)

    def chunk_step(state, chunk):
        return lax.scan(frame_step, state, chunk)

    state0 = jnp.zeros((B, H, N, N), f32)
    _, o = lax.scan(chunk_step, state0, xs)
    o = o.reshape(S, B, H, N).transpose(1, 0, 2, 3)
    mean = jnp.mean(o, axis=-1, keepdims=True)
    var = jnp.mean(jnp.square(o - mean), axis=-1, keepdims=True)
    o = ((o - mean) * lax.rsqrt(var + GN_EPS)).reshape(B, S, RWKV_WIDTH) * ln_g + ln_b
    bonus = jnp.sum(rh * kh * r_k, axis=-1, keepdims=True) * vh
    return (o + bonus.reshape(B, S, RWKV_WIDTH)) * g

def hier_moe(x, wg, bg, we, be, w_gate, w_up, w_down):
    f32 = jnp.float32
    B, S, D = x.shape
    t = x.reshape(B * S, D)
    g_probs = jax.nn.softmax((t @ wg).astype(f32) + bg, axis=-1)
    g_p, g_idx = lax.top_k(g_probs, 1)
    e_logits = ((t @ we).astype(f32) + be).reshape(-1, N_GROUPS, EXPERTS_PER_GROUP)
    sel = jax.nn.one_hot(g_idx[:, 0], N_GROUPS, dtype=f32)
    e_logits = jnp.einsum('tg,tge->te', sel, e_logits)
    e_p, e_idx = lax.top_k(jax.nn.softmax(e_logits, axis=-1), TOP_K)
    e_p = e_p / jnp.sum(e_p, axis=-1, keepdims=True)
    weights = g_p * e_p
    ids = g_idx * EXPERTS_PER_GROUP + e_idx
    combine = jnp.sum(jax.nn.one_hot(ids, N_EXPERTS, dtype=f32) * weights[..., None], axis=1)
    hid = jax.nn.silu(jnp.einsum('td,edf->tef', t, w_gate)) * jnp.einsum('td,edf->tef', t, w_up)
    hid = hid * combine[..., None].astype(hid.dtype)
    y = jnp.einsum('tef,efd->td', hid, w_down)
    return y.reshape(B, S, D).astype(x.dtype)

def first_inputs(seed: int = 0) -> dict:
    key = jax.random.key(seed)
    ks = iter(jax.random.split(key, 40))
    L = DEPTH

    def nrm(shape, scale):
        return jax.random.normal(next(ks), shape, jnp.float32) * scale

    def uni(shape, lo, hi):
        return jax.random.uniform(next(ks), shape, jnp.float32, lo, hi)

    x = nrm((BATCH, SEQ, D_MODEL), 1.0)
    norm1_g = 1.0 + nrm((L, D_MODEL), 0.02)
    w_in = nrm((L, D_MODEL, D_IN), D_MODEL ** -0.5)
    conv_w = nrm((L, CONV_WIDTH, LRU_WIDTH), CONV_WIDTH ** -0.5)
    conv_b = nrm((L, LRU_WIDTH), 0.01)
    lru_wa = nrm((L, LRU_HEADS, LRU_HEAD_DIM, LRU_HEAD_DIM), LRU_HEAD_DIM ** -0.5)
    lru_ba = nrm((L, LRU_WIDTH), 0.01)
    lru_wx = nrm((L, LRU_HEADS, LRU_HEAD_DIM, LRU_HEAD_DIM), LRU_HEAD_DIM ** -0.5)
    lru_bx = nrm((L, LRU_WIDTH), 0.01)
    a_pow = uni((L, LRU_WIDTH), 0.9, 0.999)
    s = a_pow ** (1.0 / LRU_C)
    lru_lambda = jnp.log(s) - jnp.log1p(-s)
    lru_norm_g = 1.0 + nrm((L, LRU_WIDTH), 0.02)
    fox_fb = uni((L, FOX_HEADS), 1.0, 5.0)
    fox_qnorm_g = 1.0 + nrm((L, FOX_HEAD_DIM), 0.02)
    fox_knorm_g = 1.0 + nrm((L, FOX_HEAD_DIM), 0.02)
    fox_norm_g = 1.0 + nrm((L, FOX_WIDTH), 0.02)
    rwkv_mu = uni((L, RWKV_COLS), 0.0, 1.0)
    rwkv_w0 = uni((L, RWKV_WIDTH), -4.0, 0.0)
    rwkv_w2 = nrm((L, DECAY_RANK, RWKV_WIDTH), 0.1 * DECAY_RANK ** -0.5)
    rwkv_a0 = nrm((L, RWKV_WIDTH), 0.1)
    rwkv_a2 = nrm((L, AAA_RANK, RWKV_WIDTH), 0.5 * AAA_RANK ** -0.5)
    rwkv_g2 = nrm((L, GATE_RANK, RWKV_WIDTH), GATE_RANK ** -0.5)
    rwkv_kk = 0.85 + nrm((L, RWKV_WIDTH), 0.05)
    rwkv_ka = 1.0 + nrm((L, RWKV_WIDTH), 0.05)
    rwkv_rk = nrm((L, RWKV_HEADS, RWKV_HEAD_DIM), 0.1)
    rwkv_ln_g = 1.0 + nrm((L, RWKV_WIDTH), 0.02)
    rwkv_ln_b = nrm((L, RWKV_WIDTH), 0.01)
    w_out = nrm((L, D_MIX, D_MODEL), D_MIX ** -0.5)
    norm2_g = 1.0 + nrm((L, D_MODEL), 0.02)
    router_gw = nrm((L, D_MODEL, N_GROUPS), D_MODEL ** -0.5)
    router_gb = nrm((L, N_GROUPS), 0.01)
    router_ew = nrm((L, D_MODEL, N_EXPERTS), D_MODEL ** -0.5)
    router_eb = nrm((L, N_EXPERTS), 0.01)
    exp_w_gate = nrm((L, N_EXPERTS, D_MODEL, D_EXPERT), D_MODEL ** -0.5)
    exp_w_up = nrm((L, N_EXPERTS, D_MODEL, D_EXPERT), D_MODEL ** -0.5)
    exp_w_down = nrm((L, N_EXPERTS, D_EXPERT, D_MODEL), D_EXPERT ** -0.5)
    return {'x': x, 'norm1_g': norm1_g, 'w_in': w_in, 'conv_w': conv_w, 'conv_b': conv_b,
            'lru_wa': lru_wa, 'lru_ba': lru_ba, 'lru_wx': lru_wx, 'lru_bx': lru_bx,
            'lru_lambda': lru_lambda, 'lru_norm_g': lru_norm_g, 'fox_fb': fox_fb,
            'fox_qnorm_g': fox_qnorm_g, 'fox_knorm_g': fox_knorm_g, 'fox_norm_g': fox_norm_g,
            'rwkv_mu': rwkv_mu, 'rwkv_w0': rwkv_w0, 'rwkv_w2': rwkv_w2, 'rwkv_a0': rwkv_a0,
            'rwkv_a2': rwkv_a2, 'rwkv_g2': rwkv_g2, 'rwkv_kk': rwkv_kk, 'rwkv_ka': rwkv_ka,
            'rwkv_rk': rwkv_rk, 'rwkv_ln_g': rwkv_ln_g, 'rwkv_ln_b': rwkv_ln_b, 'w_out': w_out,
            'norm2_g': norm2_g, 'router_gw': router_gw, 'router_gb': router_gb,
            'router_ew': router_ew, 'router_eb': router_eb, 'exp_w_gate': exp_w_gate,
            'exp_w_up': exp_w_up, 'exp_w_down': exp_w_down}

def first_block(x, norm1_g, w_in, conv_w, conv_b, lru_wa, lru_ba, lru_wx, lru_bx, lru_lambda,
              lru_norm_g, fox_fb, fox_qnorm_g, fox_knorm_g, fox_norm_g, rwkv_mu, rwkv_w0,
              rwkv_w2, rwkv_a0, rwkv_a2, rwkv_g2, rwkv_kk, rwkv_ka, rwkv_rk, rwkv_ln_g,
              rwkv_ln_b, w_out, norm2_g, router_gw, router_gb, router_ew, router_eb,
              exp_w_gate, exp_w_up, exp_w_down):
    splits = [LRU_WIDTH, LRU_COLS, LRU_COLS + FOX_WIDTH, LRU_COLS + 2 * FOX_WIDTH,
              LRU_COLS + 3 * FOX_WIDTH, LRU_COLS + FOX_COLS]
    for l in range(DEPTH):
        h = rms_norm(x, norm1_g[l])
        proj = h @ w_in[l]
        xa, ga, q, k, v, fl, pc = jnp.split(proj, splits, axis=-1)
        ya = rglru_group(xa, ga, conv_w[l], conv_b[l], lru_wa[l], lru_ba[l], lru_wx[l],
                         lru_bx[l], lru_lambda[l], lru_norm_g[l])
        yb = fox_group(q, k, v, fl, fox_fb[l], fox_qnorm_g[l], fox_knorm_g[l], fox_norm_g[l])
        yc = rwkv7_group(pc, rwkv_mu[l], rwkv_w0[l], rwkv_w2[l], rwkv_a0[l], rwkv_a2[l],
                         rwkv_g2[l], rwkv_kk[l], rwkv_ka[l], rwkv_rk[l], rwkv_ln_g[l], rwkv_ln_b[l])
        y = jnp.concatenate([ya, yb.astype(x.dtype), yc.astype(x.dtype)], axis=-1)
        x = x + (y @ w_out[l]).astype(x.dtype)
        x = x + hier_moe(rms_norm(x, norm2_g[l]), router_gw[l], router_gb[l], router_ew[l],
                         router_eb[l], exp_w_gate[l], exp_w_up[l], exp_w_down[l])
    return x


DEPTH_2 = 2

CHUNK_2 = 128
RET_HEADS = 4
RET_QK_DIM = 128
RET_V_DIM = 256
RET_QK_WIDTH = RET_HEADS * RET_QK_DIM
RET_V_WIDTH = RET_HEADS * RET_V_DIM
GMLP_GROUPS = 4
GMLP_WIDTH = D_MODEL
GMLP_GROUP_DIM = GMLP_WIDTH // GMLP_GROUPS
POOL_WINDOWS = (2, 4, 8, 16)
POOL_GROUPS = 4
POOL_WIDTH = D_MODEL
POOL_GROUP_DIM = POOL_WIDTH // POOL_GROUPS
N_BRANCH = 3
BRANCH_WIDTH = D_MODEL
D_FF = 4 * D_MODEL
N_MOD = 6
ROPE_BASE = 10000.0
EPS = 1e-6
SPLITS = (RET_QK_WIDTH, RET_QK_WIDTH, RET_V_WIDTH, RET_V_WIDTH,
          GMLP_WIDTH, GMLP_WIDTH, POOL_WIDTH, N_BRANCH * D_MODEL)
D_IN_2 = 2 * RET_QK_WIDTH + 2 * RET_V_WIDTH + 2 * GMLP_WIDTH + POOL_WIDTH + N_BRANCH * D_MODEL


def rms_norm_2(x, gain=None):
    xf = x.astype(jnp.float32)
    y = xf * lax.rsqrt(jnp.mean(xf * xf, axis=-1, keepdims=True) + EPS)
    if gain is not None:
        y = y * gain.astype(jnp.float32)
    return y.astype(x.dtype)

def split_columns(proj):
    pieces, start = [], 0
    for w in SPLITS:
        pieces.append(proj[..., start:start + w])
        start += w
    return pieces

def rotary(x, positions):
    half = x.shape[-1] // 2
    inv_freq = ROPE_BASE ** (-jnp.arange(half, dtype=jnp.float32) / half)
    ang = positions.astype(jnp.float32)[:, :, None] * inv_freq
    cos = jnp.cos(ang)[:, :, None, :]
    sin = jnp.sin(ang)[:, :, None, :]
    xf = x.astype(jnp.float32)
    x1, x2 = xf[..., :half], xf[..., half:]
    return jnp.concatenate([x1 * cos - x2 * sin, x2 * cos + x1 * sin], axis=-1).astype(x.dtype)

def retention(q, k, v, g, positions):
    B, S, _ = q.shape
    nc = S // CHUNK_2
    dt = q.dtype
    q = rotary(q.reshape(B, S, RET_HEADS, RET_QK_DIM), positions)
    k = rotary(k.reshape(B, S, RET_HEADS, RET_QK_DIM), positions) * (RET_QK_DIM ** -0.5)
    v = v.reshape(B, S, RET_HEADS, RET_V_DIM)
    log_gamma = jnp.log1p(-jnp.power(2.0, -5.0 - jnp.arange(RET_HEADS, dtype=jnp.float32)))
    pos = jnp.arange(CHUNK_2, dtype=jnp.float32)
    rel = pos[:, None] - pos[None, :]
    causal = rel >= 0
    decay_intra = jnp.where(causal[None],
                            jnp.exp(log_gamma[:, None, None] * jnp.where(causal, rel, 0.0)[None]),
                            0.0)
    decay_q = jnp.exp(log_gamma[:, None] * (pos + 1.0)[None])
    decay_k = jnp.exp(log_gamma[:, None] * (CHUNK_2 - 1.0 - pos)[None])
    decay_chunk = jnp.exp(log_gamma * CHUNK_2)

    qc = q.reshape(B, nc, CHUNK_2, RET_HEADS, RET_QK_DIM)
    kc = k.reshape(B, nc, CHUNK_2, RET_HEADS, RET_QK_DIM)
    vc = v.reshape(B, nc, CHUNK_2, RET_HEADS, RET_V_DIM)
    scores = jnp.einsum('bnihd,bnjhd->bnhij', qc, kc) * decay_intra.astype(dt)
    intra = jnp.einsum('bnhij,bnjhe->bnihe', scores, vc)
    kv = jnp.einsum('bnjhd,hj,bnjhe->nbhde', kc, decay_k.astype(dt), vc).astype(jnp.float32)

    def step(state, kv_n):
        return decay_chunk[None, :, None, None] * state + kv_n, state

    _, prev = lax.scan(step, jnp.zeros((B, RET_HEADS, RET_QK_DIM, RET_V_DIM), jnp.float32), kv)
    cross = jnp.einsum('bnihd,hi,nbhde->bnihe', qc, decay_q.astype(dt), prev.astype(dt))
    o = (intra + cross).reshape(B, S, RET_HEADS, RET_V_DIM)
    o = rms_norm_2(o).reshape(B, S, RET_V_WIDTH)
    return jax.nn.silu(g) * o

def spatial_gating(u, v, w_s, b_s, v_gain):
    B, S, _ = u.shape
    nc = S // CHUNK_2
    u = jax.nn.gelu(u)
    v = rms_norm_2(jax.nn.gelu(v), v_gain)
    vc = v.reshape(B, nc, CHUNK_2, GMLP_GROUPS, GMLP_GROUP_DIM)
    mask = jnp.tril(jnp.ones((CHUNK_2, CHUNK_2), dtype=bool))
    w = jnp.where(mask[None], w_s, jnp.zeros_like(w_s))
    mixed = jnp.einsum('gts,bnsgc->bntgc', w, vc) + b_s.T[None, None, :, :, None]
    return u * mixed.reshape(B, S, GMLP_WIDTH)

def multiscale_pool(p, w_pool, b_pool, scale):
    B, S, _ = p.shape
    pg = p.reshape(B, S, POOL_GROUPS, POOL_GROUP_DIM).astype(jnp.float32)
    cs = jnp.concatenate([jnp.zeros((B, 1, POOL_GROUPS, POOL_GROUP_DIM), jnp.float32),
                          jnp.cumsum(pg, axis=1)], axis=1)
    t = jnp.arange(1, S + 1)
    outs = []
    for gi, w in enumerate(POOL_WINDOWS):
        start = jnp.maximum(t - w, 0)
        window_sum = cs[:, 1:, gi] - cs[:, start, gi]
        count = jnp.minimum(t, w).astype(jnp.float32)[None, :, None]
        outs.append(window_sum / count - pg[:, :, gi])
    pooled = jnp.stack(outs, axis=2).astype(p.dtype)
    mixed = jnp.einsum('bsgc,gce->bsge', pooled, w_pool) + b_pool[None, None]
    return mixed.reshape(B, S, POOL_WIDTH) * scale

def second_inputs(seed: int = 0) -> dict:
    key = jax.random.key(seed)
    ks = jax.random.split(key, 20)
    f32 = jnp.float32
    nrm = lambda k, shape, s: jax.random.normal(k, shape, f32) * s
    return {
        "x": nrm(ks[0], (BATCH, SEQ, D_MODEL), 1.0),
        "c": nrm(ks[1], (BATCH, D_MODEL), 1.0),
        "positions": jnp.broadcast_to(jnp.arange(SEQ, dtype=jnp.int32), (BATCH, SEQ)),
        "w_ada": nrm(ks[2], (DEPTH_2, D_MODEL, N_MOD * D_MODEL), 0.5 * D_MODEL ** -0.5),
        "b_ada": nrm(ks[3], (DEPTH_2, N_MOD * D_MODEL), 0.01),
        "norm1": 1.0 + nrm(ks[4], (DEPTH_2, D_MODEL), 0.02),
        "norm2": 1.0 + nrm(ks[5], (DEPTH_2, D_MODEL), 0.02),
        "w_in": nrm(ks[6], (DEPTH_2, D_MODEL, D_IN_2), D_MODEL ** -0.5),
        "ws_gmlp": nrm(ks[7], (DEPTH_2, GMLP_GROUPS, CHUNK_2, CHUNK_2), CHUNK_2 ** -0.5),
        "bs_gmlp": 1.0 + nrm(ks[8], (DEPTH_2, GMLP_GROUPS, CHUNK_2), 0.1),
        "vnorm_gmlp": 1.0 + nrm(ks[9], (DEPTH_2, GMLP_WIDTH), 0.02),
        "w_pool": nrm(ks[10], (DEPTH_2, POOL_GROUPS, POOL_GROUP_DIM, POOL_GROUP_DIM), POOL_GROUP_DIM ** -0.5),
        "b_pool": nrm(ks[11], (DEPTH_2, POOL_GROUPS, POOL_GROUP_DIM), 0.01),
        "pool_scale": 1.0 + nrm(ks[12], (DEPTH_2, POOL_WIDTH), 0.1),
        "w_branch": nrm(ks[13], (DEPTH_2, N_BRANCH, BRANCH_WIDTH, D_MODEL), BRANCH_WIDTH ** -0.5),
        "w_out": nrm(ks[14], (DEPTH_2, D_MODEL, D_MODEL), D_MODEL ** -0.5),
        "w_ff1": nrm(ks[15], (DEPTH_2, D_MODEL, D_FF), D_MODEL ** -0.5),
        "w_ff2": nrm(ks[16], (DEPTH_2, D_FF, D_MODEL), D_FF ** -0.5),
        "final_norm": 1.0 + nrm(ks[17], (D_MODEL,), 0.02),
    }

def second_block(x, c, positions, w_ada, b_ada, norm1, norm2, w_in, ws_gmlp, bs_gmlp, vnorm_gmlp,
              w_pool, b_pool, pool_scale, w_branch, w_out, w_ff1, w_ff2, final_norm):
    B, S, _ = x.shape
    c_act = jax.nn.silu(c)
    for l in range(DEPTH_2):
        mod = c_act @ w_ada[l] + b_ada[l]
        sh1, sc1, gt1, sh2, sc2, gt2 = [m[:, None, :] for m in jnp.split(mod, N_MOD, axis=-1)]

        h = rms_norm_2(x, norm1[l]) * (1.0 + sc1) + sh1
        proj = h @ w_in[l]
        q, k, v, g, u, vs, p, gate_cols = split_columns(proj)
        y_ret = retention(q, k, v, g, positions)
        y_sgu = spatial_gating(u, vs, ws_gmlp[l], bs_gmlp[l], vnorm_gmlp[l])
        y_pool = multiscale_pool(p, w_pool[l], b_pool[l], pool_scale[l])
        branches = jnp.stack([y_ret, y_sgu, y_pool], axis=2)
        branch_proj = jnp.einsum('bsnc,ncd->bsnd', branches, w_branch[l])
        gates = jax.nn.sigmoid(gate_cols.reshape(B, S, N_BRANCH, D_MODEL))
        merged = jnp.sum(gates * branch_proj, axis=2)
        x = x + gt1 * (merged @ w_out[l])

        h2 = rms_norm_2(x, norm2[l]) * (1.0 + sc2) + sh2
        hidden = jnp.square(jax.nn.relu(h2 @ w_ff1[l]))
        x = x + gt2 * (hidden @ w_ff2[l])
    return rms_norm_2(x, final_norm)


def setup_inputs(seed=0):
    out = dict(first_inputs(seed))
    for name, value in second_inputs(seed + 1).items():
        if name != "x":
            out[name + "_2"] = value
    return out


def reference(
    x, norm1_g, w_in, conv_w, conv_b, lru_wa, lru_ba, lru_wx, lru_bx, lru_lambda, lru_norm_g,
    fox_fb, fox_qnorm_g, fox_knorm_g, fox_norm_g, rwkv_mu, rwkv_w0, rwkv_w2, rwkv_a0, rwkv_a2,
    rwkv_g2, rwkv_kk, rwkv_ka, rwkv_rk, rwkv_ln_g, rwkv_ln_b, w_out, norm2_g, router_gw,
    router_gb, router_ew, router_eb, exp_w_gate, exp_w_up, exp_w_down, c_2, positions_2,
    w_ada_2, b_ada_2, norm1_2, norm2_2, w_in_2, ws_gmlp_2, bs_gmlp_2, vnorm_gmlp_2, w_pool_2,
    b_pool_2, pool_scale_2, w_branch_2, w_out_2, w_ff1_2, w_ff2_2, final_norm_2,
):
    x = first_block(
        x, norm1_g, w_in, conv_w, conv_b, lru_wa, lru_ba, lru_wx, lru_bx, lru_lambda,
        lru_norm_g, fox_fb, fox_qnorm_g, fox_knorm_g, fox_norm_g, rwkv_mu, rwkv_w0, rwkv_w2,
        rwkv_a0, rwkv_a2, rwkv_g2, rwkv_kk, rwkv_ka, rwkv_rk, rwkv_ln_g, rwkv_ln_b, w_out,
        norm2_g, router_gw, router_gb, router_ew, router_eb, exp_w_gate, exp_w_up, exp_w_down,
    )
    return second_block(
        x, c_2, positions_2, w_ada_2, b_ada_2, norm1_2, norm2_2, w_in_2, ws_gmlp_2, bs_gmlp_2,
        vnorm_gmlp_2, w_pool_2, b_pool_2, pool_scale_2, w_branch_2, w_out_2, w_ff1_2, w_ff2_2,
        final_norm_2,
    )


_drawn_inputs = setup_inputs


def setup_inputs(seed=0):
    import zlib

    import numpy as np

    out = dict(_drawn_inputs(seed))
    spreads = {}
    factors = {'lru_ba': 8.0,
     'lru_bx': 8.0,
     'lru_norm_g': 3.165,
     'fox_qnorm_g': 3.039,
     'fox_knorm_g': 4.147,
     'fox_norm_g': 3.015,
     'rwkv_w2': 8.0,
     'rwkv_a0': 3.407,
     'rwkv_kk': 4.609,
     'rwkv_ka': 3.477,
     'rwkv_ln_g': 5.893,
     'rwkv_ln_b': 8.0,
     'norm2_g': 3.059,
     'router_gb': 3.899,
     'router_eb': 5.293,
     'b_ada_2': 3.19,
     'norm1_2': 8.0,
     'norm2_2': 6.185,
     'bs_gmlp_2': 4.513,
     'vnorm_gmlp_2': 28.388,
     'b_pool_2': 51.645,
     'pool_scale_2': 3.768,
     'final_norm_2': 7.975}
    for name, (base, spread) in spreads.items():
        noise = np.random.default_rng([zlib.crc32(name.encode()), seed]).standard_normal(out[name].shape)
        drawn = base * np.exp(spread * noise) if base else spread * noise
        out[name] = __import__('jax').numpy.asarray(drawn.astype(out[name].dtype))
    for name, factor in factors.items():
        out[name] = (out[name] * factor).astype(out[name].dtype)
    return out
```

```python
from contextlib import ExitStack, contextmanager

import concourse.bass as bass
import numpy as np
from concourse import mybir

F32 = mybir.dt.float32
F32R = mybir.dt.float32r
I32 = mybir.dt.int32
ALU = mybir.AluOpType
ACT = mybir.ActivationFunctionType
AX = mybir.AxisListType

P = 128
TOK = 512
TB = TOK // P
D = 1024
KT = D // P
SLAB_COLS = 256
SLAB = KT * SLAB_COLS
EPS = 1e-6
GN_EPS = 64e-5

IN1_PAIRS, OUT1_PAIRS = 6, 2
GROUPS, PER_GROUP = 4, 4
GROUP_PAIRS = PER_GROUP + 2
MOE_AT = IN1_PAIRS + OUT1_PAIRS
LAYERS_AT = MOE_AT + GROUPS * GROUP_PAIRS
LAYERS = 2
L_Q, L_K, L_V, L_G, L_BR0 = 0, 1, 2, 4, 6
L_VS, L_U, L_BR1 = 10, 12, 14
L_P, L_POOL, L_BR2 = 18, 20, 21
L_WOUT, L_FF = 25, 27
FF_GROUPS = 4
LAYER_PAIRS = L_FF + 4 * FF_GROUPS
PAIRS = LAYERS_AT + LAYERS * LAYER_PAIRS
ADA_COLS = 48

CH = 64
NCH = TOK // CH
HEADS = 4
LOG_DECAY = -float(np.exp(np.float32(-0.5)))
WIN = (2, 4, 8, 16)
TWO_PI = 2.0 * float(np.pi)
RET_SCALE = float(np.float32(P) ** np.float32(-0.5))


def _places(sizes):
    out, at = {}, 0
    for name, n in sizes:
        out[name] = slice(at, at + n)
        at += n
    return out, at


V1, V1_COLS = _places([
    ("norm1", 8), ("conv_w", 8), ("conv_b", 2), ("lru_ba", 2), ("lru_bx", 2), ("lru_lambda", 2),
    ("lru_norm", 2), ("fox_fb", 1), ("fox_qn", 1), ("fox_kn", 1), ("fox_norm", 4), ("mu", 7),
    ("w0", 2), ("a0", 2), ("kk", 2), ("ka", 2), ("rk", 2), ("ln_g", 2), ("ln_b", 2), ("norm2", 8),
    ("c", 8), ("inv_freq", 1), ("sign", 1), ("final", 8), ("router_b", 20), ("router_w", 160), ("decay_k", 4),
    ("inv_count", 64)])
V2, V2_COLS = _places([("norm1", 8), ("norm2", 8), ("vnorm", 8), ("b_pool", 8), ("pool_scale", 8)])
C1, C1_COLS = _places([
    ("gram", 512), ("x0", 128), ("x0t", 128), ("levels", 640), ("causal", 128),
    ("lora", 256), ("lru_wa", 256), ("lru_wx", 256)])
INVERSE_LEVELS = 5


class Steps:

    def __init__(self, eng, done):
        self.eng, self.done, self.n, self.own = eng, done, 0, 0

    def again(self, eng):
        self.eng = eng
        return self

    def __call__(self, ins, sem=None, value=None):
        if sem is None:
            self.own += 1
            ins.then_inc(self.done, 1)
            self.eng.wait_ge(self.done, self.n + self.own)
        else:
            ins.then_inc(sem, 1)
            self.eng.wait_ge(sem, value)

    @contextmanager
    def loop(self, count, steps):
        base = self.n + self.own
        with self.eng.Fori(0, count) as i:
            self.n, self.own = base + i * steps, 0
            yield i
            assert self.own == steps, (self.own, steps)
        self.n, self.own = base + count * steps, 0


def build(nc, t):
    with ExitStack() as whole:
        def sb(name, shape, dt=F32, ctx=whole):
            return ctx.enter_context(nc.sbuf_tensor("sb_" + name, shape, dt))

        def sem(name):
            return whole.enter_context(nc.semaphore(name))

        xT = sb("xT", [P, KT, TOK])
        h_hi = sb("h_hi", [P, KT, TOK], F32R)
        h_lo = sb("h_lo", [P, KT, TOK], F32R)
        raw = [sb(f"raw{j}", [P, SLAB]) for j in range(2)]
        w_hi = [sb(f"w_hi{j}", [P, SLAB], F32R) for j in range(2)]
        w_lo = [sb(f"w_lo{j}", [P, SLAB], F32R) for j in range(2)]
        T = sb("T", [P, 4, TOK])
        ident = sb("ident", [P, P])
        ones = sb("ones", [P, P])
        vec = sb("vec", [P, V1_COLS])
        pd = [whole.enter_context(nc.psum_tensor(f"pd{i}", [P, TOK], F32)) for i in range(4)]
        px = [whole.enter_context(nc.psum_tensor(f"px{i}", [P, TOK], F32)) for i in range(4)]

        raw_loaded = [sem(f"raw_loaded{j}") for j in range(2)]
        w_hi_ready = [sem(f"w_hi_ready{j}") for j in range(2)]
        w_lo_ready = [sem(f"w_lo_ready{j}") for j in range(2)]
        slab_done = [sem(f"slab_done{j}") for j in range(2)]
        slab_out = [sem(f"slab_out{j}") for j in range(2)]
        steps = {}
        loops_begun = sem("loops_begun")
        scalar_steps, vector_steps = sem("scalar_steps"), sem("vector_steps")
        x_loaded, vec_loaded, out_stored = sem("x_loaded"), sem("vec_loaded"), sem("out_stored")
        norm_sq, norm_sum, norm_root = sem("norm_sq"), sem("norm_sum"), sem("norm_root")
        norm_val, norm_hi, h_ready = sem("norm_val"), sem("norm_hi"), sem("h_ready")
        act_out, y_val, y_hi_ready, y_ready = sem("act_out"), sem("y_val"), sem("y_hi_ready"), sem("y_ready")

        def v1(name, i=0, rows=slice(0, P)):
            return vec[rows, V1[name].start + i:V1[name].start + i + 1]

        def inner(eng, count):
            eng.sem_inc(loops_begun, 1)
            return eng.Fori(0, count)

        def split(act, m, j):
            act.wait_ge(raw_loaded[j], 16 * m + 16)
            if not isinstance(m, int) or m > 0:
                act.wait_ge(slab_done[j], m)
            act.copy(w_hi[j][:], raw[j][:]).then_inc(w_hi_ready[j], 1)

        def split_next(act, m, j):
            split(act, m + j, 1 - j)

        def slab_starts(pe, m, j):
            pe.wait_ge(w_lo_ready[j], m + 1)
            if not isinstance(m, int) or m > 0:
                pe.wait_ge(slab_out[j], m)

        def slab_rows(pe, m, j, hi, lo):
            slab_starts(pe, m, j)
            for f in range(2):
                for k in range(KT):
                    cols = slice(k * SLAB_COLS + f * P, k * SLAB_COLS + f * P + P)
                    out = pd[2 * j + f][:]
                    pe.matmul(out, w_hi[j][:, cols], hi[:, k], start=(k == 0), stop=False)
                    pe.matmul(out, w_hi[j][:, cols], lo[:, k], start=False, stop=False)
                    last = pe.matmul(out, w_lo[j][:, cols], hi[:, k], start=False, stop=(k == KT - 1))
            last.then_inc(slab_done[j], 1)

        def slab_tokens(pe, m, j, hi, lo):
            slab_starts(pe, m, j)
            for b in range(TB):
                out = pd[2 * j + b // 2][:, (b % 2) * SLAB_COLS:(b % 2 + 1) * SLAB_COLS]
                toks = slice(b * P, (b + 1) * P)
                for k in range(KT):
                    cols = slice(k * SLAB_COLS, (k + 1) * SLAB_COLS)
                    pe.matmul(out, hi[:, k, toks], w_hi[j][:, cols], start=(k == 0), stop=False)
                    pe.matmul(out, lo[:, k, toks], w_hi[j][:, cols], start=False, stop=False)
                    last = pe.matmul(out, hi[:, k, toks], w_lo[j][:, cols], start=False,
                                     stop=(k == KT - 1))
            last.then_inc(slab_done[j], 1)

        def norm_scalar(act, a, u, sq, shift=None):
            for i in range(2):
                act.activation(sq[:, 4 * i:4 * i + 4], xT[:, 4 * i:4 * i + 4],
                               ACT.Square).then_inc(norm_sq, 1)
            act.wait_ge(norm_sum, u + 1)
            act.activation(T[:, 0], px[0][:], ACT.Sqrt, bias=EPS, scale=1.0 / D).then_inc(norm_root, 1)
            for k in range(KT):
                act.wait_ge(norm_val, 8 * u + k + 1)
                if shift is None:
                    ins = act.copy(h_hi[:, k], sq[:, k])
                else:
                    ins = act.activation(h_hi[:, k], sq[:, k], ACT.Identity, bias=shift(k))
                ins.then_inc(norm_hi, 1)

        def norm_tensor(pe, u, sq):
            for k in range(KT):
                if k % 4 == 0:
                    pe.wait_ge(norm_sq, 2 * u + k // 4 + 1)
                last = pe.matmul(px[0][:], ones[:], sq[:, k], start=(k == 0), stop=(k == KT - 1))
            last.then_inc(norm_sum, 1)

        def norm_vector(dve, v, u, sq, gain, shift=None):
            dve.wait_ge(norm_root, u + 1)
            v(dve.reciprocal(T[:, 1], T[:, 0]))
            for k in range(KT):
                dve.scalar_tensor_tensor(sq[:, k], xT[:, k], gain(k), T[:, 1], ALU.mult,
                                         ALU.mult).then_inc(norm_val, 1)
            for k in range(KT):
                dve.wait_ge(norm_hi, 8 * u + k + 1)
                if shift is None:
                    ins = dve.tensor_tensor(h_lo[:, k], sq[:, k], h_hi[:, k].bitcast(F32), ALU.subtract)
                else:
                    ins = dve.scalar_tensor_tensor(h_lo[:, k], sq[:, k], shift(k),
                                                   h_hi[:, k].bitcast(F32), ALU.add, ALU.subtract)
                ins.then_inc(h_ready, 1)
            dve.wait_ge(h_ready, 8 * u + 8)

        Y = sb("Y", [P, KT, TOK])
        stage = ExitStack()
        c1 = sb("c1", [P, C1_COLS], ctx=stage)
        blk = sb("blk", [P, P], ctx=stage)
        M = sb("M", [P, 36, TOK], ctx=stage)
        small = sb("small", [P, 64], ctx=stage)
        fl = sb("fl", [P, TOK], ctx=stage)

        A = M[:, 0:8]
        B_dec, B_a, kk = M[:, 8:10], M[:, 10:12], M[:, 12:14]
        cum = M[:, 14:16]
        G = M[:, 4:20]
        g_out, bonus = M[:, 20:22], M[:, 22:24]
        QR = M[:, 24:28].rearrange("p (a b) n -> p a b n", a=2)
        b_s, k_s = M[:, 28:30], M[:, 30:32]
        CT, YS = b_s, k_s
        v_tok = M[:, 32:34].rearrange("p a (b c) -> p (a b) c", b=2)
        k_tok = M[:, 34:36].rearrange("p a (b c) -> p (a b) c", b=2)
        b_tok = M[:, 2:4].rearrange("p a (b c) -> p (a b) c", b=2)
        OT = M[:, 0:2]
        X, XT = Y[:, 0:4], Y[:, 4:8]
        S_old, W_sb, U_sb, S_bd = T[:, 0, 0:256], T[:, 1, 0:256], T[:, 1, 256:512], T[:, 2, 0:256]
        d_end = small[:, 0:16].rearrange("p (a b) -> p a b", a=2)
        lru_x, lru_g = M[:, 0:2], M[:, 2:4]
        xc, lr, li, la, lb, lh = (M[:, n:n + 2] for n in (4, 6, 8, 10, 12, 14))
        q_raw, k_att = M[:, 0:4], M[:, 4:8]
        v_att = M[:, 8:12]
        o_att = M[:, 12:16]
        qz = M[:, 16:24]
        sq_att = M[:, 24:32]
        probs, probsT = M[:, 24:28], M[:, 28:32]
        maskneg = c1[:, C1["causal"]]

        def cc(name):
            return c1[:, C1[name]]

        def item(h, b):
            return b * HEADS + h

        c_loaded = sem("c_loaded")
        shifted, lora_in, lora_w, lora_a, lora_g = (sem(n) for n in (
            "shifted", "lora_in", "lora_w", "lora_a", "lora_g"))
        dec_out, gate_a, gate_g = sem("dec_out"), sem("gate_a"), sem("gate_g")
        kk_raw, kk_sq, kk_sum, kk_root = sem("kk_raw"), sem("kk_sq"), sem("kk_sum"), sem("kk_root")
        bonus_in, bonus_sum, cum_ready, prev_ready = (sem(n) for n in (
            "bonus_in", "bonus_sum", "cum_ready", "prev_ready"))
        decays, scaled = sem("decays"), sem("scaled")
        tr_done, tr_out = sem("tr_done"), sem("tr_out")
        gram_done, gram_out, x0_out, x0_ready = (sem(n) for n in (
            "gram_done", "gram_out", "x0_out", "x0_ready"))
        ct_ready, ct_x, ct_x_out, x_ct_x, x_next = (sem(n) for n in (
            "ct_ready", "ct_x", "ct_x_out", "x_ct_x", "x_next"))
        seq_w, seq_w_out, seq_u, seq_u_out, seq_s, seq_s_out, seq_o, seq_o_out = (sem(n) for n in (
            "seq_w", "seq_w_out", "seq_u", "seq_u_out", "seq_s", "seq_s_out", "seq_o", "seq_o_out"))
        ln_mean, ln_cen, ln_sq, ln_var, ln_root, y_rwkv = (sem(n) for n in (
            "ln_mean", "ln_cen", "ln_sq", "ln_var", "ln_root", "y_rwkv"))
        lru_xc, lru_gates, lru_acts, lru_sqrt_in, lru_b, lru_val, lru_sq, lru_sum, lru_root, y_lru = (
            sem(n) for n in ("lru_xc", "lru_gates", "lru_acts", "lru_sqrt_in", "lru_b", "lru_val",
                             "lru_sq", "lru_sum", "lru_root", "y_lru"))
        lru_gelu = sem("lru_gelu")
        qk_sq, qk_sum, qk_root, qk_ready, fl_exp, fl_soft, negc_ready = (sem(n) for n in (
            "qk_sq", "qk_sum", "qk_root", "qk_ready", "fl_exp", "fl_soft", "negc_ready"))
        sc_done, sc_max, sc_exp, sc_prob, sc_tr, sc_tr_out, sc_pv, pair_out = (sem(n) for n in (
            "sc_done", "sc_max", "sc_exp", "sc_prob", "sc_tr", "sc_tr_out", "sc_pv", "pair_out"))
        fox_sq, fox_sum, fox_root, y_fox, fl_in = (sem(n) for n in (
            "fox_sq", "fox_sum", "fox_root", "y_fox", "fl_in"))

        UNITS = [(h, qb) for h in range(8) for qb in range(TB)]

        mixers = ExitStack()
        block = mixers.enter_context(nc.Block())

        @block.sync
        def _(sp):
            sp.dma_start(vec[:], t["vec1"]).then_inc(vec_loaded, 16)
            sp.dma_start(ones[:], t["ones"]).then_inc(vec_loaded, 16)
            sp.dma_start(xT[:, 0:4], t["x"][:, 0:4]).then_inc(x_loaded, 16)
            sp.dma_start(xT[:, 4:8], t["x"][:, 4:8]).then_inc(x_loaded, 16)
            for j in range(2):
                sp.dma_start(raw[j][:], t["slabs"][j]).then_inc(raw_loaded[j], 16)
            sp.dma_start(c1[:], t["c1"]).then_inc(c_loaded, 16)
            sp.dma_start(blk[:], t["blk"]).then_inc(c_loaded, 16)
            sp.dma_start(ident[:], t["ident"]).then_inc(c_loaded, 16)
            with sp.Fori(1, IN1_PAIRS) as m:
                for j in range(2):
                    sp.wait_ge(w_lo_ready[j], m)
                    sp.dma_start(raw[j][:], t["slabs"][bass.ds(2 * m + j, 1)]).then_inc(raw_loaded[j], 16)

        @block.gpsimd
        def _(pool):
            pool.memset(fl[:], 0.0).then_inc(fl_in, 1)
            with pool.Fori(0, IN1_PAIRS) as m:
                for j in range(2):
                    pool.wait_ge(w_hi_ready[j], m + 1)
                    pool.tensor_tensor(w_lo[j][:], raw[j][:], w_hi[j][:].bitcast(F32),
                                       ALU.subtract).then_inc(w_lo_ready[j], 1)

        @block.tensor
        def _(pe):
            pe.wait_ge(vec_loaded, 32)
            norm_tensor(pe, 0, M[:, 0:8])
            pe.wait_ge(h_ready, 8)
            for m in range(2):
                for j in range(2):
                    slab_rows(pe, m, j, h_hi, h_lo)

            pe.wait_ge(c_loaded, 48)
            pe.wait_ge(lora_in, 1)
            lora = cc("lora")
            for n, (rows, done) in enumerate(((slice(0, 32), lora_w), (slice(32, 64), lora_a))):
                for j in range(2):
                    last = pe.matmul(px[2 * n + j][:], lora[rows, j * P:(j + 1) * P], T[rows, 3],
                                     start=True, stop=True)
                last.then_inc(done, 1)
            pe.wait_ge(dec_out, 2)
            for j in range(2):
                last = pe.matmul(px[j][:], lora[64:128, j * P:(j + 1) * P], T[64:128, 3],
                                 start=True, stop=True)
            last.then_inc(lora_g, 1)
            pe.wait_ge(gate_a, 2)
            for j in range(2):
                pe.wait_ge(kk_sq, j + 1)
                pe.matmul(px[2 + j][:], blk[:], T[:, j], start=True, stop=True).then_inc(kk_sum, 1)
            pe.wait_ge(gate_g, 2)
            for j in range(2):
                pe.wait_ge(bonus_in, j + 1)
                pe.matmul(px[j][:], blk[:], bonus[:, j], start=True, stop=True).then_inc(bonus_sum, 1)
            pe.wait_ge(scaled, 2)
            n = 0
            for src in (A[:, 4:6], k_s, b_s):
                for j in range(2):
                    if n >= 4:
                        pe.wait_ge(tr_out, n - 3)
                    for b in range(TB):
                        last = pe.transpose(px[n % 4][:, b * P:(b + 1) * P], src[:, j, b * P:(b + 1) * P],
                                            ident[:])
                    last.then_inc(tr_done, 1)
                    n += 1
            pe.wait_ge(tr_out, 6)
            for b in range(TB):
                toks = slice(b * P, (b + 1) * P)
                for h in range(HEADS):
                    i, j, rows = item(h, b), h // 2, slice(64 * (h % 2), 64 * (h % 2) + 64)
                    if i >= 2:
                        pe.wait_ge(gram_out, i - 1)
                    if h == 0 and b >= 1:
                        pe.wait_ge(x0_out, b)
                    qr = QR[rows, j, :, toks]
                    pe.matmul(px[i % 2][:, 0:256], b_s[rows, j, toks], qr, start=True, stop=True)
                    pe.matmul(px[i % 2][:, 256:512], k_s[rows, j, toks], qr, start=True, stop=True)
                    pe.matmul(px[2 + h % 2][:, j * P:(j + 1) * P], QR[rows, j, 0, toks],
                              b_s[rows, j, toks], start=True, stop=True).then_inc(gram_done, 1)
            pe.wait_ge(x0_ready, 4)
            pe.wait_ge(slab_out[0], 2)
            pe.wait_ge(slab_out[1], 2)
            with pe.Fori(0, INVERSE_LEVELS) as lv:
                def first_product(b):
                    pe.wait_ge(ct_ready, 4 * lv + b + 1)
                    for h in range(HEADS):
                        s = slice(h * P, (h + 1) * P)
                        last = pe.matmul(pd[b % 2][:, s], CT[:, b % 2, s], X[:, b, s], start=True, stop=True)
                    last.then_inc(ct_x, 1)

                def second_products(b):
                    pe.wait_ge(ct_x_out, 4 * lv + b + 1)
                    if b >= 2:
                        pe.wait_ge(x_next, 4 * lv + b - 1)
                    for h in range(HEADS):
                        s = slice(h * P, (h + 1) * P)
                        pe.matmul(px[2 * (b % 2)][:, s], XT[:, b, s], YS[:, b % 2, s], start=True, stop=True)
                        last = pe.matmul(px[2 * (b % 2) + 1][:, s], YS[:, b % 2, s], XT[:, b, s],
                                         start=True, stop=True)
                    last.then_inc(x_ct_x, 1)

                first_product(0)
                for b in range(1, TB):
                    first_product(b)
                    second_products(b - 1)
                second_products(TB - 1)
            pe.wait_ge(x_next, 4 * INVERSE_LEVELS)
            for c in range(NCH):
                b, u = c // 2, c % 2
                rows, toks = slice(u * CH, (u + 1) * CH), slice(c * CH, (c + 1) * CH)
                own = slice(u * CH, (u + 1) * CH)
                pe.wait_ge(seq_s_out, c + 1)
                for j in range(2):
                    pe.matmul(pd[0][rows, j * P:(j + 1) * P], QR[:, j, 0, toks], S_bd[:, j * P:(j + 1) * P],
                              start=(j == 0), stop=False, skip_group_check=True)
                for h in range(HEADS):
                    last = pe.matmul(pd[0][rows, h * CH:(h + 1) * CH], G[:, item(h, b), 256:384][:, own],
                                     v_tok[:, b, h * CH:(h + 1) * CH], start=False, stop=(h == HEADS - 1),
                                     skip_group_check=True)
                last.then_inc(seq_w, 1)
                for j in range(2):
                    pe.matmul(pd[2][:, j * P:(j + 1) * P], k_tok[rows, b, j * P:(j + 1) * P],
                              v_tok[rows, b, j * P:(j + 1) * P], start=(j == 0), stop=False,
                              skip_group_check=True)
                if c:
                    pe.wait_ge(seq_o_out, c)
                for j in range(2):
                    pe.matmul(pd[3][:, j * CH:(j + 1) * CH], S_bd[:, j * P:(j + 1) * P], QR[:, j, 1, toks],
                              start=(j == 0), stop=False, skip_group_check=True)
                for h in range(HEADS):
                    pe.matmul(pd[3][64 * (h % 2):64 * (h % 2) + 64, (h // 2) * CH:(h // 2 + 1) * CH],
                              v_tok[:, b, h * CH:(h + 1) * CH], G[:, item(h, b), 384:512][:, own],
                              start=False, stop=False, skip_group_check=True)
                pe.wait_ge(seq_w_out, c + 1)
                for h in range(HEADS):
                    last = pe.matmul(pd[1][rows, h * CH:(h + 1) * CH], XT[:, b, h * P:(h + 1) * P][:, own],
                                     W_sb[:, h * CH:(h + 1) * CH], start=(h == 0), stop=(h == HEADS - 1),
                                     skip_group_check=True)
                last.then_inc(seq_u, 1)
                pe.wait_ge(seq_u_out, c + 1)
                for j in range(2):
                    last = pe.matmul(pd[2][:, j * P:(j + 1) * P], b_tok[rows, b, j * P:(j + 1) * P],
                                     U_sb[rows, j * P:(j + 1) * P], start=False, stop=(j == 1),
                                     skip_group_check=True)
                last.then_inc(seq_s, 1)
                for h in range(HEADS):
                    last = pe.matmul(pd[3][64 * (h % 2):64 * (h % 2) + 64, (h // 2) * CH:(h // 2 + 1) * CH],
                                     U_sb[:, h * CH:(h + 1) * CH], G[:, item(h, b), 128:256][:, own],
                                     start=False, stop=(h == HEADS - 1), skip_group_check=True)
                last.then_inc(seq_o, 1)
            pe.wait_ge(seq_o_out, NCH)
            for j in range(2):
                pe.matmul(px[j][:], blk[:], OT[:, j], start=True, stop=True).then_inc(ln_mean, 1)
            for j in range(2):
                pe.wait_ge(ln_sq, j + 1)
                pe.matmul(px[2 + j][:], blk[:], T[:, 2 + j], start=True, stop=True).then_inc(ln_var, 1)

            pe.wait_ge(y_rwkv, 2)
            for j in range(2):
                slab_rows(pe, 2, j, h_hi, h_lo)
            for n, name in enumerate(("lru_wa", "lru_wx")):
                for j in range(2):
                    if n == 0:
                        pe.wait_ge(lru_xc, j + 1)
                    pe.matmul(px[2 * n + j][:], cc(name)[:, j * P:(j + 1) * P], xc[:, j],
                              start=True, stop=True).then_inc(lru_gates, 1)
            pe.wait_ge(lru_acts, 4)
            for j in range(2):
                pe.wait_ge(lru_sq, j + 1)
                last = pe.matmul(px[0][:], ones[:], T[:, j], start=(j == 0), stop=(j == 1))
            last.then_inc(lru_sum, 1)

            pe.wait_ge(y_lru, 2)
            for m in (3, 4):
                for j in range(2):
                    slab_rows(pe, m, j, h_hi, h_lo)
            for j in range(2):
                slab_tokens(pe, 5, j, h_hi, h_lo)
            for n in range(8):
                pe.wait_ge(qk_sq, n + 1)
                if n >= 4:
                    pe.wait_ge(qk_root, n - 3)
                pe.matmul(px[n % 4][:], blk[:], sq_att[:, n], start=True, stop=True).then_inc(qk_sum, 1)
            pe.wait_ge(slab_out[0], 6)
            pe.wait_ge(slab_out[1], 6)
            pe.wait_ge(negc_ready, 1)
            pe.wait_ge(qk_ready, 8)

            def scores(n):
                h, qb = UNITS[n]
                if n >= 3:
                    pe.wait_ge(sc_exp, n - 2)
                keys = (qb + 1) * P
                out = pd[n % 3]
                pe.matmul(out[:, 0:keys], qz[:, h, qb * P:(qb + 1) * P], k_att[:, h // 2, 0:keys],
                          start=True, stop=False)
                pe.matmul(out[:, keys - P:keys], ident[:], maskneg, start=False, stop=False)
                pe.matmul(out[:, 0:keys], ident[:, h:h + 1].to_broadcast([P, P]), fl[:, 0:keys],
                          start=False, stop=True).then_inc(sc_done, 1)

            def turn(n):
                h, qb = UNITS[n]
                pe.wait_ge(sc_prob, n + 1)
                if n >= 2:
                    pe.wait_ge(sc_tr_out, n - 1)
                for b in range(qb + 1):
                    last = pe.transpose(px[n % 2][:, b * P:(b + 1) * P], probs[:, n % 4, b * P:(b + 1) * P],
                                        ident[:])
                last.then_inc(sc_tr, 1)

            def weigh(n):
                h, qb = UNITS[n]
                pair, rows = h // 2, slice(64 * (h % 2), 64 * (h % 2) + 64)
                pe.wait_ge(sc_tr_out, n + 1)
                if pair >= 2 and h % 2 == 0 and qb == 0:
                    pe.wait_ge(pair_out, pair - 1)
                for b in range(qb + 1):
                    last = pe.matmul(px[2 + pair % 2][rows, qb * P:(qb + 1) * P],
                                     v_att[:, b, h * 64:(h + 1) * 64], probsT[:, n % 4, b * P:(b + 1) * P],
                                     start=(b == 0), stop=(b == qb), skip_group_check=True)
                last.then_inc(sc_pv, 1)

            for n in range(len(UNITS) + 3):
                if n < len(UNITS):
                    scores(n)
                if 2 <= n < len(UNITS) + 2:
                    turn(n - 2)
                if n >= 3:
                    weigh(n - 3)
            for k in range(4):
                pe.wait_ge(fox_sq, k + 1)
                last = pe.matmul(px[0][:], ones[:], sq_att[:, k], start=(k == 0), stop=(k == 3))
            last.then_inc(fox_sum, 1)

        @block.scalar
        def _(act):
            a = steps["scalar"] = Steps(act, scalar_steps)
            split(act, 0, 0)
            act.wait_ge(x_loaded, 32)
            act.wait_ge(vec_loaded, 32)
            norm_scalar(act, a, 0, M[:, 0:8])
            act.wait_ge(h_ready, 8)
            for m in range(2):
                for j in range(2):
                    split_next(act, m, j)
                    act.wait_ge(slab_done[j], m + 1)
                    n = 2 * m + j
                    act.copy(A[:, 2 * n], pd[2 * j][:])
                    if n < 3:
                        last = act.copy(A[:, 2 * n + 1], pd[2 * j + 1][:])
                    else:
                        act.wait_ge(fl_in, 1)
                        last = act.activation(fl[0:8], pd[2 * j + 1][0:8], ACT.Identity,
                                              bias=v1("fox_fb", rows=slice(0, 8)))
                    last.then_inc(slab_out[j], 1)
            act.wait_ge(shifted, 7)
            act.activation(T[0:32, 3], A[0:32, 6], ACT.Tanh)
            act.copy(T[32:64, 3], A[32:64, 6])
            act.activation(T[64:128, 3], A[64:128, 6], ACT.Sigmoid).then_inc(lora_in, 1)
            act.wait_ge(lora_w, 1)
            for j in range(2):
                act.activation(B_dec[:, j], px[j][:], ACT.Sigmoid, bias=v1("w0", j)).then_inc(dec_out, 1)
            act.wait_ge(lora_a, 1)
            for j in range(2):
                act.activation(B_a[:, j], px[2 + j][:], ACT.Sigmoid, bias=v1("a0", j)).then_inc(gate_a, 1)
            act.wait_ge(lora_g, 1)
            for j in range(2):
                act.copy(g_out[:, j], px[j][:]).then_inc(gate_g, 1)
            for j in range(2):
                act.wait_ge(kk_raw, j + 1)
                act.activation(T[:, j], kk[:, j], ACT.Square).then_inc(kk_sq, 1)
            for j in range(2):
                act.wait_ge(kk_sum, j + 1)
                act.activation(T[:, j], px[2 + j][:], ACT.Sqrt).then_inc(kk_root, 1)
            for j in range(2):
                act.wait_ge(cum_ready, j + 1)
                act.activation(QR[:, j, 1], cum[:, j], ACT.Exp)
                act.activation(k_s[:, j], cum[:, j], ACT.Exp, scale=-1.0)
                act.activation(d_end[:, j], cum[:, j, CH - 1::CH], ACT.Exp)
                act.wait_ge(prev_ready, j + 1)
                act.activation(QR[:, j, 0], b_s[:, j], ACT.Exp).then_inc(decays, 1)
            for n, dst in enumerate((v_tok, v_tok, k_tok, k_tok, b_tok, b_tok)):
                act.wait_ge(tr_done, n + 1)
                act.mul(dst[:, :, (n % 2) * P:(n % 2 + 1) * P], px[n % 4][:].rearrange(
                    "p (a b) -> p a b", a=TB), -1.0 if n >= 4 else 1.0).then_inc(tr_out, 1)
            with act.Fori(0, INVERSE_LEVELS) as lv:
                for b in range(TB):
                    act.wait_ge(ct_x, 4 * lv + b + 1)
                    act.copy(YS[:, b % 2], pd[b % 2][:]).then_inc(ct_x_out, 1)
            for c in range(NCH):
                act.wait_ge(seq_o, c + 1)
                act.copy(OT[:, :, c * CH:(c + 1) * CH], pd[3][:, 0:2 * CH].rearrange(
                    "p (a b) -> p a b", a=2)).then_inc(seq_o_out, 1)
            for j in range(2):
                act.wait_ge(ln_cen, j + 1)
                act.activation(T[:, 2 + j], T[:, j], ACT.Square).then_inc(ln_sq, 1)
            for j in range(2):
                act.wait_ge(ln_var, j + 1)
                act.activation(T[:, 2 + j], px[2 + j][:], ACT.Sqrt, bias=GN_EPS,
                               scale=1.0 / CH).then_inc(ln_root, 1)

            for j, dst in enumerate((lru_x, lru_g)):
                split_next(act, 2, j)
                act.wait_ge(slab_done[j], 3)
                act.copy(dst[:, 0], pd[2 * j][:])
                act.copy(dst[:, 1], pd[2 * j + 1][:]).then_inc(slab_out[j], 1)
            soft = small[:, 16:18]
            lam = vec[:, V1["lru_lambda"]]
            a(act.activation(small[:, 20:22], lam, ACT.Abs))
            a(act.activation(small[:, 20:22], small[:, 20:22], ACT.Exp, scale=-1.0))
            a(act.activation(small[:, 20:22], small[:, 20:22], ACT.Ln, bias=1.0))
            a(act.activation(small[:, 22:24], lam, ACT.Relu, scale=-1.0))
            for j in range(2):
                a(act.activation(soft[:, j:j + 1], small[:, 20 + j:21 + j], ACT.Identity,
                                 bias=small[:, 22 + j:23 + j]))
            a(act.mul(small[:, 16:18], small[:, 16:18], 8.0))
            a(act.mul(small[:, 18:20], small[:, 16:18], -1.0))
            for j in range(2):
                act.wait_ge(lru_gates, 1 + j)
                act.activation(lr[:, j], px[j][:], ACT.Sigmoid, bias=v1("lru_ba", j)).then_inc(lru_acts, 1)
            for j in range(2):
                act.wait_ge(lru_gates, 3 + j)
                act.activation(li[:, j], px[2 + j][:], ACT.Sigmoid, bias=v1("lru_bx", j)).then_inc(lru_acts, 1)
            act.wait_ge(lru_acts, 4)
            for j in range(2):
                act.activation(la[:, j], lr[:, j], ACT.Exp, scale=small[:, 18 + j:19 + j])
                act.activation(lb[:, j], lr[:, j], ACT.Tanh, scale=small[:, 16 + j:17 + j]).then_inc(lru_b, 1)
            for j in range(2):
                act.wait_ge(lru_sqrt_in, j + 1)
                act.activation(lb[:, j], lb[:, j], ACT.Sqrt, scale=2.0).then_inc(lru_b, 1)
            for j in range(2):
                act.activation(lr[:, j], lru_g[:, j], ACT.Gelu_apprx_tanh).then_inc(lru_gelu, 1)
            for j in range(2):
                act.wait_ge(lru_val, j + 1)
                act.activation(T[:, j], lh[:, j], ACT.Square).then_inc(lru_sq, 1)
            act.wait_ge(lru_sum, 1)
            act.activation(T[:, 2], px[0][:], ACT.Sqrt, bias=EPS, scale=1.0 / 256).then_inc(lru_root, 1)

            act.wait_ge(y_lru, 2)
            for m, dst in ((3, q_raw), (4, k_att)):
                for j in range(2):
                    split_next(act, m, j)
                    act.wait_ge(slab_done[j], m + 1)
                    act.copy(dst[:, 2 * j], pd[2 * j][:])
                    act.copy(dst[:, 2 * j + 1], pd[2 * j + 1][:]).then_inc(slab_out[j], 1)
            for j in range(2):
                if j == 0:
                    split_next(act, 5, j)
                act.wait_ge(slab_done[j], 6)
                for i in range(2):
                    last = act.copy(v_att[:, 2 * i:2 * i + 2, j * SLAB_COLS:(j + 1) * SLAB_COLS],
                                    pd[2 * j + i][:].rearrange("p (a b) -> p a b", a=2))
                last.then_inc(slab_out[j], 1)
            act.wait_ge(slab_out[0], 5)
            act.wait_ge(slab_out[1], 5)
            for n in range(8):
                act.activation(sq_att[:, n], (q_raw if n < 4 else k_att)[:, n % 4], ACT.Square).then_inc(qk_sq, 1)
            for n in range(8):
                act.wait_ge(qk_sum, n + 1)
                act.wait_ge(qk_sq, 8)
                act.activation(sq_att[:, n], px[n % 4][:], ACT.Sqrt, bias=EPS, scale=1.0 / 64).then_inc(qk_root, 1)
            a(act.activation(T[0:8, 0], fl[0:8], ACT.Abs))
            a(act.activation(T[0:8, 0], T[0:8, 0], ACT.Exp, scale=-1.0))
            a(act.activation(T[0:8, 0], T[0:8, 0], ACT.Ln, bias=1.0))
            a(act.activation(T[0:8, 1], fl[0:8], ACT.Relu, scale=-1.0), fl_soft, 1)

            def copy_turned(n):
                keys = (UNITS[n][1] + 1) * P
                act.wait_ge(sc_tr, n + 1)
                if n >= 4:
                    act.wait_ge(sc_pv, n - 3)
                act.copy(probsT[:, n % 4, 0:keys], px[n % 2][:, 0:keys]).then_inc(sc_tr_out, 1)
                h, qb = UNITS[n]

            def pair_store(pair):
                act.wait_ge(sc_pv, 8 * pair + 8)
                act.copy(o_att[:, pair], px[2 + pair % 2][:]).then_inc(pair_out, 1)

            for n in range(len(UNITS) + 3):
                if n < len(UNITS):
                    keys = (UNITS[n][1] + 1) * P
                    act.wait_ge(sc_max, n + 1)
                    if n >= 4:
                        act.wait_ge(sc_tr, n - 3)
                    act.activation(probs[:, n % 4, 0:keys], pd[n % 3][:, 0:keys], ACT.Exp,
                                   bias=small[:, 32 + n % 4:33 + n % 4],
                                   accum_out=small[:, 36 + n % 4:37 + n % 4]).then_inc(sc_exp, 1)
                if 2 <= n < len(UNITS) + 2:
                    copy_turned(n - 2)
                if n >= 4 and (n - 4) % 8 == 7:
                    pair_store((n - 4) // 8)
            pair_store(3)
            act.wait_ge(pair_out, 4)
            for k in range(4):
                act.activation(sq_att[:, k], o_att[:, k], ACT.Square).then_inc(fox_sq, 1)
            act.wait_ge(fox_sum, 1)
            act.activation(T[:, 0], px[0][:], ACT.Sqrt, bias=EPS, scale=1.0 / 512).then_inc(fox_root, 1)

        @block.vector
        def _(dve):
            v = steps["vector"] = Steps(dve, vector_steps)
            dve.wait_ge(vec_loaded, 32)
            norm_vector(dve, v, 0, M[:, 0:8], lambda k: v1("norm1", k))
            v(dve.tensor_scalar(small[:, 24:26], vec[:, V1["ka"]], -1.0, 1.0, ALU.mult, ALU.add))
            for n in range(7):
                if n % 2 == 0:
                    dve.wait_ge(slab_out[(n // 2) % 2], n // 4 + 1)
                dve.tensor_tensor(T[:, n % 2, 1:TOK], A[:, n, 0:TOK - 1], A[:, n, 1:TOK], ALU.subtract)
                v(dve.tensor_scalar(T[:, n % 2, 0:1], A[:, n, 0:1], -1.0, None, ALU.mult))
                v(dve.scalar_tensor_tensor(A[:, n], T[:, n % 2], v1("mu", n), A[:, n], ALU.mult, ALU.add),
                  shifted, n + 1)
            for j in range(2):
                v(dve.tensor_scalar(kk[:, j], A[:, 2 + j], v1("kk", j), None, ALU.mult), kk_raw, j + 1)
            dve.wait_ge(dec_out, 2)
            v(dve.tensor_scalar(B_dec[:], B_dec[:], LOG_DECAY, None, ALU.mult))
            for j in range(2):
                for c in range(NCH):
                    s = slice(c * CH, (c + 1) * CH)
                    last = dve.tensor_tensor_scan(cum[:, j, s], ones[:, 0:CH], B_dec[:, j, s], 0.0,
                                                  ALU.mult, ALU.add)
                v(last, cum_ready, j + 1)
                v(dve.tensor_tensor(b_s[:, j], cum[:, j], B_dec[:, j], ALU.subtract), prev_ready, j + 1)
            dve.wait_ge(gate_a, 2)
            for j in range(2):
                dve.wait_ge(kk_root, j + 1)
                v(dve.tensor_scalar(T[:, 2], B_a[:, j], v1("ka", j), small[:, 24 + j:25 + j], ALU.mult, ALU.add))
                v(dve.tensor_tensor(A[:, 2 + j], A[:, 2 + j], T[:, 2], ALU.mult))
                v(dve.scalar_tensor_tensor(bonus[:, j], A[:, j], v1("rk", j), A[:, 2 + j], ALU.mult, ALU.mult),
                  bonus_in, j + 1)
                v(dve.tensor_scalar(T[:, j], T[:, j], 1e-12, None, ALU.max))
                v(dve.reciprocal(T[:, j], T[:, j]))
                v(dve.tensor_tensor(kk[:, j], kk[:, j], T[:, j], ALU.mult))
                v(dve.tensor_tensor(B_a[:, j], B_a[:, j], kk[:, j], ALU.mult))
            for j in range(2):
                dve.wait_ge(bonus_sum, j + 1)
                v(dve.tensor_tensor(bonus[:, j], px[j][:], A[:, 4 + j], ALU.mult))
            for j in range(2):
                dve.wait_ge(decays, j + 1)
                dve.tensor_tensor(QR[:, j, 1], QR[:, j, 1], A[:, j], ALU.mult)
                dve.tensor_tensor(QR[:, j, 0], QR[:, j, 0], kk[:, j], ALU.mult)
                v(dve.tensor_tensor(b_s[:, j], B_a[:, j], k_s[:, j], ALU.mult))
                v(dve.tensor_tensor(k_s[:, j], A[:, 2 + j], k_s[:, j], ALU.mult), scaled, j + 1)
            dve.wait_ge(c_loaded, 48)
            dve.wait_ge(tr_out, 6)
            for b in range(TB):
                for h in range(HEADS):
                    i = item(h, b)
                    dve.wait_ge(gram_done, i + 1)
                    v(dve.tensor_tensor(G[:, i], px[i % 2][:], cc("gram"), ALU.mult), gram_out, i + 1)
                four = lambda ap: ap.unsqueeze(1).to_broadcast([P, HEADS, P])
                tiles = lambda ap: ap.rearrange("p (a b) -> p a b", a=HEADS)
                by_head = X[:, b].rearrange("p (j u n) -> p j u n", j=2, u=2)
                for u in range(2):
                    ins = dve.tensor_tensor(by_head[:, :, u], px[2 + u][:, 0:256].rearrange("p (j n) -> p j n", j=2),
                                            cc("x0").unsqueeze(1).to_broadcast([P, 2, P]), ALU.mult)
                v(ins, x0_out, b + 1)
                v(dve.tensor_tensor(tiles(XT[:, b]), G[:, 4 * b:4 * b + 4, 0:P], four(cc("x0t")), ALU.mult))
                dve.tensor_tensor(tiles(X[:, b]), tiles(X[:, b]), four(ident[:]), ALU.add)
                v(dve.tensor_tensor(tiles(XT[:, b]), tiles(XT[:, b]), four(ident[:]), ALU.add), x0_ready, b + 1)
            levels = cc("levels")
            with dve.Fori(0, INVERSE_LEVELS) as lv:
                def mask(b):
                    m = levels[:, bass.ds(lv * P, P)].unsqueeze(1).to_broadcast([P, HEADS, P])
                    v(dve.tensor_tensor(tiles(CT[:, b % 2]), G[:, 4 * b:4 * b + 4, 0:P], m, ALU.mult),
                      ct_ready, 4 * lv + b + 1)

                def update(b):
                    dve.wait_ge(x_ct_x, 4 * lv + b + 1)
                    dve.tensor_tensor(X[:, b], X[:, b], px[2 * (b % 2)][:], ALU.subtract)
                    v(dve.tensor_tensor(XT[:, b], XT[:, b], px[2 * (b % 2) + 1][:], ALU.subtract),
                      x_next, 4 * lv + b + 1)

                mask(0)
                mask(1)
                update(0)
                mask(2)
                update(1)
                mask(3)
                update(2)
                update(3)
            dve.memset(W_sb, 0.0)
            dve.memset(U_sb, 0.0)
            dve.memset(S_old, 0.0)
            v(dve.memset(S_bd, 0.0), seq_s_out, 1)
            for c in range(NCH):
                rows = slice((c % 2) * CH, (c % 2 + 1) * CH)
                dve.wait_ge(seq_w, c + 1)
                v(dve.tensor_copy(W_sb[rows], pd[0][rows, 0:256]), seq_w_out, c + 1)
                dve.wait_ge(seq_u, c + 1)
                if c:
                    dve.wait_ge(seq_o, c)
                v(dve.tensor_copy(U_sb[rows], pd[1][rows, 0:256]), seq_u_out, c + 1)
                for j in range(2):
                    last = dve.tensor_scalar(S_old[:, j * P:(j + 1) * P], S_bd[:, j * P:(j + 1) * P],
                                             d_end[:, j, c:c + 1], None, ALU.mult)
                v(last)
                dve.wait_ge(seq_s, c + 1)
                for j in range(2):
                    for u in range(2):
                        head, cols = slice(64 * u, 64 * u + 64), slice(j * P + 64 * u, j * P + 64 * u + 64)
                        last = dve.scalar_tensor_tensor(S_bd[head, cols], pd[2][head, cols],
                                                        d_end[head, j, c:c + 1], S_old[head, cols],
                                                        ALU.mult, ALU.add)
                v(last, seq_s_out, c + 2)
            for j in range(2):
                dve.wait_ge(ln_mean, j + 1)
                v(dve.scalar_tensor_tensor(T[:, j], px[j][:], -1.0 / CH, OT[:, j], ALU.mult, ALU.add), ln_cen, j + 1)
            for j in range(2):
                dve.wait_ge(ln_root, j + 1)
                v(dve.reciprocal(T[:, 2 + j], T[:, 2 + j]))
                v(dve.scalar_tensor_tensor(T[:, j], T[:, j], v1("ln_g", j), T[:, 2 + j], ALU.mult, ALU.mult))
                v(dve.scalar_tensor_tensor(T[:, j], T[:, j], v1("ln_b", j), bonus[:, j], ALU.add, ALU.add))
                v(dve.tensor_tensor(Y[:, 6 + j], T[:, j], g_out[:, j], ALU.mult), y_rwkv, j + 1)

            dve.wait_ge(slab_out[0], 3)
            for j in range(2):
                v(dve.tensor_scalar(xc[:, j], lru_x[:, j], v1("conv_w", 6 + j), v1("conv_b", j), ALU.mult, ALU.add))
                for s in range(1, 4):
                    ins = dve.scalar_tensor_tensor(xc[:, j, s:TOK], lru_x[:, j, 0:TOK - s],
                                                   v1("conv_w", 2 * (3 - s) + j), xc[:, j, s:TOK],
                                                   ALU.mult, ALU.add)
                    if s < 3:
                        v(ins)
                    else:
                        v(ins, lru_xc, j + 1)
            for j in range(2):
                dve.wait_ge(lru_b, j + 1)
                v(dve.tensor_scalar(T[:, j], lb[:, j], 1.0, None, ALU.add))
                v(dve.reciprocal(T[:, j], T[:, j]))
                v(dve.tensor_tensor(lb[:, j], lb[:, j], T[:, j], ALU.mult), lru_sqrt_in, j + 1)
            for j in range(2):
                dve.wait_ge(lru_b, 3 + j)
                v(dve.tensor_tensor(li[:, j], li[:, j], xc[:, j], ALU.mult))
                v(dve.tensor_tensor(lb[:, j], lb[:, j], li[:, j], ALU.mult))
                v(dve.tensor_tensor_scan(lh[:, j], la[:, j], lb[:, j], 0.0, ALU.mult, ALU.add))
                dve.wait_ge(lru_gelu, j + 1)
                v(dve.tensor_tensor(lh[:, j], lh[:, j], lr[:, j], ALU.mult), lru_val, j + 1)
            dve.wait_ge(lru_root, 1)
            v(dve.reciprocal(T[:, 2], T[:, 2]))
            for j in range(2):
                v(dve.scalar_tensor_tensor(Y[:, j], lh[:, j], v1("lru_norm", j), T[:, 2], ALU.mult, ALU.mult),
                  y_lru, j + 1)

            v(dve.memset(qz[:], 0.0))
            v(dve.tensor_scalar(small[:, 30:31], v1("fox_qn"), 0.125, None, ALU.mult))
            for n in range(8):
                dve.wait_ge(qk_root, n + 1)
                v(dve.reciprocal(sq_att[:, n], sq_att[:, n]))
                if n < 4:
                    for u in range(2):
                        rows = slice(64 * u, 64 * u + 64)
                        last = dve.scalar_tensor_tensor(qz[rows, 2 * n + u], q_raw[rows, n], small[rows, 30:31],
                                                        sq_att[rows, n], ALU.mult, ALU.mult)
                    v(last, qk_ready, n + 1)
                else:
                    v(dve.scalar_tensor_tensor(k_att[:, n - 4], k_att[:, n - 4], v1("fox_kn"), sq_att[:, n],
                                               ALU.mult, ALU.mult), qk_ready, n + 1)
            dve.wait_ge(fl_soft, 1)
            v(dve.tensor_tensor(T[0:8, 0], T[0:8, 0], T[0:8, 1], ALU.add))
            v(dve.memset(T[0:8, 1], 1.0))
            v(dve.tensor_tensor_scan(fl[0:8], T[0:8, 1], T[0:8, 0], 0.0, ALU.mult, ALU.add), negc_ready, 1)
            for n in range(len(UNITS) + 1):
                if n < len(UNITS):
                    keys = (UNITS[n][1] + 1) * P
                    dve.wait_ge(sc_done, n + 1)
                    if n >= 4:
                        dve.wait_ge(sc_exp, n - 3)
                    v(dve.tensor_reduce(small[:, 32 + n % 4:33 + n % 4], pd[n % 3][:, 0:keys], AX.X, ALU.max,
                                        negate=True), sc_max, n + 1)
                if n >= 1:
                    p = n - 1
                    keys = (UNITS[p][1] + 1) * P
                    dve.wait_ge(sc_exp, p + 1)
                    v(dve.reciprocal(small[:, 40 + p % 4:41 + p % 4], small[:, 36 + p % 4:37 + p % 4]))
                    v(dve.tensor_scalar(probs[:, p % 4, 0:keys], probs[:, p % 4, 0:keys],
                                        small[:, 40 + p % 4:41 + p % 4], None, ALU.mult), sc_prob, p + 1)
            dve.wait_ge(fox_root, 1)
            v(dve.reciprocal(T[:, 0], T[:, 0]))
            for k in range(4):
                v(dve.scalar_tensor_tensor(Y[:, 2 + k], o_att[:, k], v1("fox_norm", k), T[:, 0],
                                           ALU.mult, ALU.mult), y_fox, k + 1)

        mixers.close()
        stage.close()
        y_hi = sb("y_hi", [P, KT, TOK], F32R)
        y_lo = sb("y_lo", [P, KT, TOK], F32R)
        V, QK, MG = (sb(n, [P, KT, TOK]) for n in ("V", "QK", "MG"))
        O = Y
        v2 = sb("v2", [P, LAYERS, V2_COLS])
        mod = sb("mod", [P, LAYERS * ADA_COLS])
        b_ada = sb("b_ada", [P, LAYERS * ADA_COLS])
        swap = sb("swap", [P, P])
        lay = sb("lay", [P, V2_COLS + ADA_COLS + 16])
        small2 = sb("small2", [P, 64])
        V_tok = V[:].rearrange("p (b a) n -> p b (a n)", b=TB)
        MOD = V2_COLS
        GAIN = V2_COLS + ADA_COLS

        ada = [QK[:, 4 * j:4 * j + 4].rearrange("p a n -> p (a n)") for j in range(2)]
        combT = V[0:PER_GROUP, 0:GROUPS]
        c_act = small2[:, 0:8]
        rt = T[:, 3]
        cos, sin, decT, decq = MG[:, 0], MG[:, 1], MG[:, 2], MG[:, 3]
        pos, ang, turns = MG[:, 4], MG[:, 5], MG[:, 6]
        SCT, KD, QD, ST, ST3 = MG[:, 4], MG[:, 5], MG[:, 6], MG[:, 7], T[:, 3]
        w_sgu, tri, b_sgu = QK[:, 0], QK[:, 1, 0:P], QK[:, 2]

        stage2_loaded, ada_loaded, ada_done = sem("stage2_loaded"), [sem(f"ada_loaded{j}") for j in range(2)], [
            sem(f"ada_done{j}") for j in range(2)]
        mod_ready = sem("mod_ready")
        logits, r_exp_in, r_exp, comb_ready, comb_tr, combT_ready = (sem(n) for n in (
            "logits", "r_exp_in", "r_exp", "comb_ready", "comb_tr", "combT_ready"))
        c_silu, comb_mm, moe_act = sem("c_silu"), sem("comb_mm"), sem("moe_act")
        tables_loaded, angle, table_abs, tables_ready = (sem(n) for n in (
            "tables_loaded", "angle", "table_abs", "tables_ready"))
        swapped, rotated, ret_sc, ret_scaled, ret_kv, ret_state, ret_out, ret_stored = (sem(n) for n in (
            "swapped", "rotated", "ret_sc", "ret_scaled", "ret_kv", "ret_state", "ret_out", "ret_stored"))
        ret_sq, ret_sum, ret_root, ret_norm = (sem(n) for n in ("ret_sq", "ret_sum", "ret_root", "ret_norm"))
        sgu_loaded, vs_root, vs_norm, sgu_w, mixed, mixed_out = (sem(n) for n in (
            "sgu_loaded", "vs_root", "vs_norm", "sgu_w", "mixed", "mixed_out"))
        pooled, pool_act, merged = sem("pooled"), sem("pool_act"), sem("merged")
        lay_ready, branch_part = sem("lay_ready"), sem("branch_part")

        def lv_(i):
            return lay[:, i:i + 1]

        Y_MOE = KT
        Y_LAYERS, Y_PER_LAYER = Y_MOE + 2 * GROUPS * PER_GROUP, 5 * KT + 8 * FF_GROUPS
        Y_G, Y_U, Y_PIN, Y_POUT, Y_MG, Y_FF = (KT * n for n in range(6))
        VAL_LAYERS, VAL_PER_LAYER = 2 * GROUPS * PER_GROUP, 3 * KT + 8 * FF_GROUPS
        VAL_G, VAL_U, VAL_POUT, VAL_FF = (KT * n for n in range(4))

        def y_scalar(act, m, j, func, n, yb, vb, banks=None, signal=None):
            act.wait_ge(slab_done[j], m + 1)
            act.wait_ge(y_ready, yb + 2 * n - 2)
            tj = 2 * j if banks is None else 2 * (n % 2)
            for f in range(2):
                bank = pd[2 * j + f] if banks is None else banks[f]
                ins = act.activation(T[:, tj + f], bank[:], func)
            ins.then_inc(slab_out[j] if signal is None else signal, 1)
            for f in range(2):
                act.wait_ge(y_val, vb + 2 * n + f + 1)
                act.copy(y_hi[:, bass.ds(2 * n + f, 1)], T[:, tj + f:tj + f + 1]).then_inc(y_hi_ready, 1)

        def y_vector(dve, v, m, j, value, n, yb, vb, tj=None, wait=None):
            if wait is None:
                dve.wait_ge(slab_out[j], m + 1)
            else:
                dve.wait_ge(*wait)
            tj = 2 * j if tj is None else tj
            for f in range(2):
                value(T[:, tj + f:tj + f + 1], f).then_inc(y_val, 1)
            for f in range(2):
                dve.wait_ge(y_hi_ready, yb + 2 * n + f + 1)
                dve.tensor_tensor(y_lo[:, bass.ds(2 * n + f, 1)], T[:, tj + f:tj + f + 1],
                                  y_hi[:, bass.ds(2 * n + f, 1)].bitcast(F32), ALU.subtract).then_inc(y_ready, 1)
            dve.wait_ge(y_ready, yb + 2 * n + 2)

        def round_scalar(act, src, yb):
            for k in range(KT):
                act.copy(y_hi[:, k], src[:, k]).then_inc(y_hi_ready, 1)

        def round_vector(dve, src, yb):
            for k in range(KT):
                dve.wait_ge(y_hi_ready, yb + k + 1)
                dve.tensor_tensor(y_lo[:, k], src[:, k], y_hi[:, k].bitcast(F32), ALU.subtract).then_inc(y_ready, 1)
            dve.wait_ge(y_ready, yb + KT)

        def add_to_x(dve, v, m, j, tile, gate=None):
            dve.wait_ge(slab_done[j], m + 1)
            for f in range(2):
                to = xT[:, bass.ds(tile + 2 * j + f, 1)]
                bank = pd[2 * j + f][:].unsqueeze(1)
                if gate is None:
                    ins = dve.tensor_tensor(to, bank, to, ALU.add)
                else:
                    ins = dve.scalar_tensor_tensor(to, bank, lay[:, bass.ds(gate + tile + 2 * j + f, 1)], to,
                                                   ALU.mult, ALU.add)
            ins.then_inc(slab_out[j], 1)
            dve.wait_ge(slab_out[j], m + 1)

        def add_scalar(act, m, j):
            split_next(act, m, j)

        rest = ExitStack()
        block = rest.enter_context(nc.Block())

        @block.sync
        def _(sp):
            sp.dma_start(v2[:], t["vec2"]).then_inc(stage2_loaded, 16)
            sp.dma_start(b_ada[:], t["b_ada"]).then_inc(stage2_loaded, 16)
            sp.dma_start(swap[:], t["swap"]).then_inc(stage2_loaded, 16)

            def load(m):
                for j in range(2):
                    sp.wait_ge(w_lo_ready[j], m)
                    sp.dma_start(raw[j][:], t["slabs"][bass.ds(2 * m + j, 1)]).then_inc(raw_loaded[j], 16)

            def load_ada(i):
                for j in range(2):
                    sp.dma_start(ada[j], t["ada"][bass.ds(2 * i + j, 1)]).then_inc(ada_loaded[j], 16)

            with sp.Fori(IN1_PAIRS, MOE_AT) as m:
                load(m)
            load(MOE_AT)
            load_ada(0)
            with sp.Fori(1, GROUPS * GROUP_PAIRS) as i:
                load(MOE_AT + i)
                for j in range(2):
                    sp.wait_ge(ada_done[j], i)
                load_ada(i)
            with sp.Fori(LAYERS_AT, PAIRS) as m:
                load(m)
            sp.wait_ge(w_lo_ready[0], PAIRS)
            sp.dma_start(raw[0][:], t["slabs"][2 * PAIRS]).then_inc(raw_loaded[0], 16)

        @block.gpsimd
        def _(pool):
            def remainder(m, j):
                pool.wait_ge(w_hi_ready[j], m + 1)
                pool.tensor_tensor(w_lo[j][:], raw[j][:], w_hi[j][:].bitcast(F32),
                                   ALU.subtract).then_inc(w_lo_ready[j], 1)

            with pool.Fori(IN1_PAIRS, PAIRS) as m:
                for j in range(2):
                    remainder(m, j)
            remainder(PAIRS, 0)

        @block.tensor
        def _(pe):
            pe.wait_ge(y_ready, KT)
            for m in range(IN1_PAIRS, MOE_AT):
                for j in range(2):
                    slab_rows(pe, m, j, y_hi, y_lo)
            norm_tensor(pe, 1, MG)
            pe.wait_ge(h_ready, 16)
            router_w = vec[:, V1["router_w"]].rearrange("p (k n) -> p k n", k=KT)
            for b in range(TB):
                for k in range(KT):
                    last = pe.matmul(px[1][:, b * 20:(b + 1) * 20], MG[:, k, b * P:(b + 1) * P], router_w[:, k],
                                     start=(k == 0), stop=(k == KT - 1))
            last.then_inc(logits, 1)
            pe.wait_ge(comb_ready, 1)
            for g in range(GROUPS):
                for b in range(TB):
                    last = pe.transpose(px[g][0:PER_GROUP, b * P:(b + 1) * P],
                                        rt[:, 256 + 16 * b + 4 * g:256 + 16 * b + 4 * g + 4], ident[:])
            last.then_inc(comb_tr, 1)

            def ada_products(m):
                for j in range(2):
                    pe.wait_ge(ada_loaded[j], 16 * (m - MOE_AT) + 16)
                    for f in range(2):
                        for k in range(KT):
                            cols = slice(k * SLAB_COLS + f * P, k * SLAB_COLS + f * P + P)
                            last = pe.matmul(px[2 + j][:, f:f + 1], ada[j][:, cols], c_act[:, k:k + 1],
                                             start=(k == 0), stop=(k == KT - 1))
                    last.then_inc(ada_done[j], 1)

            pe.wait_ge(combT_ready, 4)
            pe.wait_ge(c_silu, 1)
            with pe.Fori(0, GROUPS) as g:
                for e in range(PER_GROUP):
                    m = MOE_AT + GROUP_PAIRS * g + e
                    slab_rows(pe, m, 0, h_hi, h_lo)
                    pe.matmul(px[e % 2][:], ident[0:PER_GROUP, e:e + 1].to_broadcast([PER_GROUP, P]),
                              combT[:, bass.ds(g, 1)], start=True, stop=True).then_inc(comb_mm, 1)
                    slab_rows(pe, m, 1, h_hi, h_lo)
                    ada_products(m)
                pe.wait_ge(y_ready, Y_MOE + 8 * g + 8)
                with inner(pe, 2) as d:
                    m = MOE_AT + GROUP_PAIRS * g + PER_GROUP + d
                    for j in range(2):
                        slab_rows(pe, m, j, y_hi, y_lo)
                    ada_products(m)

            with pe.Fori(0, LAYERS) as l:
                L = LAYERS_AT + LAYER_PAIRS * l
                yb = Y_LAYERS + Y_PER_LAYER * l

                def rows(at, pairs, hi, lo):
                    with inner(pe, pairs) as i:
                        for j in range(2):
                            slab_rows(pe, L + at + i, j, hi, lo)

                def branch(at):
                    with inner(pe, 4) as i:
                        slab_rows(pe, L + at + i, 0, h_hi, h_lo)
                        slab_rows(pe, L + at + i, 1, y_hi, y_lo)

                def tokens(at):
                    with inner(pe, 2) as i:
                        for j in range(2):
                            slab_tokens(pe, L + at + i, j, h_hi, h_lo)

                norm_tensor(pe, 2 + 2 * l, O)
                pe.wait_ge(h_ready, 8 * (2 * l + 2) + 8)
                rows(L_Q, 2, h_hi, h_lo)
                tokens(L_V)
                for n in range(8):
                    if n % 4 == 0:
                        pe.wait_ge(slab_out[0], L + n // 4 + 1)
                        pe.wait_ge(slab_out[1], L + n // 4 + 1)
                    if n >= 4:
                        pe.wait_ge(rotated, 8 * l + n - 3)
                    pe.matmul(px[n % 4][:], swap[:], QK[:, n], start=True, stop=True).then_inc(swapped, 1)
                pe.wait_ge(rotated, 8 * l + 8)
                pe.wait_ge(slab_out[0], L + 4)
                pe.wait_ge(slab_out[1], L + 4)
                for h in range(HEADS):
                    q, k = QK[:, h], QK[:, 4 + h]
                    if h:
                        pe.wait_ge(ret_norm, 4 * l + h)
                    for c in range(TB):
                        s = slice(c * P, (c + 1) * P)
                        pe.matmul(px[0][:, s], k[:, s], q[:, s], start=True, stop=True)
                        last = pe.transpose(px[1][:, s], k[:, s], ident[:])
                    last.then_inc(ret_sc, 1)
                    pe.wait_ge(ret_scaled, 4 * l + h + 1)
                    for c in range(TB - 1):
                        last = pe.matmul(px[2 + c // 2][:, (c % 2) * 256:(c % 2) * 256 + 256],
                                         KD[:, c * P:(c + 1) * P], V_tok[:, c, h * 256:(h + 1) * 256],
                                         start=True, stop=True)
                    last.then_inc(ret_kv, 1)
                    pe.wait_ge(ret_state, 4 * l + h + 1)
                    for et in range(2):
                        for c in range(TB):
                            s, e0 = slice(c * P, (c + 1) * P), h * 256 + et * P
                            last = pe.matmul(px[et][:, s], V_tok[:, c, e0:e0 + P], SCT[:, s],
                                             start=True, stop=(c == 0))
                            if c:
                                state = ST[:, (c - 1) * 256 + et * P:(c - 1) * 256 + et * P + P] if c < 3 \
                                    else ST3[:, et * P:et * P + P]
                                last = pe.matmul(px[et][:, s], state, QD[:, s], start=False, stop=True)
                    last.then_inc(ret_out, 1)
                    for et in range(2):
                        pe.wait_ge(ret_sq, 8 * l + 2 * h + et + 1)
                        last = pe.matmul(px[2][:], ones[:], T[:, et], start=(et == 0), stop=(et == 1))
                    last.then_inc(ret_sum, 1)
                pe.wait_ge(ret_norm, 4 * l + 4)
                rows(L_G, 2, h_hi, h_lo)
                pe.wait_ge(y_ready, yb + Y_G + KT)
                branch(L_BR0)
                tokens(L_VS)
                pe.wait_ge(vs_norm, l + 1)
                pe.wait_ge(sgu_w, l + 1)
                for k in range(KT):
                    if k >= 4:
                        pe.wait_ge(mixed_out, 8 * l + k - 3)
                    for c in range(TB):
                        last = pe.matmul(px[k % 4][:, c * P:(c + 1) * P], V_tok[:, c, k * P:(k + 1) * P],
                                         w_sgu[:, (k // 2) * P:(k // 2 + 1) * P], start=True, stop=True)
                    last.then_inc(mixed, 1)
                pe.wait_ge(mixed_out, 8 * l + 8)
                rows(L_U, 2, h_hi, h_lo)
                pe.wait_ge(y_ready, yb + Y_U + KT)
                branch(L_BR1)
                rows(L_P, 2, h_hi, h_lo)
                pe.wait_ge(y_ready, yb + Y_PIN + KT)
                for j in range(2):
                    m = L + L_POOL
                    slab_starts(pe, m, j)
                    for gi in range(2):
                        for et in range(2):
                            out = (pd if gi == 0 else px)[2 * j + et][:]
                            for kt in range(2):
                                cols = slice((2 * gi + kt) * SLAB_COLS + et * P,
                                             (2 * gi + kt) * SLAB_COLS + et * P + P)
                                k = 2 * (2 * j + gi) + kt
                                pe.matmul(out, w_hi[j][:, cols], y_hi[:, k], start=(kt == 0), stop=False)
                                pe.matmul(out, w_hi[j][:, cols], y_lo[:, k], start=False, stop=False)
                                last = pe.matmul(out, w_lo[j][:, cols], y_hi[:, k], start=False, stop=(kt == 1))
                    last.then_inc(slab_done[j], 1)
                pe.wait_ge(y_ready, yb + Y_POUT + KT)
                branch(L_BR2)
                pe.wait_ge(y_ready, yb + Y_MG + KT)
                rows(L_WOUT, 2, y_hi, y_lo)
                norm_tensor(pe, 3 + 2 * l, O)
                pe.wait_ge(h_ready, 8 * (2 * l + 3) + 8)
                with inner(pe, FF_GROUPS) as q:
                    with inner(pe, 2) as i:
                        for j in range(2):
                            slab_rows(pe, L + L_FF + 4 * q + i, j, h_hi, h_lo)
                    pe.wait_ge(y_ready, yb + Y_FF + 8 * q + 8)
                    with inner(pe, 2) as i:
                        for j in range(2):
                            slab_rows(pe, L + L_FF + 4 * q + 2 + i, j, y_hi, y_lo)
            norm_tensor(pe, 2 + 2 * LAYERS, O)

        @block.scalar
        def _(act):
            a = steps["scalar"].again(act)
            split(act, IN1_PAIRS, 0)
            act.activation(c_act, vec[:, V1["c"]], ACT.Silu).then_inc(c_silu, 1)
            round_scalar(act, Y, 0)
            for m in range(IN1_PAIRS, MOE_AT):
                for j in range(2):
                    split_next(act, m, j)
            for j in range(2):
                act.wait_ge(slab_out[j], MOE_AT)
            norm_scalar(act, a, 1, MG)
            for n in range(2):
                act.wait_ge(r_exp_in, n + 1)
                s = slice(0, 16) if n == 0 else slice(16, 80)
                act.activation(rt[:, s], rt[:, s], ACT.Exp).then_inc(r_exp, 1)
            act.wait_ge(comb_tr, 1)
            for g in range(GROUPS):
                act.copy(combT[:, g], px[g][0:PER_GROUP]).then_inc(combT_ready, 1)
            with act.Fori(0, GROUPS) as g:
                for e in range(PER_GROUP):
                    m = MOE_AT + GROUP_PAIRS * g + e
                    split_next(act, m, 0)
                    act.wait_ge(slab_done[0], m + 1)
                    act.wait_ge(y_ready, Y_MOE + 8 * g + 2 * e)
                    act.activation(T[:, 0], pd[0][:], ACT.Silu)
                    act.activation(T[:, 1], pd[1][:], ACT.Silu).then_inc(slab_out[0], 1)
                    act.wait_ge(comb_mm, 4 * g + e + 1)
                    act.copy(T[:, 2], px[e % 2][:]).then_inc(moe_act, 1)
                    split_next(act, m, 1)
                    for f in range(2):
                        act.wait_ge(y_val, 8 * g + 2 * e + f + 1)
                        act.copy(y_hi[:, 2 * e + f], T[:, f]).then_inc(y_hi_ready, 1)
                with inner(act, 2) as d:
                    for j in range(2):
                        split_next(act, MOE_AT + GROUP_PAIRS * g + PER_GROUP + d, j)

            with a.loop(LAYERS, TB) as l:
                L = LAYERS_AT + LAYER_PAIRS * l
                yb = Y_LAYERS + Y_PER_LAYER * l
                vb = VAL_LAYERS + VAL_PER_LAYER * l
                for j in range(2):
                    act.wait_ge(slab_out[j], L)
                act.wait_ge(lay_ready, l + 1)
                act.dma_start(pos.bitcast(I32), t["positions"].partition_broadcast(P)).then_inc(tables_loaded, 16)
                act.dma_start(MG[:, 2:4], t["decays"]).then_inc(tables_loaded, 16)
                norm_scalar(act, a, 2 + 2 * l, O, lambda k: lv_(MOD + k))
                act.wait_ge(angle, l + 1)
                act.activation(turns, ang, ACT.Abs).then_inc(table_abs, 1)
                act.activation(sin, ang, ACT.Sin, scale=1.0)
                act.wait_ge(table_abs, l + 1)
                act.activation(cos, turns, ACT.Sin, bias=0.5 * float(np.pi), scale=-1.0).then_inc(tables_ready, 1)

                def plain(m, j, k, func=ACT.Copy, scale=1.0):
                    split_next(act, m, j)
                    act.wait_ge(slab_done[j], m + 1)
                    for f in range(2):
                        ins = act.activation(QK[:, k + f], pd[2 * j + f][:], func, scale=scale)
                    ins.then_inc(slab_out[j], 1)

                def by_tokens(at, func):
                    with inner(act, 2) as i:
                        for j in range(2):
                            split_next(act, L + at + i, j)
                            act.wait_ge(slab_done[j], L + at + i + 1)
                            for half in range(2):
                                ins = act.activation(
                                    V_tok[:, 2 * half:2 * half + 2, bass.ds(i * 512 + j * SLAB_COLS, SLAB_COLS)],
                                    pd[2 * j + half][:].rearrange("p (a b) -> p a b", a=2), func)
                            ins.then_inc(slab_out[j], 1)

                def y_phase(at, func, yo, vo):
                    with inner(act, 2) as i:
                        for j in range(2):
                            split_next(act, L + at + i, j)
                            y_scalar(act, L + at + i, j, func, 2 * i + j, yb + yo, vb + vo)

                def branch(at):
                    with inner(act, 4) as i:
                        m = L + at + i
                        split_next(act, m, 0)
                        act.wait_ge(slab_done[0], m + 1)
                        act.wait_ge(slab_out[1], m)
                        act.activation(T[:, 0], pd[0][:], ACT.Sigmoid)
                        act.activation(T[:, 1], pd[1][:], ACT.Sigmoid).then_inc(slab_out[0], 1)
                        split_next(act, m, 1)

                for n in range(4):
                    plain(L + n // 2, n % 2, 2 * n, scale=1.0 if n < 2 else RET_SCALE)
                by_tokens(L_V, ACT.Copy)
                for h in range(HEADS):
                    act.wait_ge(ret_out, 4 * l + h + 1)
                    for et in range(2):
                        act.copy(O[:, 2 * h + et], px[et][:]).then_inc(ret_stored, 1)
                    for et in range(2):
                        act.wait_ge(ret_stored, 8 * l + 2 * h + et + 1)
                        act.activation(T[:, et], O[:, 2 * h + et], ACT.Square).then_inc(ret_sq, 1)
                    act.wait_ge(ret_sum, 4 * l + h + 1)
                    act.activation(T[:, 2], px[2][:], ACT.Sqrt, bias=EPS, scale=1.0 / 256).then_inc(ret_root, 1)
                act.wait_ge(ret_norm, 4 * l + 4)
                y_phase(L_G, ACT.Silu, Y_G, VAL_G)
                branch(L_BR0)
                for dst, name in ((w_sgu, "w_sgu"), (b_sgu, "b_sgu")):
                    act.dma_start(dst, t[name][bass.ds(l, 1)] if name == "w_sgu" else
                                  t[name][bass.ds(l, 1)].partition_broadcast(P)).then_inc(sgu_loaded, 16)
                act.dma_start(tri, t["tri"]).then_inc(sgu_loaded, 16)
                by_tokens(L_VS, ACT.Gelu_apprx_tanh)
                for j in range(2):
                    act.wait_ge(slab_out[j], L + L_VS + 2)
                for b in range(TB):
                    ins = act.activation(O[:, 2 * (b % 2):2 * (b % 2) + 2], V_tok[:, b].rearrange(
                        "p (a n) -> p a n", a=2), ACT.Square, accum_out=small2[:, 12 + b:13 + b])
                    a(ins)
                act.activation(small2[:, 16:20], small2[:, 12:16], ACT.Sqrt, bias=EPS,
                               scale=1.0 / D).then_inc(vs_root, 1)
                act.wait_ge(mixed_out, 8 * l + 8)
                y_phase(L_U, ACT.Gelu_apprx_tanh, Y_U, VAL_U)
                branch(L_BR1)
                for n in range(4):
                    plain(L + L_P + n // 2, n % 2, 2 * n)
                act.wait_ge(pooled, l + 1)
                round_scalar(act, O, yb + Y_PIN)
                for j in range(2):
                    split_next(act, L + L_POOL, j)
                    for gi in range(2):
                        y_scalar(act, L + L_POOL, j, ACT.Copy, 2 * j + gi, yb + Y_POUT, vb + VAL_POUT,
                                 banks=[(pd if gi == 0 else px)[2 * j + et] for et in range(2)],
                                 signal=slab_out[j] if gi == 0 else pool_act)
                branch(L_BR2)
                act.wait_ge(slab_out[1], L + L_BR2 + 4)
                round_scalar(act, MG, yb + Y_MG)
                with inner(act, 2) as i:
                    for j in range(2):
                        split_next(act, L + L_WOUT + i, j)
                for j in range(2):
                    act.wait_ge(slab_out[j], L + L_WOUT + 2)
                norm_scalar(act, a, 3 + 2 * l, O, lambda k: lv_(MOD + 24 + k))
                with inner(act, FF_GROUPS) as q:
                    with inner(act, 2) as i:
                        for j in range(2):
                            m = L + L_FF + 4 * q + i
                            split_next(act, m, j)
                            y_scalar(act, m, j, ACT.Relu, 2 * i + j, yb + Y_FF + 8 * q, vb + VAL_FF + 8 * q)
                    with inner(act, 2) as i:
                        for j in range(2):
                            split_next(act, L + L_FF + 4 * q + 2 + i, j)
            for j in range(2):
                act.wait_ge(slab_out[j], PAIRS)
            u = 2 + 2 * LAYERS
            for i in range(2):
                act.activation(O[:, 4 * i:4 * i + 4], xT[:, 4 * i:4 * i + 4], ACT.Square).then_inc(norm_sq, 1)
            act.wait_ge(norm_sum, u + 1)
            act.activation(T[:, 0], px[0][:], ACT.Sqrt, bias=EPS, scale=1.0 / D).then_inc(norm_root, 1)
            for i in range(2):
                act.wait_ge(norm_val, 8 * u + 4 * i + 4)
                act.dma_start(t["out"][:, 4 * i:4 * i + 4], O[:, 4 * i:4 * i + 4]).then_inc(out_stored, 16)
            act.wait_ge(out_stored, 32)

        @block.vector
        def _(dve):
            v = steps["vector"].again(dve)
            round_vector(dve, Y, 0)
            for m in range(IN1_PAIRS, MOE_AT):
                for j in range(2):
                    add_to_x(dve, v, m, j, 4 * (m - IN1_PAIRS))
            norm_vector(dve, v, 1, MG, lambda k: v1("norm2", k))

            GL = rt[:, 0:16].rearrange("p (b g) -> p b g", b=TB)
            EL = rt[:, 16:80].rearrange("p (n e) -> p n e", e=4)
            lg = px[1][:, 0:80].rearrange("p (b n) -> p b n", b=TB)
            rb = vec[:, V1["router_b"]]
            dve.wait_ge(logits, 1)
            dve.tensor_tensor(GL, lg[:, :, 0:4], rb[:, 0:4].unsqueeze(1).to_broadcast([P, TB, 4]), ALU.add)
            v(dve.tensor_tensor(rt[:, 16:80].rearrange("p (b n) -> p b n", b=TB), lg[:, :, 4:20],
                                rb[:, 4:20].unsqueeze(1).to_broadcast([P, TB, 16]), ALU.add))
            at = 80

            def ranked(VL, n, first, exp_no):
                mx, rk, cmp = rt[:, first:first + n], rt[:, first + 16:first + 16 + 4 * n], rt[:, 400:400 + 3 * n]
                rk = rk.rearrange("p (n e) -> p n e", e=4)
                v(dve.tensor_reduce(mx, VL, AX.X, ALU.max))
                v(dve.tensor_tensor(VL, VL, mx.unsqueeze(2).to_broadcast([P, n, 4]), ALU.subtract), r_exp_in, exp_no)
                dve.wait_ge(r_exp, exp_no)
                v(dve.memset(rk, 0.0))
                for d in range(1, 4):
                    w = 4 - d
                    cm = cmp[:, 0:n * w].rearrange("p (n e) -> p n e", e=w)
                    v(dve.tensor_tensor(cm, VL[:, :, d:4], VL[:, :, 0:w], ALU.is_gt))
                    v(dve.tensor_tensor(rk[:, :, 0:w], rk[:, :, 0:w], cm, ALU.add))
                    v(dve.tensor_scalar(cm, cm, -1.0, 1.0, ALU.mult, ALU.add))
                    v(dve.tensor_tensor(rk[:, :, d:4], rk[:, :, d:4], cm, ALU.add))
                return mx, rk

            mx, rk = ranked(GL, TB, 80, 1)
            v(dve.tensor_reduce(mx, GL, AX.X, ALU.add))
            v(dve.reciprocal(mx, mx))
            v(dve.tensor_scalar(rk, rk, 0.5, None, ALU.is_lt))
            v(dve.tensor_tensor(GL, rk, mx.unsqueeze(2).to_broadcast([P, TB, 4]), ALU.mult))
            mx, rk = ranked(EL, 4 * TB, 120, 2)
            v(dve.tensor_scalar(rk, rk, 1.5, None, ALU.is_lt))
            v(dve.tensor_tensor(EL, EL, rk, ALU.mult))
            v(dve.tensor_reduce(mx, EL, AX.X, ALU.add))
            v(dve.reciprocal(mx, mx))
            v(dve.tensor_tensor(mx, mx, rt[:, 0:16], ALU.mult))
            v(dve.tensor_tensor(rt[:, 256:320].rearrange("p (n e) -> p n e", e=4), EL,
                                mx.unsqueeze(2).to_broadcast([P, 4 * TB, 4]), ALU.mult), comb_ready, 1)
            dve.wait_ge(stage2_loaded, 48)

            def mod_store(m):
                for j in range(2):
                    dve.wait_ge(ada_done[j], m - MOE_AT + 1)
                    at = 4 * (m - MOE_AT) + 2 * j
                    ins = dve.tensor_tensor(mod[:, bass.ds(at, 2)], px[2 + j][:, 0:2], b_ada[:, bass.ds(at, 2)],
                                            ALU.add)
                return ins

            with v.loop(GROUPS, PER_GROUP) as g:
                for e in range(PER_GROUP):
                    m = MOE_AT + GROUP_PAIRS * g + e
                    dve.wait_ge(moe_act, 4 * g + e + 1)
                    for f in range(2):
                        last = dve.tensor_tensor(T[:, f], T[:, f], T[:, 2], ALU.mult)
                    v(last)
                    dve.wait_ge(slab_done[1], m + 1)
                    for f in range(2):
                        dve.tensor_tensor(T[:, f], T[:, f], pd[2 + f][:], ALU.mult).then_inc(y_val, 1)
                    mod_store(m).then_inc(slab_out[1], 1)
                    for f in range(2):
                        dve.wait_ge(y_hi_ready, Y_MOE + 8 * g + 2 * e + f + 1)
                        dve.tensor_tensor(y_lo[:, 2 * e + f], T[:, f], y_hi[:, 2 * e + f].bitcast(F32),
                                          ALU.subtract).then_inc(y_ready, 1)
                    dve.wait_ge(y_ready, Y_MOE + 8 * g + 2 * e + 2)
                with inner(dve, 2) as d:
                    m = MOE_AT + GROUP_PAIRS * g + PER_GROUP + d
                    add_to_x(dve, v, m, 0, 4 * d)
                    dve.wait_ge(slab_done[1], m + 1)
                    for f in range(2):
                        to = xT[:, bass.ds(4 * d + 2 + f, 1)]
                        dve.tensor_tensor(to, pd[2 + f][:].unsqueeze(1), to, ALU.add)
                    mod_store(m).then_inc(slab_out[1], 1)
                    dve.wait_ge(slab_out[1], m + 1)
            sgn = v1("sign")
            with v.loop(LAYERS, LAYER_VECTOR_STEPS) as l:
                L = LAYERS_AT + LAYER_PAIRS * l
                yb = Y_LAYERS + Y_PER_LAYER * l
                vb = VAL_LAYERS + VAL_PER_LAYER * l
                dve.tensor_copy(lay[:, 0:V2_COLS], v2[:, bass.ds(l, 1)])
                v(dve.tensor_copy(lay[:, MOD:MOD + ADA_COLS], mod[:, bass.ds(ADA_COLS * l, ADA_COLS)]))
                for n in range(2):
                    ins = dve.scalar_tensor_tensor(lay[:, GAIN + 8 * n:GAIN + 8 * n + 8],
                                                   lay[:, MOD + 24 * n + 8:MOD + 24 * n + 16], 1.0,
                                                   lay[:, 8 * n:8 * n + 8], ALU.add, ALU.mult)
                v(ins, lay_ready, l + 1)
                norm_vector(dve, v, 2 + 2 * l, O, lambda k: lv_(GAIN + k), lambda k: lv_(MOD + k))
                dve.wait_ge(tables_loaded, 32 * l + 32)
                v(dve.tensor_scalar(ang, pos.bitcast(I32), v1("inv_freq"), None, ALU.mult))
                v(dve.tensor_scalar(turns, ang, 1.0 / TWO_PI, ROUND, ALU.mult, ALU.add))
                v(dve.tensor_scalar(turns, turns, ROUND, None, ALU.subtract))
                for part in TURN_PARTS:
                    v(dve.scalar_tensor_tensor(ang, turns, -part, ang, ALU.mult, ALU.add))
                v(dve.tensor_scalar(ang, ang, PI_BELOW, -PI_BELOW, ALU.min, ALU.max), angle, l + 1)
                dve.wait_ge(tables_ready, l + 1)
                v(dve.tensor_scalar(sin, sin, sgn, None, ALU.mult))
                for n in range(8):
                    dve.wait_ge(swapped, 8 * l + n + 1)
                    dve.tensor_tensor(T[:, n % 2], px[n % 4][:], sin, ALU.mult)
                    v(dve.tensor_tensor(QK[:, n], QK[:, n], cos, ALU.mult))
                    v(dve.tensor_tensor(QK[:, n], QK[:, n], T[:, n % 2], ALU.add), rotated, 8 * l + n + 1)
                by_chunk = lambda ap: ap.rearrange("p (c n) -> p c n", c=TB)
                for h in range(HEADS):
                    dec = lambda ap: ap[:, h * P:(h + 1) * P].unsqueeze(1).to_broadcast([P, TB, P])
                    dve.tensor_tensor(by_chunk(QD), by_chunk(QK[:, h]), dec(decq), ALU.mult)
                    dve.wait_ge(ret_sc, 4 * l + h + 1)
                    dve.tensor_scalar(KD, px[1][:], v1("decay_k", h), None, ALU.mult)
                    v(dve.tensor_tensor(by_chunk(SCT), by_chunk(px[0][:]), dec(decT), ALU.mult),
                      ret_scaled, 4 * l + h + 1)
                    dve.wait_ge(ret_kv, 4 * l + h + 1)
                    dc = DECAY_CHUNK[h]
                    v(dve.tensor_copy(ST[:, 0:256], px[2][:, 0:256]))
                    v(dve.scalar_tensor_tensor(ST[:, 256:512], ST[:, 0:256], dc, px[2][:, 256:512], ALU.mult, ALU.add))
                    v(dve.scalar_tensor_tensor(ST3[:, 0:256], ST[:, 256:512], dc, px[3][:, 0:256], ALU.mult, ALU.add),
                      ret_state, 4 * l + h + 1)
                    dve.wait_ge(ret_root, 4 * l + h + 1)
                    v(dve.reciprocal(T[:, 2], T[:, 2]))
                    for et in range(2):
                        last = dve.tensor_tensor(O[:, 2 * h + et], O[:, 2 * h + et], T[:, 2], ALU.mult)
                    v(last, ret_norm, 4 * l + h + 1)

                def y_phase(at, value, yo, vo):
                    with inner(dve, 2) as i:
                        for j in range(2):
                            y_vector(dve, v, L + at + i, j, lambda tile, f: value(tile, 4 * i + 2 * j + f),
                                     2 * i + j, yb + yo, vb + vo)

                def times_o(tile, k):
                    return dve.tensor_tensor(tile, tile, O[:, bass.ds(k, 1)], ALU.mult)

                def branch(at, first):
                    with inner(dve, 4) as i:
                        m = L + at + i
                        dve.wait_ge(slab_out[0], m + 1)
                        dve.wait_ge(slab_done[1], m + 1)
                        for f in range(2):
                            to = MG[:, bass.ds(2 * i + f, 1)]
                            dst = to if first else T[:, 2 + f:3 + f]
                            ins = dve.tensor_tensor(dst, T[:, f:f + 1], pd[2 + f][:].unsqueeze(1), ALU.mult)
                        if not first:
                            ins.then_inc(branch_part, 1)
                            dve.wait_ge(branch_part, 8 * l + (0 if at == L_BR1 else 4) + i + 1)
                            for f in range(2):
                                to = MG[:, bass.ds(2 * i + f, 1)]
                                ins = dve.tensor_tensor(to, to, T[:, 2 + f:3 + f], ALU.add)
                        ins.then_inc(slab_out[1], 1)
                        dve.wait_ge(slab_out[1], m + 1)

                y_phase(L_G, times_o, Y_G, VAL_G)
                branch(L_BR0, True)
                dve.wait_ge(sgu_loaded, 48 * l + 48)
                v(dve.tensor_tensor(by_chunk(w_sgu), by_chunk(w_sgu), tri.unsqueeze(1).to_broadcast([P, TB, P]),
                                    ALU.mult), sgu_w, l + 1)
                dve.wait_ge(vs_root, l + 1)
                v(dve.reciprocal(small2[:, 20:24], small2[:, 16:20]))
                for b in range(TB):
                    last = dve.tensor_scalar(V_tok[:, b], V_tok[:, b], small2[:, 20 + b:21 + b], None, ALU.mult)
                v(last, vs_norm, l + 1)
                for k in range(KT):
                    dve.wait_ge(mixed, 8 * l + k + 1)
                    bias = b_sgu[:, (k // 2) * P:(k // 2 + 1) * P].unsqueeze(1).to_broadcast([P, TB, P])
                    v(dve.scalar_tensor_tensor(by_chunk(O[:, k]), by_chunk(px[k % 4][:]), lv_(16 + k), bias,
                                               ALU.mult, ALU.add), mixed_out, 8 * l + k + 1)
                y_phase(L_U, times_o, Y_U, VAL_U)
                branch(L_BR1, False)
                for j in range(2):
                    dve.wait_ge(slab_out[j], L + L_P + 2)
                for g, w in enumerate(WIN):
                    p = QK[:, 2 * g:2 * g + 2]
                    cur, d, n = p, 1, 0
                    while d < w:
                        nxt = V[:, 4 * (g % 2) + 2 * (n % 2):4 * (g % 2) + 2 * (n % 2) + 2]
                        dve.tensor_tensor(nxt[:, :, d:TOK], cur[:, :, d:TOK], cur[:, :, 0:TOK - d], ALU.add)
                        v(dve.tensor_copy(nxt[:, :, 0:d], cur[:, :, 0:d]))
                        cur, d, n = nxt, 2 * d, n + 1
                    count = vec[:, V1["inv_count"]][:, 16 * g:16 * g + 16].unsqueeze(1).to_broadcast([P, 2, 16])
                    dve.scalar_tensor_tensor(O[:, 2 * g:2 * g + 2, 16:TOK], cur[:, :, 16:TOK], 1.0 / w,
                                             p[:, :, 16:TOK], ALU.mult, ALU.subtract)
                    head = small2[:, 32:64].rearrange("p (a n) -> p a n", a=2)
                    v(dve.tensor_tensor(head, cur[:, :, 0:16], count, ALU.mult))
                    ins = dve.tensor_tensor(O[:, 2 * g:2 * g + 2, 0:16], head, p[:, :, 0:16], ALU.subtract)
                    if g < 3:
                        v(ins)
                    else:
                        v(ins, pooled, l + 1)
                round_vector(dve, O, yb + Y_PIN)
                for j in range(2):
                    for gi in range(2):
                        def scaled_value(tile, f):
                            k = 4 * j + 2 * gi + f
                            return dve.tensor_scalar(tile, tile, lv_(24 + k), lv_(32 + k), ALU.add, ALU.mult)
                        y_vector(dve, v, L + L_POOL, j, scaled_value, 2 * j + gi, yb + Y_POUT, vb + VAL_POUT,
                                 tj=2 * gi, wait=(slab_out[j], L + L_POOL + 1) if gi == 0 else (pool_act, 2 * l + j + 1))
                branch(L_BR2, False)
                round_vector(dve, MG, yb + Y_MG)
                with inner(dve, 2) as i:
                    for j in range(2):
                        add_to_x(dve, v, L + L_WOUT + i, j, 4 * i, MOD + 16)
                norm_vector(dve, v, 3 + 2 * l, O, lambda k: lv_(GAIN + 8 + k), lambda k: lv_(MOD + 24 + k))
                with inner(dve, FF_GROUPS) as q:
                    with inner(dve, 2) as i:
                        for j in range(2):
                            y_vector(dve, v, L + L_FF + 4 * q + i, j,
                                     lambda tile, f: dve.tensor_tensor(tile, tile, tile, ALU.mult),
                                     2 * i + j, yb + Y_FF + 8 * q, vb + VAL_FF + 8 * q)
                    with inner(dve, 2) as i:
                        for j in range(2):
                            add_to_x(dve, v, L + L_FF + 4 * q + 2 + i, j, 4 * i, MOD + 40)
            u = 2 + 2 * LAYERS
            dve.wait_ge(norm_root, u + 1)
            v(dve.reciprocal(T[:, 1], T[:, 0]))
            for k in range(KT):
                dve.scalar_tensor_tensor(O[:, k], xT[:, k], v1("final", k), T[:, 1], ALU.mult,
                                         ALU.mult).then_inc(norm_val, 1)

        rest.close()


def feature_tiles(a):
    return np.ascontiguousarray(np.asarray(a).reshape(-1, P).T)


def slabs_of(w):
    n = w.shape[1] // SLAB_COLS
    return w.reshape(KT, P, n, SLAB_COLS).transpose(2, 1, 0, 3).reshape(n, P, SLAB)


def constants():
    s, q = np.arange(P)[:, None], np.arange(P)[None, :]
    same = s // CH == q // CH
    before, upto = (same & (s < q)).astype(np.float32), (same & (s <= q)).astype(np.float32)
    level = []
    for n in range(INVERSE_LEVELS + 1):
        m = 1 << n
        level.append(((q // (2 * m) == s // (2 * m)) & (q // m % 2 == 1) & (s // m % 2 == 0)).astype(np.float32))
    c1 = {
        "gram": np.concatenate([before, -upto, before, upto], 1), "x0": -level[0].T, "x0t": -level[0],
        "levels": np.concatenate(level[1:], 1), "causal": np.where(q <= s, 0.0, -1e30).astype(np.float32)}
    f = np.float32
    log_gamma = np.log1p(-np.power(f(2.0), f(-5.0) - np.arange(HEADS, dtype=f)).astype(f)).astype(f)
    pos = np.arange(P, dtype=f)
    rel = pos[None, :] - pos[:, None]
    dec = [np.where(rel >= 0, np.exp(log_gamma[h] * np.maximum(rel, 0)), 0).astype(f) for h in range(HEADS)]
    dec_q = [np.broadcast_to(np.exp(log_gamma[h] * (pos + 1)).astype(f), (P, P)) for h in range(HEADS)]
    dec_k = np.exp(log_gamma[None, :] * (P - 1 - pos[:, None])).astype(f)
    half = P // 2
    inv_freq = np.power(f(10000.0), -np.arange(half, dtype=f) / f(half)).astype(f)
    inv_count = np.concatenate([1.0 / np.minimum(np.arange(1, 17), w) for w in WIN]).astype(f)
    return {
        "c1": c1, "decays": np.stack([np.concatenate(dec, 1), np.concatenate(dec_q, 1)], 1), "decay_k": dec_k,
        "decay_chunk": [float(np.exp(log_gamma[h] * f(P))) for h in range(HEADS)],
        "inv_freq": np.concatenate([inv_freq, inv_freq])[:, None], "sign": np.repeat([[-1.0], [1.0]], half, 0).astype(f),
        "inv_count": np.broadcast_to(inv_count, (P, 64)), "tri": (s <= q).astype(f),
        "swap": (q == (s + half) % P).astype(f), "ident": np.eye(P, dtype=f), "ones": np.ones((P, P), f),
        "blk": same.astype(f)}


ROUND = 12582912.0
TURN_PARTS = (6.28125, 0.0019350051879882812, float(2 * np.pi - 6.28125 - 0.0019350051879882812))
PI_BELOW = 3.1415925
DECAY_CHUNK = constants()["decay_chunk"]
LAYER_VECTOR_STEPS = 48


def lay_out(inputs):
    a = {n: np.asarray(x) for n, x in inputs.items()}
    k = constants()
    f = np.float32
    w_in = a["w_in"][0]
    lru, q_at, f_at, p_at = 512, 512, 2048, 2056
    misc = np.zeros((D, SLAB_COLS), f)
    misc[:, 0:P] = w_in[:, p_at + 768:p_at + 896]
    misc[:, P:P + 8] = w_in[:, f_at:p_at]
    parts = [w_in[:, p_at:p_at + 768], misc, w_in[:, 0:lru], w_in[:, q_at:f_at], a["w_out"][0]]
    slabs = [slabs_of(p) for p in parts]
    for g in range(GROUPS):
        for e in range(g * PER_GROUP, (g + 1) * PER_GROUP):
            slabs += [slabs_of(a["exp_w_gate"][0, e]), slabs_of(a["exp_w_up"][0, e])]
        slabs.append(slabs_of(a["exp_w_down"][0, g * PER_GROUP:(g + 1) * PER_GROUP].reshape(D, D)))
    for l in range(LAYERS):
        w = a["w_in_2"][l]
        cols = {n: slabs_of(w[:, s:e]) for n, s, e in (
            ("q", 0, 512), ("k", 512, 1024), ("v", 1024, 2048), ("g", 2048, 3072), ("u", 3072, 4096),
            ("vs", 4096, 5120), ("p", 5120, 6144))}
        gate = [slabs_of(w[:, 6144 + D * n:6144 + D * (n + 1)]) for n in range(3)]
        br = [slabs_of(a["w_branch_2"][l, n]) for n in range(3)]
        both = [np.stack([gate[n], br[n]], 1).reshape(8, P, SLAB) for n in range(3)]
        pool = np.zeros((2, P, SLAB), f)
        wp = a["w_pool_2"][l].reshape(2, 2, 2, P, SLAB_COLS)
        pool[:, :, 0:SLAB // 2] = wp.transpose(0, 3, 1, 2, 4).reshape(2, P, SLAB // 2)
        slabs += [cols["q"], cols["k"], cols["v"], cols["g"], both[0], cols["vs"], cols["u"], both[1],
                  cols["p"], pool, both[2], slabs_of(a["w_out_2"][l])]
        for n in range(FF_GROUPS):
            slabs += [slabs_of(a["w_ff1_2"][l][:, n * D:(n + 1) * D]), slabs_of(a["w_ff2_2"][l][n * D:(n + 1) * D])]
    slabs.append(np.zeros((1, P, SLAB), f))
    slabs = np.concatenate(slabs)
    assert slabs.shape[0] == 2 * PAIRS + 1, slabs.shape

    vec1 = np.zeros((P, V1_COLS), f)

    def put(name, x):
        vec1[:, V1[name]] = x

    for name, src in (("norm1", "norm1_g"), ("conv_w", "conv_w"), ("conv_b", "conv_b"), ("lru_ba", "lru_ba"),
                      ("lru_bx", "lru_bx"), ("lru_lambda", "lru_lambda"), ("lru_norm", "lru_norm_g"),
                      ("fox_norm", "fox_norm_g"), ("mu", "rwkv_mu"), ("w0", "rwkv_w0"), ("a0", "rwkv_a0"),
                      ("kk", "rwkv_kk"), ("ka", "rwkv_ka"), ("rk", "rwkv_rk"), ("ln_g", "rwkv_ln_g"),
                      ("ln_b", "rwkv_ln_b"), ("norm2", "norm2_g"), ("c", "c_2"), ("final", "final_norm_2")):
        put(name, feature_tiles(a[src]))
    vec1[0:8, V1["fox_fb"]] = a["fox_fb"].reshape(8, 1)
    put("fox_qn", np.concatenate([a["fox_qnorm_g"][0]] * 2)[:, None])
    put("fox_kn", np.concatenate([a["fox_knorm_g"][0]] * 2)[:, None])
    put("router_b", np.broadcast_to(np.concatenate([a["router_gb"][0], a["router_eb"][0]]), (P, 20)))
    rw = np.concatenate([a["router_gw"][0], a["router_ew"][0]], 1)
    put("router_w", rw.reshape(KT, P, 20).transpose(1, 0, 2).reshape(P, 160))
    for name in ("decay_k", "inv_freq", "sign", "inv_count"):
        put(name, k[name])

    c1 = np.zeros((P, C1_COLS), f)
    for name, x in k["c1"].items():
        c1[:, C1[name]] = x
    c1[:, C1["lora"]] = np.concatenate([a["rwkv_w2"][0], a["rwkv_a2"][0], a["rwkv_g2"][0]], 0)
    for name in ("lru_wa", "lru_wx"):
        for h in range(HEADS):
            u, j = h % 2, h // 2
            at = C1[name].start + j * P + 64 * u
            c1[64 * u:64 * u + 64, at:at + 64] = a[name][0, h]

    vec2 = np.zeros((P, LAYERS, V2_COLS), f)
    for l in range(LAYERS):
        for name, src in (("norm1", "norm1_2"), ("norm2", "norm2_2"), ("vnorm", "vnorm_gmlp_2"),
                          ("b_pool", "b_pool_2"), ("pool_scale", "pool_scale_2")):
            vec2[:, l, V2[name]] = feature_tiles(a[src][l])
    return {
        "x": np.ascontiguousarray(a["x"][0].T.reshape(KT, P, TOK).transpose(1, 0, 2)), "slabs": slabs,
        "ada": np.concatenate([slabs_of(a["w_ada_2"][l]) for l in range(LAYERS)]),
        "vec1": vec1, "vec2": vec2, "c1": c1, "b_ada": feature_tiles(a["b_ada_2"]),
        "positions": np.ascontiguousarray(a["positions_2"][0]),
        "w_sgu": np.ascontiguousarray(a["ws_gmlp_2"].transpose(0, 3, 1, 2).reshape(LAYERS, P, 4 * P)),
        "b_sgu": np.ascontiguousarray(a["bs_gmlp_2"].reshape(LAYERS, 4 * P)),
        "decays": k["decays"], "tri": k["tri"], "swap": k["swap"], "ident": k["ident"], "ones": k["ones"],
        "blk": k["blk"]}


def kernel(**inputs):
    import concourse.bacc as bacc
    from concourse.bass_utils import run_bass_kernel_spmd

    nc = bacc.Bacc("TRN2", target_bir_lowering=False, num_devices=1)
    arrays, t = {}, {}
    for name, x in lay_out(inputs).items():
        arrays[f"in_{name}"] = np.ascontiguousarray(x)
        t[name] = nc.dram_tensor(f"in_{name}", x.shape, mybir.dt.from_np(x.dtype), kind="ExternalInput").ap()
    t["out"] = nc.dram_tensor("out_0", (P, KT, TOK), F32, kind="ExternalOutput").ap()
    build(nc, t)
    r = run_bass_kernel_spmd(nc, [arrays], core_ids=[0])
    out = r.results[0]["out_0"]
    return np.ascontiguousarray(out.transpose(2, 1, 0)).reshape(1, TOK, D)
```

```python
from contextlib import ExitStack, contextmanager

import concourse.bass as bass
import numpy as np
from concourse import mybir

F32 = mybir.dt.float32
F32R = mybir.dt.float32r
I32 = mybir.dt.int32
ALU = mybir.AluOpType
ACT = mybir.ActivationFunctionType
AX = mybir.AxisListType

P = 128
TOK = 512
TB = TOK // P
D = 1024
KT = D // P
SLAB_COLS = 256
SLAB = KT * SLAB_COLS
EPS = 1e-6
GN_EPS = 64e-5

IN1_PAIRS, OUT1_PAIRS = 6, 2
GROUPS, PER_GROUP = 4, 4
GROUP_PAIRS = PER_GROUP + 2
MOE_AT = IN1_PAIRS + OUT1_PAIRS
LAYERS_AT = MOE_AT + GROUPS * GROUP_PAIRS
LAYERS = 2
L_Q, L_K, L_V, L_G = 0, 1, 2, 4
L_VS, L_BR0, L_U, L_P, L_BR1 = 6, 8, 12, 14, 16
L_POOL, L_BR2 = 20, 21
L_WOUT, L_FF = 25, 27
FF_GROUPS = 4
LAYER_PAIRS = L_FF + 4 * FF_GROUPS
PAIRS = LAYERS_AT + LAYERS * LAYER_PAIRS
ADA_COLS = 48

CH = 64
NCH = TOK // CH
HEADS = 4
LOG_DECAY = -float(np.exp(np.float32(-0.5)))
WIN = (2, 4, 8, 16)
TWO_PI = 2.0 * float(np.pi)
RET_SCALE = float(np.float32(P) ** np.float32(-0.5))


def _places(sizes):
    out, at = {}, 0
    for name, n in sizes:
        out[name] = slice(at, at + n)
        at += n
    return out, at


V1, V1_COLS = _places([
    ("norm1", 8), ("conv_w", 8), ("conv_b", 2), ("lru_ba", 2), ("lru_bx", 2), ("lru_lambda", 2),
    ("lru_norm", 2), ("fox_fb", 1), ("fox_qn", 1), ("fox_kn", 1), ("fox_norm", 4), ("mu", 7),
    ("w0", 2), ("a0", 2), ("kk", 2), ("ka", 2), ("rk", 2), ("ln_g", 2), ("ln_b", 2), ("norm2", 8),
    ("c", 8), ("inv_freq", 1), ("sign", 1), ("final", 8), ("router_b", 20), ("router_w", 160), ("decay_k", 4),
    ("inv_count", 64)])
V2, V2_COLS = _places([("norm1", 8), ("norm2", 8), ("vnorm", 8), ("b_pool", 8), ("pool_scale", 8)])
C1, C1_COLS = _places([
    ("gram", 512), ("x0", 128), ("x0t", 128), ("levels", 640), ("causal", 128),
    ("lora", 256), ("lru_wa", 256), ("lru_wx", 256), ("halves", 32)])
INVERSE_LEVELS = 5


class Steps:

    def __init__(self, eng, done):
        self.eng, self.done, self.n, self.own = eng, done, 0, 0

    def again(self, eng):
        self.eng = eng
        return self

    def __call__(self, ins, sem=None, value=None):
        if sem is None:
            self.own += 1
            ins.then_inc(self.done, 1)
            self.eng.wait_ge(self.done, self.n + self.own)
        else:
            ins.then_inc(sem, 1)
            self.eng.wait_ge(sem, value)

    @contextmanager
    def loop(self, count, steps):
        base = self.n + self.own
        with self.eng.Fori(0, count) as i:
            self.n, self.own = base + i * steps, 0
            yield i
            assert self.own == steps, (self.own, steps)
        self.n, self.own = base + count * steps, 0


def build(nc, t):
    with ExitStack() as whole:
        def sb(name, shape, dt=F32, ctx=whole):
            return ctx.enter_context(nc.sbuf_tensor("sb_" + name, shape, dt))

        def sem(name):
            return whole.enter_context(nc.semaphore(name))

        xT = sb("xT", [P, KT, TOK])
        h_hi = sb("h_hi", [P, KT, TOK], F32R)
        h_lo = sb("h_lo", [P, KT, TOK], F32R)
        raw = [sb(f"raw{j}", [P, SLAB]) for j in range(2)]
        w_hi = [sb(f"w_hi{j}", [P, SLAB], F32R) for j in range(2)]
        w_lo = [sb(f"w_lo{j}", [P, SLAB], F32R) for j in range(2)]
        T = sb("T", [P, 4, TOK])
        ident = sb("ident", [P, P])
        ones = sb("ones", [P, P])
        vec = sb("vec", [P, V1_COLS])
        pd = [whole.enter_context(nc.psum_tensor(f"pd{i}", [P, TOK], F32)) for i in range(4)]
        px = [whole.enter_context(nc.psum_tensor(f"px{i}", [P, TOK], F32)) for i in range(4)]

        raw_loaded = [sem(f"raw_loaded{j}") for j in range(2)]
        w_hi_ready = [sem(f"w_hi_ready{j}") for j in range(2)]
        w_lo_ready = [sem(f"w_lo_ready{j}") for j in range(2)]
        slab_done = [sem(f"slab_done{j}") for j in range(2)]
        slab_out = [sem(f"slab_out{j}") for j in range(2)]
        steps = {}
        loops_begun = sem("loops_begun")
        scalar_steps, vector_steps = sem("scalar_steps"), sem("vector_steps")
        x_loaded = [sem(f"x_loaded{n}") for n in range(4)]
        vec_loaded, out_stored = sem("vec_loaded"), sem("out_stored")
        norm_sq, norm_sum, norm_root = sem("norm_sq"), sem("norm_sum"), sem("norm_root")
        norm_added = sem("norm_added")
        norm_val, norm_hi, h_ready = sem("norm_val"), sem("norm_hi"), sem("h_ready")
        y_val, y_hi_ready, y_ready = sem("y_val"), sem("y_hi_ready"), sem("y_ready")

        def v1(name, i=0, rows=slice(0, P)):
            return vec[rows, V1[name].start + i:V1[name].start + i + 1]

        def inner(eng, count):
            eng.sem_inc(loops_begun, 1)
            return eng.Fori(0, count)

        def split(act, m, j):
            act.wait_ge(raw_loaded[j], 16 * m + 16)
            if not isinstance(m, int) or m > 0:
                act.wait_ge(slab_done[j], m)
            act.copy(w_hi[j][:], raw[j][:]).then_inc(w_hi_ready[j], 1)

        def split_next(act, m, j):
            split(act, m + j, 1 - j)

        def remainder(pool, m, j):
            pool.wait_ge(w_hi_ready[j], m + 1)
            pool.tensor_tensor(w_lo[j][:], raw[j][:], w_hi[j][:].bitcast(F32),
                               ALU.subtract).then_inc(w_lo_ready[j], 1)

        def slab_starts(pe, m, j):
            pe.wait_ge(w_lo_ready[j], m + 1)
            if not isinstance(m, int) or m > 0:
                pe.wait_ge(slab_out[j], m)

        def slab_rows(pe, m, j, hi, lo, ready=None):
            slab_starts(pe, m, j)
            for k in range(KT):
                if ready is not None:
                    pe.wait_ge(ready[0], ready[1] + k + 1)
                slab_piece(pe, j, k, hi, lo)

        def slab_piece(pe, j, k, hi, lo):
            for f in range(2):
                cols = slice(k * SLAB_COLS + f * P, k * SLAB_COLS + f * P + P)
                out = pd[2 * j + f][:]
                pe.matmul(out, w_hi[j][:, cols], hi[:, k], start=(k == 0), stop=False)
                pe.matmul(out, w_hi[j][:, cols], lo[:, k], start=False, stop=False)
                last = pe.matmul(out, w_lo[j][:, cols], hi[:, k], start=False, stop=(k == KT - 1))
            if k == KT - 1:
                last.then_inc(slab_done[j], 1)

        def slab_tokens(pe, m, j, hi, lo):
            slab_starts(pe, m, j)
            for b in range(TB):
                out = pd[2 * j + b // 2][:, (b % 2) * SLAB_COLS:(b % 2 + 1) * SLAB_COLS]
                toks = slice(b * P, (b + 1) * P)
                for k in range(KT):
                    cols = slice(k * SLAB_COLS, (k + 1) * SLAB_COLS)
                    pe.matmul(out, hi[:, k, toks], w_hi[j][:, cols], start=(k == 0), stop=False)
                    pe.matmul(out, lo[:, k, toks], w_hi[j][:, cols], start=False, stop=False)
                    last = pe.matmul(out, hi[:, k, toks], w_lo[j][:, cols], start=False,
                                     stop=(k == KT - 1))
            last.then_inc(slab_done[j], 1)

        def norm_squares(act, sq, parts):
            for n in parts:
                act.activation(sq[:, 2 * n:2 * n + 2], xT[:, 2 * n:2 * n + 2], ACT.Square).then_inc(norm_sq, 1)

        def norm_scalar(act, u, sq, shift=None, first=0):
            norm_squares(act, sq, range(first, 4))
            act.wait_ge(norm_sum, u + 1)
            act.activation(T[:, 0], px[0][:], ACT.Sqrt, bias=EPS, scale=1.0 / D).then_inc(norm_root, 1)
            for k in range(KT):
                act.wait_ge(norm_val, 8 * u + k + 1)
                if shift is None:
                    ins = act.copy(h_hi[:, k], sq[:, k])
                else:
                    ins = act.activation(h_hi[:, k], sq[:, k], ACT.Identity, bias=shift(k))
                ins.then_inc(norm_hi, 1)

        def norm_tensor(pe, u, sq):
            for n in range(4):
                pe.wait_ge(norm_sq, 4 * u + n + 1)
                for k in range(2 * n, 2 * n + 2):
                    last = pe.matmul(px[0][:], ones[:], sq[:, k], start=(k == 0), stop=(k == KT - 1))
            last.then_inc(norm_sum, 1)

        def norm_tail(pe, u, sq):
            pe.wait_ge(norm_added, 2 * u)
            for k in (0, 1):
                pe.matmul(px[0][:], ones[:], sq[:, k], start=(k == 0), stop=False)
            pe.wait_ge(norm_sq, 4 * u + 4)
            for k in (6, 7):
                last = pe.matmul(px[0][:], ones[:], sq[:, k], start=False, stop=(k == 7))
            last.then_inc(norm_sum, 1)

        def norm_add(dve, u, sq):
            for n in (1, 2):
                dve.wait_ge(norm_sq, 4 * u + n + 1)
                dve.tensor_tensor(sq[:, 0:2], sq[:, 0:2], sq[:, 2 * n:2 * n + 2], ALU.add).then_inc(norm_added, 1)
                dve.wait_ge(norm_added, 2 * (u - 1) + n)

        def slabs_to_x(pe, m, hi, lo, ready, u, sq):
            for n in range(4):
                slab_rows(pe, m + n // 2, n % 2, hi, lo, ready if n == 0 else None)
            norm_tail(pe, u, sq)

        def slabs_to_x_scalar(act, m, sq):
            for n in range(4):
                split_next(act, m + n // 2, n % 2)
                if n:
                    act.wait_ge(slab_out[(n - 1) % 2], m + (n - 1) // 2 + 1)
                    norm_squares(act, sq, [n - 1])
            act.wait_ge(slab_out[1], m + 2)

        def norm_vector(dve, v, u, sq, gain, shift=None):
            dve.wait_ge(norm_root, u + 1)
            v(dve.reciprocal(T[:, 1], T[:, 0]))
            for step in range(KT + 1):
                if step < KT:
                    dve.scalar_tensor_tensor(sq[:, step], xT[:, step], gain(step), T[:, 1], ALU.mult,
                                             ALU.mult).then_inc(norm_val, 1)
                if step == 0:
                    continue
                k = step - 1
                dve.wait_ge(norm_hi, 8 * u + k + 1)
                if shift is None:
                    ins = dve.tensor_tensor(h_lo[:, k], sq[:, k], h_hi[:, k].bitcast(F32), ALU.subtract)
                else:
                    ins = dve.scalar_tensor_tensor(h_lo[:, k], sq[:, k], shift(k),
                                                   h_hi[:, k].bitcast(F32), ALU.add, ALU.subtract)
                ins.then_inc(h_ready, 1)
            dve.wait_ge(h_ready, 8 * u + 8)

        Y = sb("Y", [P, KT, TOK])
        stage = ExitStack()
        c1 = sb("c1", [P, C1_COLS], ctx=stage)
        blk = sb("blk", [P, P], ctx=stage)
        M = sb("M", [P, 36, TOK], ctx=stage)
        small = sb("small", [P, 64], ctx=stage)
        fl = sb("fl", [P, TOK], ctx=stage)

        A = M[:, 0:8]
        B_dec, B_a, kk = M[:, 8:10], M[:, 10:12], M[:, 12:14]
        cum = M[:, 14:16]
        G = M[:, 4:20]
        g_out, bonus = M[:, 20:22], M[:, 22:24]
        QR = M[:, 24:28].rearrange("p (a b) n -> p a b n", a=2)
        b_s, k_s = M[:, 28:30], M[:, 30:32]
        CT, YS = b_s, k_s
        v_tok = M[:, 32:34].rearrange("p a (b c) -> p (a b) c", b=2)
        k_tok = M[:, 34:36].rearrange("p a (b c) -> p (a b) c", b=2)
        b_tok = M[:, 2:4].rearrange("p a (b c) -> p (a b) c", b=2)
        OT = M[:, 28:30]
        X, XT = Y[:, 0:4], Y[:, 4:8]
        S_old, W_sb, U_sb, S_bd = T[:, 0, 0:256], T[:, 1, 0:256], T[:, 1, 256:512], T[:, 2, 0:256]
        d_end = small[:, 0:16].rearrange("p (a b) -> p a b", a=2)
        lru_x, lru_g = M[:, 0:2], M[:, 30:32]
        xc, lr, li, la, lb, lh = (M[:, n:n + 2] for n in (6, 8, 10, 12, 14, 16))
        q_raw, k_att = M[:, 24:28], M[:, 2:6]
        v_att = M[:, 32:36]
        o_att = M[:, 28:32]
        sq_att = Y[:, 2:6]
        qk_rstd = T[0:16, 3]
        spread = Y[0:16, 0:2].rearrange("p a n -> p (a n)")
        fl_a, fl_b = Y[0:8, 0], Y[0:8, 1]
        probs, probsT = M[:, 6:10], M[:, 10:14]

        def qz(h):
            return M[:, 18 + h] if h < 6 else M[:, h - 6]

        maskneg = c1[:, C1["causal"]]

        def cc(name):
            return c1[:, C1[name]]

        def item(h, b):
            return b * HEADS + h

        c_loaded = sem("c_loaded")
        shifted, lora_in, lora_w, lora_a, lora_g = (sem(n) for n in (
            "shifted", "lora_in", "lora_w", "lora_a", "lora_g"))
        dec_out, gate_a, gate_g = sem("dec_out"), sem("gate_a"), sem("gate_g")
        kk_raw, kk_sq, kk_sum, kk_root = sem("kk_raw"), sem("kk_sq"), sem("kk_sum"), sem("kk_root")
        bonus_in, bonus_sum, cum_ready, prev_ready = (sem(n) for n in (
            "bonus_in", "bonus_sum", "cum_ready", "prev_ready"))
        decays, scaled = sem("decays"), sem("scaled")
        tr_done, tr_out = sem("tr_done"), sem("tr_out")
        gram_done, gram_out, x0_out, x0_ready = (sem(n) for n in (
            "gram_done", "gram_out", "x0_out", "x0_ready"))
        ct_ready, ct_x, ct_x_out, x_ct_x, x_next = (sem(n) for n in (
            "ct_ready", "ct_x", "ct_x_out", "x_ct_x", "x_next"))
        seq_w, seq_w_out, seq_u, seq_u_out, seq_s, seq_s_out, seq_o, seq_o_out = (sem(n) for n in (
            "seq_w", "seq_w_out", "seq_u", "seq_u_out", "seq_s", "seq_s_out", "seq_o", "seq_o_out"))
        ln_mean, ln_cen, ln_sq, ln_var, ln_root, y_rwkv = (sem(n) for n in (
            "ln_mean", "ln_cen", "ln_sq", "ln_var", "ln_root", "y_rwkv"))
        lru_xc, lru_gates, lru_acts, lru_sqrt_in, lru_b, lru_val, lru_sq, lru_sum, lru_root, y_lru = (
            sem(n) for n in ("lru_xc", "lru_gates", "lru_acts", "lru_sqrt_in", "lru_b", "lru_val",
                             "lru_sq", "lru_sum", "lru_root", "y_lru"))
        lru_gelu = sem("lru_gelu")
        qk_inv, qk_spread = sem("qk_inv"), sem("qk_spread")
        qk_sq, qk_sum, qk_root, qk_ready, fl_soft, negc_ready = (sem(n) for n in (
            "qk_sq", "qk_sum", "qk_root", "qk_ready", "fl_soft", "negc_ready"))
        sc_done, sc_max, sc_exp, sc_prob, sc_tr, sc_tr_out, sc_pv, pair_out = (sem(n) for n in (
            "sc_done", "sc_max", "sc_exp", "sc_prob", "sc_tr", "sc_tr_out", "sc_pv", "pair_out"))
        fox_sq, fox_sum, fox_root, y_fox, fl_in = (sem(n) for n in (
            "fox_sq", "fox_sum", "fox_root", "y_fox", "fl_in"))

        UNITS = [(h, qb) for h in range(8) for qb in range(TB)]

        mixers = ExitStack()
        block = mixers.enter_context(nc.Block())

        @block.sync
        def _(sp):
            for n in range(4):
                sp.dma_start(xT[:, 2 * n:2 * n + 2], t["x"][:, 2 * n:2 * n + 2]).then_inc(x_loaded[n], 16)
            sp.dma_start(ones[:], t["ones"]).then_inc(vec_loaded, 16)
            sp.dma_start(vec[:], t["vec1"]).then_inc(vec_loaded, 16)
            for j in range(2):
                sp.dma_start(raw[j][:], t["slabs"][j]).then_inc(raw_loaded[j], 16)
            sp.dma_start(c1[:], t["c1"]).then_inc(c_loaded, 16)
            sp.dma_start(blk[:], t["blk"]).then_inc(c_loaded, 16)
            sp.dma_start(ident[:], t["ident"]).then_inc(c_loaded, 16)
            with sp.Fori(1, IN1_PAIRS + 1) as m:
                for j in range(2):
                    sp.wait_ge(w_lo_ready[j], m)
                    sp.dma_start(raw[j][:], t["slabs"][bass.ds(2 * m + j, 1)]).then_inc(raw_loaded[j], 16)

        @block.gpsimd
        def _(pool):
            pool.memset(fl[:], 0.0).then_inc(fl_in, 1)
            with pool.Fori(0, IN1_PAIRS) as m:
                for j in range(2):
                    remainder(pool, m, j)
            remainder(pool, IN1_PAIRS, 0)

        @block.tensor
        def _(pe):
            pe.wait_ge(vec_loaded, 32)
            norm_tensor(pe, 0, M[:, 0:8])
            for m in range(2):
                for j in range(2):
                    slab_rows(pe, m, j, h_hi, h_lo, (h_ready, 0) if m + j == 0 else None)

            def pieces(m, j, first, count):
                if first == 0:
                    slab_starts(pe, m, j)
                for k in range(first, first + count):
                    slab_piece(pe, j, k, h_hi, h_lo)

            pieces(2, 0, 0, 4)
            pe.wait_ge(c_loaded, 48)
            pe.wait_ge(lora_in, 1)
            lora = cc("lora")
            for n, (rows, done) in enumerate(((slice(0, 32), lora_w), (slice(32, 64), lora_a))):
                for j in range(2):
                    last = pe.matmul(px[2 * n + j][:], lora[rows, j * P:(j + 1) * P], T[rows, 3],
                                     start=True, stop=True)
                last.then_inc(done, 1)
            pieces(2, 0, 4, 2)
            pe.wait_ge(dec_out, 2)
            for j in range(2):
                last = pe.matmul(px[j][:], lora[64:128, j * P:(j + 1) * P], T[64:128, 3],
                                 start=True, stop=True)
            last.then_inc(lora_g, 1)
            pieces(2, 0, 6, 2)
            pe.wait_ge(gate_a, 2)
            for j in range(2):
                pe.wait_ge(kk_sq, j + 1)
                pe.matmul(px[2 + j][:], blk[:], T[:, j], start=True, stop=True).then_inc(kk_sum, 1)
            pieces(2, 1, 0, 4)
            pe.wait_ge(gate_g, 2)
            for j in range(2):
                pe.wait_ge(bonus_in, j + 1)
                pe.matmul(px[j][:], blk[:], bonus[:, j], start=True, stop=True).then_inc(bonus_sum, 1)
            pieces(2, 1, 4, 4)
            pe.wait_ge(scaled, 2)
            n = 0
            for src in (A[:, 4:6], k_s, b_s):
                for j in range(2):
                    if n >= 4:
                        pe.wait_ge(tr_out, n - 3)
                    for b in range(TB):
                        last = pe.transpose(px[n % 4][:, b * P:(b + 1) * P], src[:, j, b * P:(b + 1) * P],
                                            ident[:])
                    last.then_inc(tr_done, 1)
                    n += 1
            pe.wait_ge(tr_out, 6)
            for b in range(TB):
                toks = slice(b * P, (b + 1) * P)
                for h in range(HEADS):
                    i, j, rows = item(h, b), h // 2, slice(64 * (h % 2), 64 * (h % 2) + 64)
                    if i >= 2:
                        pe.wait_ge(gram_out, i - 1)
                    if h == 0 and b >= 1:
                        pe.wait_ge(x0_out, b)
                    qr = QR[rows, j, :, toks]
                    pe.matmul(px[i % 2][:, 0:256], b_s[rows, j, toks], qr, start=True, stop=True)
                    pe.matmul(px[i % 2][:, 256:512], k_s[rows, j, toks], qr, start=True, stop=True)
                    pe.matmul(px[2 + h % 2][:, j * P:(j + 1) * P], QR[rows, j, 0, toks],
                              b_s[rows, j, toks], start=True, stop=True).then_inc(gram_done, 1)
            pe.wait_ge(x0_ready, 4)
            pe.wait_ge(slab_out[0], 3)
            with pe.Fori(0, INVERSE_LEVELS) as lv:
                def first_product(b):
                    pe.wait_ge(ct_ready, 4 * lv + b + 1)
                    for h in range(HEADS):
                        s = slice(h * P, (h + 1) * P)
                        last = pe.matmul(pd[b % 2][:, s], CT[:, b % 2, s], X[:, b, s], start=True, stop=True)
                    last.then_inc(ct_x, 1)

                def second_products(b):
                    pe.wait_ge(ct_x_out, 4 * lv + b + 1)
                    if b >= 2:
                        pe.wait_ge(x_next, 4 * lv + b - 1)
                    for h in range(HEADS):
                        s = slice(h * P, (h + 1) * P)
                        pe.matmul(px[2 * (b % 2)][:, s], XT[:, b, s], YS[:, b % 2, s], start=True, stop=True)
                        last = pe.matmul(px[2 * (b % 2) + 1][:, s], YS[:, b % 2, s], XT[:, b, s],
                                         start=True, stop=True)
                    last.then_inc(x_ct_x, 1)

                first_product(0)
                for b in range(1, TB):
                    first_product(b)
                    second_products(b - 1)
                second_products(TB - 1)
            pe.wait_ge(x_next, 4 * INVERSE_LEVELS)
            for c in range(NCH):
                b, u = c // 2, c % 2
                rows, toks = slice(u * CH, (u + 1) * CH), slice(c * CH, (c + 1) * CH)
                own = slice(u * CH, (u + 1) * CH)
                pe.wait_ge(seq_s_out, c + 1)
                for j in range(2):
                    pe.matmul(px[0][rows, j * P:(j + 1) * P], QR[:, j, 0, toks], S_bd[:, j * P:(j + 1) * P],
                              start=(j == 0), stop=False, skip_group_check=True)
                for h in range(HEADS):
                    last = pe.matmul(px[0][rows, h * CH:(h + 1) * CH], G[:, item(h, b), 256:384][:, own],
                                     v_tok[:, b, h * CH:(h + 1) * CH], start=False, stop=(h == HEADS - 1),
                                     skip_group_check=True)
                last.then_inc(seq_w, 1)
                pieces(3, c // 4, 2 * c % 8, 1)
                for j in range(2):
                    pe.matmul(px[2][:, j * P:(j + 1) * P], k_tok[rows, b, j * P:(j + 1) * P],
                              v_tok[rows, b, j * P:(j + 1) * P], start=(j == 0), stop=False,
                              skip_group_check=True)
                if c:
                    pe.wait_ge(seq_o_out, c)
                for j in range(2):
                    pe.matmul(px[3][:, j * CH:(j + 1) * CH], S_bd[:, j * P:(j + 1) * P], QR[:, j, 1, toks],
                              start=(j == 0), stop=False, skip_group_check=True)
                for h in range(HEADS):
                    pe.matmul(px[3][64 * (h % 2):64 * (h % 2) + 64, (h // 2) * CH:(h // 2 + 1) * CH],
                              v_tok[:, b, h * CH:(h + 1) * CH], G[:, item(h, b), 384:512][:, own],
                              start=False, stop=False, skip_group_check=True)
                pe.wait_ge(seq_w_out, c + 1)
                for h in range(HEADS):
                    last = pe.matmul(px[1][rows, h * CH:(h + 1) * CH], XT[:, b, h * P:(h + 1) * P][:, own],
                                     W_sb[:, h * CH:(h + 1) * CH], start=(h == 0), stop=(h == HEADS - 1),
                                     skip_group_check=True)
                last.then_inc(seq_u, 1)
                pieces(3, c // 4, 2 * c % 8 + 1, 1)
                pe.wait_ge(seq_u_out, c + 1)
                for j in range(2):
                    last = pe.matmul(px[2][:, j * P:(j + 1) * P], b_tok[rows, b, j * P:(j + 1) * P],
                                     U_sb[rows, j * P:(j + 1) * P], start=False, stop=(j == 1),
                                     skip_group_check=True)
                last.then_inc(seq_s, 1)
                for h in range(HEADS):
                    last = pe.matmul(px[3][64 * (h % 2):64 * (h % 2) + 64, (h // 2) * CH:(h // 2 + 1) * CH],
                                     U_sb[:, h * CH:(h + 1) * CH], G[:, item(h, b), 128:256][:, own],
                                     start=False, stop=(h == HEADS - 1), skip_group_check=True)
                last.then_inc(seq_o, 1)
            pe.wait_ge(seq_o_out, NCH)
            for j in range(2):
                pe.matmul(px[j][:], blk[:], OT[:, j], start=True, stop=True).then_inc(ln_mean, 1)
            slab_rows(pe, 4, 0, h_hi, h_lo)
            for j in range(2):
                pe.wait_ge(ln_sq, j + 1)
                pe.matmul(px[2 + j][:], blk[:], T[:, 2 + j], start=True, stop=True).then_inc(ln_var, 1)

            pe.wait_ge(ln_cen, 2)
            pe.wait_ge(ln_root, 2)
            for n, name in enumerate(("lru_wa", "lru_wx")):
                for j in range(2):
                    if n == 0:
                        pe.wait_ge(lru_xc, j + 1)
                    pe.matmul(px[2 * n + j][:], cc(name)[:, j * P:(j + 1) * P], xc[:, j],
                              start=True, stop=True).then_inc(lru_gates, 1)
            slab_rows(pe, 4, 1, h_hi, h_lo)
            pe.wait_ge(lru_acts, 4)
            for n in range(8):
                pe.wait_ge(qk_sq, n + 1)
                pe.matmul(px[0][0:16], cc("halves")[:, 16 - 2 * n:32 - 2 * n], sq_att[:, n % 4], start=(n == 0),
                          stop=(n == 7)).then_inc(qk_sum, 1)
            slab_tokens(pe, 5, 0, h_hi, h_lo)
            for j in range(2):
                pe.wait_ge(lru_sq, j + 1)
                last = pe.matmul(px[1][:], ones[:], T[:, j], start=(j == 0), stop=(j == 1))
            last.then_inc(lru_sum, 1)
            pe.wait_ge(qk_inv, 1)
            for n in range(8):
                if n == 3:
                    pe.wait_ge(lru_root, 1)
                if n >= 4:
                    pe.wait_ge(qk_ready, n - 3)
                pe.matmul(px[(n + 2) % 4][:], spread[:, n * P:(n + 1) * P],
                          qk_rstd, start=True, stop=True).then_inc(qk_spread, 1)
            slab_tokens(pe, 5, 1, h_hi, h_lo)
            pe.wait_ge(slab_out[0], 6)
            pe.wait_ge(slab_out[1], 6)
            pe.wait_ge(negc_ready, 1)
            pe.wait_ge(qk_ready, 8)

            def scores(n):
                h, qb = UNITS[n]
                if n >= 3:
                    pe.wait_ge(sc_exp, n - 2)
                keys = (qb + 1) * P
                out = pd[n % 3]
                pe.matmul(out[:, 0:keys], qz(h)[:, qb * P:(qb + 1) * P], k_att[:, h // 2, 0:keys],
                          start=True, stop=False)
                pe.matmul(out[:, keys - P:keys], ident[:], maskneg, start=False, stop=False)
                pe.matmul(out[:, 0:keys], ident[:, h:h + 1].to_broadcast([P, P]), fl[:, 0:keys],
                          start=False, stop=True).then_inc(sc_done, 1)

            def turn(n):
                h, qb = UNITS[n]
                pe.wait_ge(sc_prob, n + 1)
                if n >= 2:
                    pe.wait_ge(sc_tr_out, n - 1)
                for b in range(qb + 1):
                    last = pe.transpose(px[n % 2][:, b * P:(b + 1) * P], probs[:, n % 4, b * P:(b + 1) * P],
                                        ident[:])
                last.then_inc(sc_tr, 1)

            def weigh(n):
                h, qb = UNITS[n]
                pair, rows = h // 2, slice(64 * (h % 2), 64 * (h % 2) + 64)
                pe.wait_ge(sc_tr_out, n + 1)
                if pair >= 2 and h % 2 == 0 and qb == 0:
                    pe.wait_ge(pair_out, pair - 1)
                for b in range(qb + 1):
                    last = pe.matmul(px[2 + pair % 2][rows, qb * P:(qb + 1) * P],
                                     v_att[:, b, h * 64:(h + 1) * 64], probsT[:, n % 4, b * P:(b + 1) * P],
                                     start=(b == 0), stop=(b == qb), skip_group_check=True)
                last.then_inc(sc_pv, 1)

            for n in range(len(UNITS) + 3):
                if n < len(UNITS):
                    scores(n)
                if 2 <= n < len(UNITS) + 2:
                    turn(n - 2)
                if n >= 3:
                    weigh(n - 3)
            for k in range(4):
                pe.wait_ge(fox_sq, k + 1)
                last = pe.matmul(px[0][:], ones[:], sq_att[:, k], start=(k == 0), stop=(k == 3))
            last.then_inc(fox_sum, 1)

        @block.scalar
        def _(act):
            a = steps["scalar"] = Steps(act, scalar_steps)
            for n in range(4):
                act.wait_ge(x_loaded[n], 16)
                norm_squares(act, M[:, 0:8], [n])
            split(act, 0, 0)
            norm_scalar(act, 0, M[:, 0:8], first=4)
            act.wait_ge(vec_loaded, 32)
            act.wait_ge(h_ready, 8)
            def store(m, j, dst):
                act.wait_ge(slab_done[j], m + 1)
                for f in range(2):
                    last = act.copy(dst[:, f], pd[2 * j + f][:])
                last.then_inc(slab_out[j], 1)

            for m in range(2):
                for j in range(2):
                    split_next(act, m, j)
                    act.wait_ge(slab_done[j], m + 1)
                    n = 2 * m + j
                    act.copy(A[:, 2 * n], pd[2 * j][:])
                    if n < 3:
                        last = act.copy(A[:, 2 * n + 1], pd[2 * j + 1][:])
                    else:
                        act.wait_ge(fl_in, 1)
                        last = act.activation(fl[0:8], pd[2 * j + 1][0:8], ACT.Identity,
                                              bias=v1("fox_fb", rows=slice(0, 8)))
                    last.then_inc(slab_out[j], 1)
            act.wait_ge(shifted, 7)
            act.activation(T[0:32, 3], A[0:32, 6], ACT.Tanh)
            act.copy(T[32:64, 3], A[32:64, 6])
            act.activation(T[64:128, 3], A[64:128, 6], ACT.Sigmoid).then_inc(lora_in, 1)
            split_next(act, 2, 0)
            act.wait_ge(lora_w, 1)
            for j in range(2):
                act.activation(B_dec[:, j], px[j][:], ACT.Sigmoid, bias=v1("w0", j)).then_inc(dec_out, 1)
            act.wait_ge(lora_a, 1)
            for j in range(2):
                act.activation(B_a[:, j], px[2 + j][:], ACT.Sigmoid, bias=v1("a0", j)).then_inc(gate_a, 1)
            act.wait_ge(lora_g, 1)
            for j in range(2):
                act.copy(g_out[:, j], px[j][:]).then_inc(gate_g, 1)
            for j in range(2):
                act.wait_ge(kk_raw, j + 1)
                act.activation(T[:, j], kk[:, j], ACT.Square).then_inc(kk_sq, 1)
            for j in range(2):
                act.wait_ge(kk_sum, j + 1)
                act.activation(T[:, j], px[2 + j][:], ACT.Sqrt).then_inc(kk_root, 1)
            for j in range(2):
                act.wait_ge(cum_ready, j + 1)
                act.activation(QR[:, j, 1], cum[:, j], ACT.Exp)
                act.activation(k_s[:, j], cum[:, j], ACT.Exp, scale=-1.0)
                act.activation(d_end[:, j], cum[:, j, CH - 1::CH], ACT.Exp)
                act.wait_ge(prev_ready, j + 1)
                act.activation(QR[:, j, 0], b_s[:, j], ACT.Exp).then_inc(decays, 1)
            for n, dst in enumerate((v_tok, v_tok, k_tok, k_tok, b_tok, b_tok)):
                act.wait_ge(tr_done, n + 1)
                act.mul(dst[:, :, (n % 2) * P:(n % 2 + 1) * P], px[n % 4][:].rearrange(
                    "p (a b) -> p a b", a=TB), -1.0 if n >= 4 else 1.0).then_inc(tr_out, 1)
            act.wait_ge(scaled, 2)
            store(2, 0, lru_x)
            split_next(act, 2, 1)
            with act.Fori(0, INVERSE_LEVELS) as lv:
                for b in range(TB):
                    act.wait_ge(ct_x, 4 * lv + b + 1)
                    act.copy(YS[:, b % 2], pd[b % 2][:]).then_inc(ct_x_out, 1)

            soft = small[:, 16:18]
            lam = vec[:, V1["lru_lambda"]]
            a(act.activation(small[:, 20:22], lam, ACT.Abs))
            a(act.activation(small[:, 20:22], small[:, 20:22], ACT.Exp, scale=-1.0))
            a(act.activation(small[:, 20:22], small[:, 20:22], ACT.Ln, bias=1.0))
            a(act.activation(small[:, 22:24], lam, ACT.Relu, scale=-1.0))
            for j in range(2):
                a(act.activation(soft[:, j:j + 1], small[:, 20 + j:21 + j], ACT.Identity,
                                 bias=small[:, 22 + j:23 + j]))
            a(act.mul(small[:, 16:18], small[:, 16:18], 8.0))
            a(act.mul(small[:, 18:20], small[:, 16:18], -1.0))
            act.wait_ge(x_next, 4 * INVERSE_LEVELS)
            store(2, 1, lru_g)
            split_next(act, 3, 0)
            for c in range(NCH):
                act.wait_ge(seq_o, c + 1)
                act.copy(OT[:, :, c * CH:(c + 1) * CH], px[3][:, 0:2 * CH].rearrange(
                    "p (a b) -> p a b", a=2)).then_inc(seq_o_out, 1)
                if c == 4:
                    split_next(act, 3, 1)
            store(3, 0, q_raw[:, 0:2])
            store(3, 1, q_raw[:, 2:4])
            split_next(act, 4, 0)
            for j in range(2):
                act.wait_ge(ln_cen, j + 1)
                act.activation(T[:, 2 + j], T[:, j], ACT.Square).then_inc(ln_sq, 1)
            for j in range(2):
                act.wait_ge(ln_var, j + 1)
                act.activation(T[:, 2 + j], px[2 + j][:], ACT.Sqrt, bias=GN_EPS,
                               scale=1.0 / CH).then_inc(ln_root, 1)

            for j in range(2):
                act.wait_ge(lru_gates, 1 + j)
                act.activation(lr[:, j], px[j][:], ACT.Sigmoid, bias=v1("lru_ba", j)).then_inc(lru_acts, 1)
            for j in range(2):
                act.wait_ge(lru_gates, 3 + j)
                act.activation(li[:, j], px[2 + j][:], ACT.Sigmoid, bias=v1("lru_bx", j)).then_inc(lru_acts, 1)
            act.wait_ge(lru_acts, 4)
            for j in range(2):
                act.activation(la[:, j], lr[:, j], ACT.Exp, scale=small[:, 18 + j:19 + j])
                act.activation(lb[:, j], lr[:, j], ACT.Tanh, scale=small[:, 16 + j:17 + j]).then_inc(lru_b, 1)
            store(4, 0, k_att[:, 0:2])
            split_next(act, 4, 1)
            for j in range(2):
                act.wait_ge(lru_sqrt_in, j + 1)
                act.activation(lb[:, j], lb[:, j], ACT.Sqrt, scale=2.0).then_inc(lru_b, 1)
            for j in range(2):
                act.activation(lr[:, j], lru_g[:, j], ACT.Gelu_apprx_tanh).then_inc(lru_gelu, 1)

            for n in range(8):
                if n == 4:
                    store(4, 1, k_att[:, 2:4])
                    act.wait_ge(slab_out[0], 5)
                    act.wait_ge(slab_out[1], 5)
                    split_next(act, 5, 0)
                if n >= 4:
                    act.wait_ge(qk_sum, n - 3)
                act.activation(sq_att[:, n % 4], (q_raw if n < 4 else k_att)[:, n % 4],
                               ACT.Square).then_inc(qk_sq, 1)
            a(act.activation(fl_a, fl[0:8], ACT.Abs))
            a(act.activation(fl_a, fl_a, ACT.Exp, scale=-1.0))
            a(act.activation(fl_a, fl_a, ACT.Ln, bias=1.0))
            a(act.activation(fl_b, fl[0:8], ACT.Relu, scale=-1.0), fl_soft, 1)
            act.wait_ge(qk_sum, 8)
            act.wait_ge(y_rwkv, 2)
            act.activation(qk_rstd, px[0][0:16], ACT.Sqrt, bias=EPS, scale=1.0 / 64).then_inc(qk_root, 1)
            for j in range(2):
                act.wait_ge(lru_val, j + 1)
                act.activation(T[:, j], lh[:, j], ACT.Square).then_inc(lru_sq, 1)
            for j in range(2):
                act.wait_ge(slab_done[j], 6)
                for i in range(2):
                    last = act.copy(v_att[:, 2 * i:2 * i + 2, j * SLAB_COLS:(j + 1) * SLAB_COLS],
                                    pd[2 * j + i][:].rearrange("p (a b) -> p a b", a=2))
                last.then_inc(slab_out[j], 1)
                if j == 1:
                    split_next(act, 5, 1)
                if j == 0:
                    act.wait_ge(lru_sum, 1)
                    act.activation(T[:, 2], px[1][:], ACT.Sqrt, bias=EPS, scale=1.0 / 256).then_inc(lru_root, 1)
            act.wait_ge(y_lru, 2)

            def copy_turned(n):
                keys = (UNITS[n][1] + 1) * P
                act.wait_ge(sc_tr, n + 1)
                if n >= 4:
                    act.wait_ge(sc_pv, n - 3)
                act.copy(probsT[:, n % 4, 0:keys], px[n % 2][:, 0:keys]).then_inc(sc_tr_out, 1)

            def pair_store(pair):
                act.wait_ge(sc_pv, 8 * pair + 8)
                act.copy(o_att[:, pair], px[2 + pair % 2][:]).then_inc(pair_out, 1)

            for n in range(len(UNITS) + 3):
                if n < len(UNITS):
                    keys = (UNITS[n][1] + 1) * P
                    act.wait_ge(sc_max, n + 1)
                    if n >= 4:
                        act.wait_ge(sc_tr, n - 3)
                    act.activation(probs[:, n % 4, 0:keys], pd[n % 3][:, 0:keys], ACT.Exp,
                                   bias=small[:, 32 + n % 4:33 + n % 4],
                                   accum_out=small[:, 36 + n % 4:37 + n % 4]).then_inc(sc_exp, 1)
                if 2 <= n < len(UNITS) + 2:
                    copy_turned(n - 2)
                if n >= 4 and (n - 4) % 8 == 7:
                    pair_store((n - 4) // 8)
            pair_store(3)
            act.wait_ge(pair_out, 4)
            for k in range(4):
                act.activation(sq_att[:, k], o_att[:, k], ACT.Square).then_inc(fox_sq, 1)
            act.wait_ge(fox_sum, 1)
            act.activation(T[:, 0], px[0][:], ACT.Sqrt, bias=EPS, scale=1.0 / 512).then_inc(fox_root, 1)

        @block.vector
        def _(dve):
            v = steps["vector"] = Steps(dve, vector_steps)
            dve.wait_ge(vec_loaded, 32)
            norm_vector(dve, v, 0, M[:, 0:8], lambda k: v1("norm1", k))
            v(dve.tensor_scalar(small[:, 24:26], vec[:, V1["ka"]], -1.0, 1.0, ALU.mult, ALU.add))
            for n in range(7):
                if n % 2 == 0:
                    dve.wait_ge(slab_out[(n // 2) % 2], n // 4 + 1)
                dve.tensor_tensor(T[:, n % 2, 1:TOK], A[:, n, 0:TOK - 1], A[:, n, 1:TOK], ALU.subtract)
                v(dve.tensor_scalar(T[:, n % 2, 0:1], A[:, n, 0:1], -1.0, None, ALU.mult))
                v(dve.scalar_tensor_tensor(A[:, n], T[:, n % 2], v1("mu", n), A[:, n], ALU.mult, ALU.add),
                  shifted, n + 1)
            for j in range(2):
                v(dve.tensor_scalar(kk[:, j], A[:, 2 + j], v1("kk", j), None, ALU.mult), kk_raw, j + 1)
            dve.wait_ge(dec_out, 2)
            v(dve.tensor_scalar(B_dec[:], B_dec[:], LOG_DECAY, None, ALU.mult))
            for j in range(2):
                for c in range(NCH):
                    s = slice(c * CH, (c + 1) * CH)
                    last = dve.tensor_tensor_scan(cum[:, j, s], ones[:, 0:CH], B_dec[:, j, s], 0.0,
                                                  ALU.mult, ALU.add)
                v(last, cum_ready, j + 1)
                v(dve.tensor_tensor(b_s[:, j], cum[:, j], B_dec[:, j], ALU.subtract), prev_ready, j + 1)
            dve.wait_ge(gate_a, 2)
            for j in range(2):
                dve.wait_ge(kk_root, j + 1)
                v(dve.tensor_scalar(T[:, 2], B_a[:, j], v1("ka", j), small[:, 24 + j:25 + j], ALU.mult, ALU.add))
                v(dve.tensor_tensor(A[:, 2 + j], A[:, 2 + j], T[:, 2], ALU.mult))
                v(dve.scalar_tensor_tensor(bonus[:, j], A[:, j], v1("rk", j), A[:, 2 + j], ALU.mult, ALU.mult),
                  bonus_in, j + 1)
                v(dve.tensor_scalar(T[:, j], T[:, j], 1e-12, None, ALU.max))
                v(dve.reciprocal(T[:, j], T[:, j]))
                v(dve.tensor_tensor(kk[:, j], kk[:, j], T[:, j], ALU.mult))
                v(dve.tensor_tensor(B_a[:, j], B_a[:, j], kk[:, j], ALU.mult))
            for j in range(2):
                dve.wait_ge(bonus_sum, j + 1)
                v(dve.tensor_tensor(bonus[:, j], px[j][:], A[:, 4 + j], ALU.mult))
            for j in range(2):
                dve.wait_ge(decays, j + 1)
                dve.tensor_tensor(QR[:, j, 1], QR[:, j, 1], A[:, j], ALU.mult)
                dve.tensor_tensor(QR[:, j, 0], QR[:, j, 0], kk[:, j], ALU.mult)
                v(dve.tensor_tensor(b_s[:, j], B_a[:, j], k_s[:, j], ALU.mult))
                v(dve.tensor_tensor(k_s[:, j], A[:, 2 + j], k_s[:, j], ALU.mult), scaled, j + 1)
            dve.wait_ge(c_loaded, 48)
            dve.wait_ge(tr_out, 6)
            for b in range(TB):
                for h in range(HEADS):
                    i = item(h, b)
                    dve.wait_ge(gram_done, i + 1)
                    v(dve.tensor_tensor(G[:, i], px[i % 2][:], cc("gram"), ALU.mult), gram_out, i + 1)
                four = lambda ap: ap.unsqueeze(1).to_broadcast([P, HEADS, P])
                tiles = lambda ap: ap.rearrange("p (a b) -> p a b", a=HEADS)
                by_head = X[:, b].rearrange("p (j u n) -> p j u n", j=2, u=2)
                for u in range(2):
                    ins = dve.tensor_tensor(by_head[:, :, u], px[2 + u][:, 0:256].rearrange("p (j n) -> p j n", j=2),
                                            cc("x0").unsqueeze(1).to_broadcast([P, 2, P]), ALU.mult)
                v(ins, x0_out, b + 1)
                v(dve.tensor_tensor(tiles(XT[:, b]), G[:, 4 * b:4 * b + 4, 0:P], four(cc("x0t")), ALU.mult))
                dve.tensor_tensor(tiles(X[:, b]), tiles(X[:, b]), four(ident[:]), ALU.add)
                v(dve.tensor_tensor(tiles(XT[:, b]), tiles(XT[:, b]), four(ident[:]), ALU.add), x0_ready, b + 1)
            levels = cc("levels")
            with dve.Fori(0, INVERSE_LEVELS) as lv:
                def mask(b):
                    m = levels[:, bass.ds(lv * P, P)].unsqueeze(1).to_broadcast([P, HEADS, P])
                    v(dve.tensor_tensor(tiles(CT[:, b % 2]), G[:, 4 * b:4 * b + 4, 0:P], m, ALU.mult),
                      ct_ready, 4 * lv + b + 1)

                def update(b):
                    dve.wait_ge(x_ct_x, 4 * lv + b + 1)
                    dve.tensor_tensor(X[:, b], X[:, b], px[2 * (b % 2)][:], ALU.subtract)
                    v(dve.tensor_tensor(XT[:, b], XT[:, b], px[2 * (b % 2) + 1][:], ALU.subtract),
                      x_next, 4 * lv + b + 1)

                mask(0)
                mask(1)
                update(0)
                mask(2)
                update(1)
                mask(3)
                update(2)
                update(3)
            dve.memset(W_sb, 0.0)
            dve.memset(U_sb, 0.0)
            dve.memset(S_old, 0.0)
            v(dve.memset(S_bd, 0.0), seq_s_out, 1)
            for c in range(NCH):
                rows = slice((c % 2) * CH, (c % 2 + 1) * CH)
                dve.wait_ge(seq_w, c + 1)
                v(dve.tensor_copy(W_sb[rows], px[0][rows, 0:256]), seq_w_out, c + 1)
                dve.wait_ge(seq_u, c + 1)
                if c:
                    dve.wait_ge(seq_o, c)
                v(dve.tensor_copy(U_sb[rows], px[1][rows, 0:256]), seq_u_out, c + 1)
                for j in range(2):
                    last = dve.tensor_scalar(S_old[:, j * P:(j + 1) * P], S_bd[:, j * P:(j + 1) * P],
                                             d_end[:, j, c:c + 1], None, ALU.mult)
                v(last)
                dve.wait_ge(seq_s, c + 1)
                for j in range(2):
                    for u in range(2):
                        head, cols = slice(64 * u, 64 * u + 64), slice(j * P + 64 * u, j * P + 64 * u + 64)
                        last = dve.scalar_tensor_tensor(S_bd[head, cols], px[2][head, cols],
                                                        d_end[head, j, c:c + 1], S_old[head, cols],
                                                        ALU.mult, ALU.add)
                v(last, seq_s_out, c + 2)
            for j in range(2):
                dve.wait_ge(ln_mean, j + 1)
                v(dve.scalar_tensor_tensor(T[:, j], px[j][:], -1.0 / CH, OT[:, j], ALU.mult, ALU.add), ln_cen, j + 1)
            dve.wait_ge(slab_out[0], 3)
            for j in range(2):
                v(dve.tensor_scalar(xc[:, j], lru_x[:, j], v1("conv_w", 6 + j), v1("conv_b", j), ALU.mult, ALU.add))
                for s in range(1, 4):
                    ins = dve.scalar_tensor_tensor(xc[:, j, s:TOK], lru_x[:, j, 0:TOK - s],
                                                   v1("conv_w", 2 * (3 - s) + j), xc[:, j, s:TOK],
                                                   ALU.mult, ALU.add)
                    if s < 3:
                        v(ins)
                    else:
                        v(ins, lru_xc, j + 1)
            for j in range(2):
                dve.wait_ge(ln_root, j + 1)
                v(dve.reciprocal(T[:, 2 + j], T[:, 2 + j]))
                v(dve.scalar_tensor_tensor(T[:, j], T[:, j], v1("ln_g", j), T[:, 2 + j], ALU.mult, ALU.mult))
                v(dve.scalar_tensor_tensor(T[:, j], T[:, j], v1("ln_b", j), bonus[:, j], ALU.add, ALU.add))
                v(dve.tensor_tensor(Y[:, 6 + j], T[:, j], g_out[:, j], ALU.mult), y_rwkv, j + 1)

            dve.memset(M[:, 18:24], 0.0)
            v(dve.memset(M[:, 0:2], 0.0))
            v(dve.tensor_scalar(small[:, 30:31], v1("fox_qn"), 0.125, None, ALU.mult))
            for j in range(2):
                dve.wait_ge(lru_b, j + 1)
                v(dve.tensor_scalar(T[:, j], lb[:, j], 1.0, None, ALU.add))
                v(dve.reciprocal(T[:, j], T[:, j]))
                v(dve.tensor_tensor(lb[:, j], lb[:, j], T[:, j], ALU.mult), lru_sqrt_in, j + 1)
            for j in range(2):
                dve.wait_ge(lru_b, 3 + j)
                v(dve.tensor_tensor(li[:, j], li[:, j], xc[:, j], ALU.mult))
                v(dve.tensor_tensor(lb[:, j], lb[:, j], li[:, j], ALU.mult))
                v(dve.tensor_tensor_scan(lh[:, j], la[:, j], lb[:, j], 0.0, ALU.mult, ALU.add))
                dve.wait_ge(lru_gelu, j + 1)
                v(dve.tensor_tensor(lh[:, j], lh[:, j], lr[:, j], ALU.mult), lru_val, j + 1)
            dve.wait_ge(fl_soft, 1)
            v(dve.tensor_tensor(fl_a, fl_a, fl_b, ALU.add))
            v(dve.memset(fl_b, 1.0))
            v(dve.tensor_tensor_scan(fl[0:8], fl_b, fl_a, 0.0, ALU.mult, ALU.add), negc_ready, 1)
            v(dve.tensor_copy(spread.rearrange("p (h n) -> p h n", n=CH),
                              ident[0:16, 0:16].unsqueeze(2).to_broadcast([16, 16, CH])))
            dve.wait_ge(qk_root, 1)
            v(dve.reciprocal(qk_rstd, qk_rstd), qk_inv, 1)
            for n in range(8):
                dve.wait_ge(qk_spread, n + 1)
                inv = px[(n + 2) % 4]
                if n < 4:
                    for u in range(2):
                        rows = slice(64 * u, 64 * u + 64)
                        last = dve.scalar_tensor_tensor(qz(2 * n + u)[rows], q_raw[rows, n], small[rows, 30:31],
                                                        inv[rows], ALU.mult, ALU.mult)
                    v(last, qk_ready, n + 1)
                else:
                    v(dve.scalar_tensor_tensor(k_att[:, n - 4], k_att[:, n - 4], v1("fox_kn"), inv[:],
                                               ALU.mult, ALU.mult), qk_ready, n + 1)
            dve.wait_ge(lru_root, 1)
            v(dve.reciprocal(T[:, 2], T[:, 2]))
            for j in range(2):
                v(dve.scalar_tensor_tensor(Y[:, j], lh[:, j], v1("lru_norm", j), T[:, 2], ALU.mult, ALU.mult),
                  y_lru, j + 1)

            for n in range(len(UNITS) + 1):
                if n < len(UNITS):
                    keys = (UNITS[n][1] + 1) * P
                    dve.wait_ge(sc_done, n + 1)
                    if n >= 4:
                        dve.wait_ge(sc_exp, n - 3)
                    v(dve.tensor_reduce(small[:, 32 + n % 4:33 + n % 4], pd[n % 3][:, 0:keys], AX.X, ALU.max,
                                        negate=True), sc_max, n + 1)
                if n >= 1:
                    p = n - 1
                    keys = (UNITS[p][1] + 1) * P
                    dve.wait_ge(sc_exp, p + 1)
                    v(dve.reciprocal(small[:, 40 + p % 4:41 + p % 4], small[:, 36 + p % 4:37 + p % 4]))
                    v(dve.tensor_scalar(probs[:, p % 4, 0:keys], probs[:, p % 4, 0:keys],
                                        small[:, 40 + p % 4:41 + p % 4], None, ALU.mult), sc_prob, p + 1)
            dve.wait_ge(fox_root, 1)
            v(dve.reciprocal(T[:, 0], T[:, 0]))
            for k in range(4):
                v(dve.scalar_tensor_tensor(Y[:, 2 + k], o_att[:, k], v1("fox_norm", k), T[:, 0],
                                           ALU.mult, ALU.mult), y_fox, k + 1)

        mixers.close()
        stage.close()
        y_hi = sb("y_hi", [P, KT, TOK], F32R)
        y_lo = sb("y_lo", [P, KT, TOK], F32R)
        V, QK, MG = (sb(n, [P, KT, TOK]) for n in ("V", "QK", "MG"))
        O = Y
        v2 = sb("v2", [P, LAYERS, V2_COLS])
        mod = sb("mod", [P, LAYERS * ADA_COLS])
        b_ada = sb("b_ada", [P, LAYERS * ADA_COLS])
        swap = sb("swap", [P, P])
        lay = sb("lay", [P, V2_COLS + ADA_COLS + 16])
        small2 = sb("small2", [P, 64])
        V_tok = V[:].rearrange("p (b a) n -> p b (a n)", b=TB)
        MOD = V2_COLS
        GAIN = V2_COLS + ADA_COLS

        ada = QK[:].rearrange("p (j a) n -> p j (a n)", j=2)
        combT = V[0:PER_GROUP, 0:GROUPS]
        c_act = small2[:, 0:8]
        rt = T[:, 3]
        cos, sin, decT, decq = MG[:, 0], MG[:, 1], MG[:, 2], MG[:, 3]
        pos, ang, turns = MG[:, 4], MG[:, 5], MG[:, 6]
        SCT, KD, QD, ST, ST3 = MG[:, 4], MG[:, 5], MG[:, 6], MG[:, 7], T[:, 3]
        w_sgu, tri, b_sgu = QK[:, 5], QK[:, 6, 0:P], QK[:, 7]

        stage2_loaded = sem("stage2_loaded")
        ada_loaded, ada_part, ada_done = sem("ada_loaded"), sem("ada_part"), sem("ada_done")
        logits_out, logits_tr = sem("logits_out"), sem("logits_tr")
        logits, r_exp_in, r_exp, comb_ready, comb_tr, combT_ready = (sem(n) for n in (
            "logits", "r_exp_in", "r_exp", "comb_ready", "comb_tr", "combT_ready"))
        c_silu, comb_mm, moe_act = sem("c_silu"), sem("comb_mm"), sem("moe_act")
        tables_loaded, angle, table_abs, tables_ready = (sem(n) for n in (
            "tables_loaded", "angle", "table_abs", "tables_ready"))
        swapped, rotated, ret_sc, ret_scaled, ret_kv, ret_state, ret_out, ret_stored = (sem(n) for n in (
            "swapped", "rotated", "ret_sc", "ret_scaled", "ret_kv", "ret_state", "ret_out", "ret_stored"))
        ret_sq, ret_sum, ret_root = (sem(n) for n in ("ret_sq", "ret_sum", "ret_root"))
        sgu_loaded, vs_root, vs_norm, sgu_w, mixed, mixed_out = (sem(n) for n in (
            "sgu_loaded", "vs_root", "vs_norm", "sgu_w", "mixed", "mixed_out"))
        pooled, pool_act = sem("pooled"), sem("pool_act")
        lay_ready, branch_part = sem("lay_ready"), sem("branch_part")

        def lv_(i):
            return lay[:, i:i + 1]

        Y_MOE = KT
        Y_LAYERS, Y_PER_LAYER = Y_MOE + 2 * GROUPS * PER_GROUP, 5 * KT + 8 * FF_GROUPS
        Y_G, Y_U, Y_PIN, Y_POUT, Y_MG, Y_FF = (KT * n for n in range(6))
        VAL_LAYERS, VAL_PER_LAYER = 2 * GROUPS * PER_GROUP, 3 * KT + 8 * FF_GROUPS
        VAL_G, VAL_U, VAL_POUT, VAL_FF = (KT * n for n in range(4))

        def y_scalar(act, m, j, func, n, yb, vb):
            act.wait_ge(slab_done[j], m + 1)
            act.wait_ge(y_ready, yb + 2 * n - 2)
            tj = 2 * j
            for f in range(2):
                ins = act.activation(T[:, tj + f], pd[2 * j + f][:], func)
            ins.then_inc(slab_out[j], 1)
            for f in range(2):
                act.wait_ge(y_val, vb + 2 * n + f + 1)
                act.copy(y_hi[:, bass.ds(2 * n + f, 1)], T[:, tj + f:tj + f + 1]).then_inc(y_hi_ready, 1)

        def y_vector(dve, v, m, j, value, n, yb, vb, tj=None, wait=None):
            if wait is None:
                dve.wait_ge(slab_out[j], m + 1)
            else:
                dve.wait_ge(*wait)
            tj = 2 * j if tj is None else tj
            for f in range(2):
                value(T[:, tj + f:tj + f + 1], f).then_inc(y_val, 1)
            for f in range(2):
                dve.wait_ge(y_hi_ready, yb + 2 * n + f + 1)
                dve.tensor_tensor(y_lo[:, bass.ds(2 * n + f, 1)], T[:, tj + f:tj + f + 1],
                                  y_hi[:, bass.ds(2 * n + f, 1)].bitcast(F32), ALU.subtract).then_inc(y_ready, 1)
            dve.wait_ge(y_ready, yb + 2 * n + 2)

        def round_scalar(act, src, yb):
            for k in range(KT):
                act.copy(y_hi[:, k], src[:, k]).then_inc(y_hi_ready, 1)

        def round_vector(dve, src, yb):
            for k in range(KT):
                dve.wait_ge(y_hi_ready, yb + k + 1)
                dve.tensor_tensor(y_lo[:, k], src[:, k], y_hi[:, k].bitcast(F32), ALU.subtract).then_inc(y_ready, 1)
            dve.wait_ge(y_ready, yb + KT)

        def add_to_x(dve, v, m, j, tile, gate=None):
            dve.wait_ge(slab_done[j], m + 1)
            for f in range(2):
                to = xT[:, bass.ds(tile + 2 * j + f, 1)]
                bank = pd[2 * j + f][:].unsqueeze(1)
                if gate is None:
                    ins = dve.tensor_tensor(to, bank, to, ALU.add)
                else:
                    ins = dve.scalar_tensor_tensor(to, bank, lay[:, bass.ds(gate + tile + 2 * j + f, 1)], to,
                                                   ALU.mult, ALU.add)
            ins.then_inc(slab_out[j], 1)
            dve.wait_ge(slab_out[j], m + 1)

        rest = ExitStack()
        block = rest.enter_context(nc.Block())

        @block.sync
        def _(sp):
            sp.dma_start(v2[:], t["vec2"]).then_inc(stage2_loaded, 16)
            sp.dma_start(b_ada[:], t["b_ada"]).then_inc(stage2_loaded, 16)
            sp.dma_start(swap[:], t["swap"]).then_inc(stage2_loaded, 16)

            def load(m):
                for j in range(2):
                    sp.wait_ge(w_lo_ready[j], m)
                    sp.dma_start(raw[j][:], t["slabs"][bass.ds(2 * m + j, 1)]).then_inc(raw_loaded[j], 16)

            def load_ada(i):
                for j in range(2):
                    sp.dma_start(ada[:, j], t["ada"][bass.ds(2 * i + j, 1)]).then_inc(ada_loaded, 16)

            for m in range(IN1_PAIRS + 1, MOE_AT + 1):
                load(m)
            load_ada(0)
            with sp.Fori(1, GROUPS * GROUP_PAIRS) as i:
                load(MOE_AT + i)
                sp.wait_ge(ada_done, i)
                load_ada(i)
            with sp.Fori(LAYERS_AT, PAIRS) as m:
                load(m)
            sp.wait_ge(w_lo_ready[0], PAIRS)
            sp.dma_start(raw[0][:], t["slabs"][2 * PAIRS]).then_inc(raw_loaded[0], 16)

        @block.gpsimd
        def _(pool):
            remainder(pool, IN1_PAIRS, 1)
            with pool.Fori(IN1_PAIRS + 1, PAIRS) as m:
                for j in range(2):
                    remainder(pool, m, j)
            remainder(pool, PAIRS, 0)

        @block.tensor
        def _(pe):
            slabs_to_x(pe, IN1_PAIRS, y_hi, y_lo, (y_ready, 0), 1, MG)
            router_w = vec[:, V1["router_w"]].rearrange("p (k n) -> p k n", k=KT)
            slab_starts(pe, MOE_AT, 0)
            for k in range(KT):
                pe.wait_ge(norm_val, KT + k + 1)
                last = pe.matmul(px[1][0:20], router_w[:, k], MG[:, k], start=(k == 0), stop=(k == KT - 1))
                if k == KT - 1:
                    last.then_inc(logits, 1)
                pe.wait_ge(h_ready, KT + k + 1)
                slab_piece(pe, 0, k, h_hi, h_lo)
            pe.wait_ge(logits_out, 1)
            for b in range(TB):
                last = pe.transpose(px[1][:, b * 20:(b + 1) * 20], T[0:20, 2, b * P:(b + 1) * P], ident[0:20, 0:20])
            last.then_inc(logits_tr, 1)
            slab_rows(pe, MOE_AT, 1, h_hi, h_lo)
            pe.wait_ge(comb_ready, 1)
            for g in range(GROUPS):
                for b in range(TB):
                    last = pe.transpose(px[g][0:PER_GROUP, b * P:(b + 1) * P],
                                        rt[:, 256 + 16 * b + 4 * g:256 + 16 * b + 4 * g + 4], ident[:])
            last.then_inc(comb_tr, 1)

            def ada_products(m):
                pe.wait_ge(ada_part, KT * (m - MOE_AT) + KT)
                for j in range(2):
                    for f in range(2):
                        last = pe.matmul(px[2 + j][:, f:f + 1], ada[:, j, f * P:(f + 1) * P], ones[:, 0:1],
                                         start=True, stop=True)
                last.then_inc(ada_done, 1)

            pe.wait_ge(combT_ready, 4)
            def experts(g, first_group=False, last_group=False):
                for e in range(PER_GROUP):
                    m = MOE_AT + GROUP_PAIRS * g + e
                    ahead = first_group and e == 0
                    if not ahead:
                        slab_rows(pe, m, 0, h_hi, h_lo)
                    pe.matmul(px[e % 2][:], ident[0:PER_GROUP, e:e + 1].to_broadcast([PER_GROUP, P]),
                              combT[:, bass.ds(g, 1)], start=True, stop=True).then_inc(comb_mm, 1)
                    if not ahead:
                        slab_rows(pe, m, 1, h_hi, h_lo)
                    ada_products(m)
                at = MOE_AT + GROUP_PAIRS * g + PER_GROUP
                for n in range(4):
                    slab_rows(pe, at + n // 2, n % 2, y_hi, y_lo, (y_ready, Y_MOE + 8 * g) if n == 0 else None)
                    if n % 2:
                        ada_products(at + n // 2)

            experts(0, first_group=True)
            with pe.Fori(1, GROUPS - 1) as g:
                experts(g)
            experts(GROUPS - 1, last_group=True)
            norm_tail(pe, 2, O)

            with pe.Fori(0, LAYERS) as l:
                L = LAYERS_AT + LAYER_PAIRS * l
                yb = Y_LAYERS + Y_PER_LAYER * l

                def rows(at, hi, lo, ready=None):
                    for n in range(4):
                        slab_rows(pe, L + at + n // 2, n % 2, hi, lo, ready if n == 0 else None)

                def branch(at, y_at):
                    with inner(pe, 4) as i:
                        slab_rows(pe, L + at + i, 0, h_hi, h_lo)
                        pe.wait_ge(y_ready, yb + y_at + KT)
                        slab_rows(pe, L + at + i, 1, y_hi, y_lo)

                rows(L_Q, h_hi, h_lo, (h_ready, 8 * (2 * l + 2)))
                for n in range(4):
                    slab_tokens(pe, L + L_V + n // 2, n % 2, h_hi, h_lo)
                    for tile in range(4 * n, 4 * n + 4) if n < 2 else ():
                        if tile % 4 == 0:
                            pe.wait_ge(slab_out[0], L + n + 1)
                            pe.wait_ge(slab_out[1], L + n + 1)
                        if tile >= 4:
                            pe.wait_ge(rotated, 8 * l + tile - 3)
                        pe.matmul(px[tile % 4][:], swap[:], QK[:, tile], start=True, stop=True).then_inc(swapped, 1)
                pe.wait_ge(rotated, 8 * l + 8)

                def head_norm(h):
                    for et in range(2):
                        pe.wait_ge(ret_sq, 8 * l + 2 * h + et + 1)
                        last = pe.matmul(px[2][:], ones[:], T[:, et], start=(et == 0), stop=(et == 1))
                    last.then_inc(ret_sum, 1)

                for h in range(HEADS):
                    q, k = QK[:, h], QK[:, 4 + h]
                    if h:
                        pe.wait_ge(ret_stored, 8 * l + 2 * h)
                    for c in range(TB):
                        s = slice(c * P, (c + 1) * P)
                        pe.matmul(px[0][:, s], k[:, s], q[:, s], start=True, stop=True)
                        last = pe.transpose(px[1][:, s], k[:, s], ident[:])
                    last.then_inc(ret_sc, 1)
                    if h:
                        head_norm(h - 1)
                    slab_starts(pe, L + L_G + h // 2, h % 2)
                    for piece in range(6):
                        slab_piece(pe, h % 2, piece, h_hi, h_lo)
                    if h == 0:
                        for j in range(2):
                            pe.wait_ge(slab_out[j], L + 4)
                    else:
                        pe.wait_ge(ret_root, 4 * l + h)
                    pe.wait_ge(ret_scaled, 4 * l + h + 1)
                    for c in range(TB - 1):
                        last = pe.matmul(px[2 + c // 2][:, (c % 2) * 256:(c % 2) * 256 + 256],
                                         KD[:, c * P:(c + 1) * P], V_tok[:, c, h * 256:(h + 1) * 256],
                                         start=True, stop=True)
                    last.then_inc(ret_kv, 1)
                    for piece in range(6, KT):
                        slab_piece(pe, h % 2, piece, h_hi, h_lo)
                    pe.wait_ge(ret_state, 4 * l + h + 1)
                    for et in range(2):
                        for c in range(TB):
                            s, e0 = slice(c * P, (c + 1) * P), h * 256 + et * P
                            last = pe.matmul(px[et][:, s], V_tok[:, c, e0:e0 + P], SCT[:, s],
                                             start=True, stop=(c == 0))
                            if c:
                                state = ST[:, (c - 1) * 256 + et * P:(c - 1) * 256 + et * P + P] if c < 3 \
                                    else ST3[:, et * P:et * P + P]
                                last = pe.matmul(px[et][:, s], state, QD[:, s], start=False, stop=True)
                    last.then_inc(ret_out, 1)
                for n in range(4):
                    slab_tokens(pe, L + L_VS + n // 2, n % 2, h_hi, h_lo)
                    if n == 0:
                        head_norm(HEADS - 1)
                branch(L_BR0, Y_G)
                for n in range(4):
                    slab_rows(pe, L + L_U + n // 2, n % 2, h_hi, h_lo)

                def mix(k):
                    if k >= 4:
                        pe.wait_ge(mixed_out, 8 * l + k - 3)
                    for c in range(TB):
                        last = pe.matmul(px[k % 4][:, c * P:(c + 1) * P], V_tok[:, c, k * P:(k + 1) * P],
                                         w_sgu[:, (k // 2) * P:(k // 2 + 1) * P], start=True, stop=True)
                    last.then_inc(mixed, 1)

                pe.wait_ge(vs_norm, l + 1)
                pe.wait_ge(sgu_w, l + 1)
                for k in range(4):
                    mix(k)
                for n in range(4):
                    slab_rows(pe, L + L_P + n // 2, n % 2, h_hi, h_lo)
                    for k in range(4, KT) if n == 0 else ():
                        mix(k)
                branch(L_BR1, Y_U)
                for j in range(2):
                    m = L + L_POOL
                    slab_starts(pe, m, j)
                    for gi in range(2):
                        for et in range(2):
                            out = (pd if gi == 0 else px)[2 * j + et][:]
                            for kt in range(2):
                                cols = slice((2 * gi + kt) * SLAB_COLS + et * P,
                                             (2 * gi + kt) * SLAB_COLS + et * P + P)
                                k = 2 * (2 * j + gi) + kt
                                pe.wait_ge(y_ready, yb + Y_PIN + k + 1)
                                pe.matmul(out, w_hi[j][:, cols], y_hi[:, k], start=(kt == 0), stop=False)
                                pe.matmul(out, w_hi[j][:, cols], y_lo[:, k], start=False, stop=False)
                                last = pe.matmul(out, w_lo[j][:, cols], y_hi[:, k], start=False, stop=(kt == 1))
                    last.then_inc(slab_done[j], 1)
                branch(L_BR2, Y_POUT)
                slabs_to_x(pe, L + L_WOUT, h_hi, h_lo, (y_ready, yb + Y_MG), 3 + 2 * l, O)

                def up_down(q, last_group=False):
                    at = L + L_FF + 4 * q
                    for n in range(4):
                        slab_rows(pe, at + n // 2, n % 2, h_hi, h_lo, (h_ready, 8 * (2 * l + 3)) if n == 0 else None)
                    down_ready = (y_ready, yb + Y_FF + 8 * q)
                    if last_group:
                        slabs_to_x(pe, at + 2, y_hi, y_lo, down_ready, 4 + 2 * l, O)
                    else:
                        for n in range(4):
                            slab_rows(pe, at + 2 + n // 2, n % 2, y_hi, y_lo, down_ready if n == 0 else None)

                with inner(pe, FF_GROUPS - 1) as q:
                    up_down(q)
                up_down(FF_GROUPS - 1, True)

        @block.scalar
        def _(act):
            a = steps["scalar"].again(act)
            round_scalar(act, Y, 0)
            act.activation(c_act, vec[:, V1["c"]], ACT.Silu).then_inc(c_silu, 1)
            slabs_to_x_scalar(act, IN1_PAIRS, MG)
            norm_scalar(act, 1, MG, first=3)
            split_next(act, MOE_AT, 0)
            act.wait_ge(logits, 1)
            act.copy(T[0:20, 2], px[1][0:20]).then_inc(logits_out, 1)
            for n in range(2):
                act.wait_ge(r_exp_in, n + 1)
                s = slice(0, 16) if n == 0 else slice(16, 80)
                act.activation(rt[:, s], rt[:, s], ACT.Exp).then_inc(r_exp, 1)

            def expert_gate(m):
                act.wait_ge(slab_done[0], m + 1)
                act.activation(T[:, 0], pd[0][:], ACT.Silu)
                act.activation(T[:, 1], pd[1][:], ACT.Silu).then_inc(slab_out[0], 1)

            expert_gate(MOE_AT)
            split_next(act, MOE_AT, 1)
            act.wait_ge(comb_tr, 1)
            for g in range(GROUPS):
                act.copy(combT[:, g], px[g][0:PER_GROUP]).then_inc(combT_ready, 1)
            def experts(g, first_group=False, last_group=False):
                for e in range(PER_GROUP):
                    m = MOE_AT + GROUP_PAIRS * g + e
                    ahead = first_group and e == 0
                    if not ahead:
                        split_next(act, m, 0)
                        act.wait_ge(y_ready, Y_MOE + 8 * g + 2 * e)
                        expert_gate(m)
                    act.wait_ge(comb_mm, 4 * g + e + 1)
                    act.copy(T[:, 2], px[e % 2][:]).then_inc(moe_act, 1)
                    if not ahead:
                        split_next(act, m, 1)
                    for f in range(2):
                        act.wait_ge(y_val, 8 * g + 2 * e + f + 1)
                        act.copy(y_hi[:, 2 * e + f], T[:, f]).then_inc(y_hi_ready, 1)
                at = MOE_AT + GROUP_PAIRS * g + PER_GROUP
                if last_group:
                    slabs_to_x_scalar(act, at, O)
                else:
                    for n in range(4):
                        split_next(act, at + n // 2, n % 2)

            experts(0, first_group=True)
            with act.Fori(1, GROUPS - 1) as g:
                experts(g)
            experts(GROUPS - 1, last_group=True)
            with a.loop(LAYERS, TB) as l:
                L = LAYERS_AT + LAYER_PAIRS * l
                yb = Y_LAYERS + Y_PER_LAYER * l
                vb = VAL_LAYERS + VAL_PER_LAYER * l
                act.wait_ge(lay_ready, l + 1)
                act.dma_start(pos.bitcast(I32), t["positions"].partition_broadcast(P)).then_inc(tables_loaded, 16)
                act.dma_start(MG[:, 2:4], t["decays"]).then_inc(tables_loaded, 16)
                norm_scalar(act, 2 + 2 * l, O, lambda k: lv_(MOD + k), first=3)
                split_next(act, L + L_Q, 0)
                act.wait_ge(angle, l + 1)
                act.activation(turns, ang, ACT.Abs).then_inc(table_abs, 1)
                act.activation(sin, ang, ACT.Sin, scale=1.0)
                act.wait_ge(table_abs, l + 1)
                act.activation(cos, turns, ACT.Sin, bias=0.5 * float(np.pi), scale=-1.0).then_inc(tables_ready, 1)

                def plain(m, j, k, func=ACT.Copy, scale=1.0, split_yet=True):
                    if split_yet:
                        split_next(act, m, j)
                    act.wait_ge(slab_done[j], m + 1)
                    for f in range(2):
                        ins = act.activation(QK[:, k + f], pd[2 * j + f][:], func, scale=scale)
                    ins.then_inc(slab_out[j], 1)

                def by_tokens(at, func, behind_first=None):
                    for n in range(4):
                        m, j = L + at + n // 2, n % 2
                        if n != 1 or behind_first is None:
                            split_next(act, m, j)
                        act.wait_ge(slab_done[j], m + 1)
                        for half in range(2):
                            ins = act.activation(
                                V_tok[:, 2 * half:2 * half + 2, n * SLAB_COLS:(n + 1) * SLAB_COLS],
                                pd[2 * j + half][:].rearrange("p (a b) -> p a b", a=2), func)
                        ins.then_inc(slab_out[j], 1)
                        if n == 0 and behind_first is not None:
                            split_next(act, m, 1)
                            behind_first()

                def round_value(k, yo, vo):
                    act.wait_ge(y_val, vb + vo + k + 1)
                    act.copy(y_hi[:, k], O[:, k]).then_inc(y_hi_ready, 1)

                def branch_gate(m):
                    split_next(act, m, 0)
                    act.wait_ge(slab_done[0], m + 1)
                    act.wait_ge(slab_out[1], m)
                    act.activation(T[:, 0], pd[0][:], ACT.Sigmoid)
                    act.activation(T[:, 1], pd[1][:], ACT.Sigmoid).then_inc(slab_out[0], 1)
                    split_next(act, m, 1)

                def branch(at):
                    with inner(act, 4) as i:
                        branch_gate(L + at + i)

                for n in range(4):
                    plain(L + n // 2, n % 2, 2 * n, scale=1.0 if n < 2 else RET_SCALE, split_yet=n > 0)
                by_tokens(L_V, ACT.Copy)

                def head_norm(h):
                    act.wait_ge(ret_sum, 4 * l + h + 1)
                    act.activation(T[:, 2], px[2][:], ACT.Sqrt, bias=EPS, scale=1.0 / 256).then_inc(ret_root, 1)
                    for et in range(2):
                        round_value(2 * h + et, Y_G, VAL_G)

                for h in range(HEADS):
                    m, j = L + L_G + h // 2, h % 2
                    split_next(act, m, j)
                    if h:
                        head_norm(h - 1)
                    act.wait_ge(slab_done[j], m + 1)
                    act.wait_ge(ret_scaled, 4 * l + h + 1)
                    for f in range(2):
                        ins = act.activation(QK[:, 4 * f + h], pd[2 * j + f][:], ACT.Silu)
                    ins.then_inc(slab_out[j], 1)
                    act.wait_ge(ret_out, 4 * l + h + 1)
                    for et in range(2):
                        act.copy(O[:, 2 * h + et], px[et][:]).then_inc(ret_stored, 1)
                    for et in range(2):
                        act.wait_ge(ret_stored, 8 * l + 2 * h + et + 1)
                        act.activation(T[:, et], O[:, 2 * h + et], ACT.Square).then_inc(ret_sq, 1)
                by_tokens(L_VS, ACT.Gelu_apprx_tanh, lambda: head_norm(HEADS - 1))
                for dst, name in ((w_sgu, "w_sgu"), (b_sgu, "b_sgu")):
                    act.dma_start(dst, t[name][bass.ds(l, 1)] if name == "w_sgu" else
                                  t[name][bass.ds(l, 1)].partition_broadcast(P)).then_inc(sgu_loaded, 16)
                act.dma_start(tri, t["tri"]).then_inc(sgu_loaded, 16)
                branch_gate(L + L_BR0)
                for j in range(2):
                    act.wait_ge(slab_out[j], L + L_VS + 2)
                act.wait_ge(y_ready, yb + Y_G + KT)
                for b in range(TB):
                    ins = act.activation(O[:, 2 * (b % 2):2 * (b % 2) + 2], V_tok[:, b].rearrange(
                        "p (a n) -> p a n", a=2), ACT.Square, accum_out=small2[:, 12 + b:13 + b])
                    a(ins)
                act.activation(small2[:, 16:20], small2[:, 12:16], ACT.Sqrt, bias=EPS,
                               scale=1.0 / D).then_inc(vs_root, 1)
                with inner(act, 3) as i:
                    branch_gate(L + L_BR0 + 1 + i)
                for n in range(4):
                    m, j = L + L_U + n // 2, n % 2
                    split_next(act, m, j)
                    act.wait_ge(slab_done[j], m + 1)
                    for f in range(2):
                        ins = act.activation(O[:, 2 * n + f], pd[2 * j + f][:], ACT.Gelu_apprx_tanh)
                    ins.then_inc(slab_out[j], 1)
                for n in range(4):
                    if n == 2:
                        act.wait_ge(mixed_out, 8 * l + 8)
                    plain(L + L_P + n // 2, n % 2, 2 * n)
                    for k in range(4 * n, 4 * n + 4) if n < 2 else ():
                        round_value(k, Y_U, VAL_U)
                branch(L_BR1)
                act.wait_ge(slab_out[1], L + L_BR1 + 4)
                act.wait_ge(pooled, l + 1)
                round_scalar(act, O, yb + Y_PIN)
                for j in range(2):
                    if j == 0:
                        split_next(act, L + L_POOL, 0)
                    act.wait_ge(slab_done[j], L + L_POOL + 1)
                    if j:
                        act.wait_ge(y_ready, yb + Y_POUT + 4)
                    for gi in range(2):
                        for et in range(2):
                            ins = act.copy(T[:, 2 * gi + et], (pd if gi == 0 else px)[2 * j + et][:])
                        ins.then_inc(slab_out[j] if gi == 0 else pool_act, 1)
                    if j == 0:
                        split_next(act, L + L_POOL, 1)
                    for n in range(4):
                        act.wait_ge(y_val, vb + VAL_POUT + 4 * j + n + 1)
                        act.copy(y_hi[:, 4 * j + n], T[:, n]).then_inc(y_hi_ready, 1)
                act.wait_ge(y_ready, yb + Y_POUT + KT)
                branch(L_BR2)
                act.wait_ge(slab_out[1], L + L_BR2 + 3)
                for k in range(KT):
                    if k == 6:
                        act.wait_ge(slab_out[1], L + L_BR2 + 4)
                    act.copy(h_hi[:, k], MG[:, k]).then_inc(y_hi_ready, 1)
                slabs_to_x_scalar(act, L + L_WOUT, O)
                norm_scalar(act, 3 + 2 * l, O, lambda k: lv_(MOD + 24 + k), first=3)

                def up_down(q, last_group=False):
                    at = L + L_FF + 4 * q
                    with inner(act, 2) as i:
                        for j in range(2):
                            split_next(act, at + i, j)
                            y_scalar(act, at + i, j, ACT.Relu, 2 * i + j, yb + Y_FF + 8 * q, vb + VAL_FF + 8 * q)
                    if last_group:
                        slabs_to_x_scalar(act, at + 2, O)
                    else:
                        for n in range(4):
                            split_next(act, at + 2 + n // 2, n % 2)

                with inner(act, FF_GROUPS - 1) as q:
                    up_down(q)
                up_down(FF_GROUPS - 1, True)
            u = 2 + 2 * LAYERS
            norm_squares(act, O, [3])
            act.wait_ge(norm_sum, u + 1)
            act.activation(T[:, 0], px[0][:], ACT.Sqrt, bias=EPS, scale=1.0 / D).then_inc(norm_root, 1)
            for i in range(2):
                act.wait_ge(norm_val, 8 * u + 4 * i + 4)
                act.dma_start(t["out"][:, 4 * i:4 * i + 4], O[:, 4 * i:4 * i + 4]).then_inc(out_stored, 16)
            act.wait_ge(out_stored, 32)

        @block.vector
        def _(dve):
            v = steps["vector"].again(dve)
            round_vector(dve, Y, 0)
            for m in range(IN1_PAIRS, MOE_AT):
                for j in range(2):
                    add_to_x(dve, v, m, j, 4 * (m - IN1_PAIRS))
                    if m == MOE_AT - 1 and j == 0:
                        norm_add(dve, 1, MG)
            norm_vector(dve, v, 1, MG, lambda k: v1("norm2", k))

            GL = rt[:, 0:16].rearrange("p (b g) -> p b g", b=TB)
            EL = rt[:, 16:80].rearrange("p (n e) -> p n e", e=4)
            lg = px[1][:, 0:80].rearrange("p (b n) -> p b n", b=TB)
            rb = vec[:, V1["router_b"]]
            dve.wait_ge(logits_tr, 1)
            dve.tensor_tensor(GL, lg[:, :, 0:4], rb[:, 0:4].unsqueeze(1).to_broadcast([P, TB, 4]), ALU.add)
            v(dve.tensor_tensor(rt[:, 16:80].rearrange("p (b n) -> p b n", b=TB), lg[:, :, 4:20],
                                rb[:, 4:20].unsqueeze(1).to_broadcast([P, TB, 16]), ALU.add))

            def ranked(VL, n, first, exp_no):
                mx, rk, cmp = rt[:, first:first + n], rt[:, first + 16:first + 16 + 4 * n], rt[:, 400:400 + 3 * n]
                rk = rk.rearrange("p (n e) -> p n e", e=4)
                v(dve.tensor_reduce(mx, VL, AX.X, ALU.max))
                v(dve.tensor_tensor(VL, VL, mx.unsqueeze(2).to_broadcast([P, n, 4]), ALU.subtract), r_exp_in, exp_no)
                dve.wait_ge(r_exp, exp_no)
                v(dve.memset(rk, 0.0))
                for d in range(1, 4):
                    w = 4 - d
                    cm = cmp[:, 0:n * w].rearrange("p (n e) -> p n e", e=w)
                    v(dve.tensor_tensor(cm, VL[:, :, d:4], VL[:, :, 0:w], ALU.is_gt))
                    v(dve.tensor_tensor(rk[:, :, 0:w], rk[:, :, 0:w], cm, ALU.add))
                    v(dve.tensor_scalar(cm, cm, -1.0, 1.0, ALU.mult, ALU.add))
                    v(dve.tensor_tensor(rk[:, :, d:4], rk[:, :, d:4], cm, ALU.add))
                return mx, rk

            mx, rk = ranked(GL, TB, 80, 1)
            v(dve.tensor_reduce(mx, GL, AX.X, ALU.add))
            v(dve.reciprocal(mx, mx))
            v(dve.tensor_scalar(rk, rk, 0.5, None, ALU.is_lt))
            v(dve.tensor_tensor(GL, rk, mx.unsqueeze(2).to_broadcast([P, TB, 4]), ALU.mult))
            mx, rk = ranked(EL, 4 * TB, 120, 2)
            v(dve.tensor_scalar(rk, rk, 1.5, None, ALU.is_lt))
            v(dve.tensor_tensor(EL, EL, rk, ALU.mult))
            v(dve.tensor_reduce(mx, EL, AX.X, ALU.add))
            v(dve.reciprocal(mx, mx))
            v(dve.tensor_tensor(mx, mx, rt[:, 0:16], ALU.mult))
            v(dve.tensor_tensor(rt[:, 256:320].rearrange("p (n e) -> p n e", e=4), EL,
                                mx.unsqueeze(2).to_broadcast([P, 4 * TB, 4]), ALU.mult), comb_ready, 1)
            dve.wait_ge(stage2_loaded, 48)

            def ada_sum(m):
                i = m - MOE_AT
                dve.wait_ge(ada_loaded, 32 * i + 32)
                acc = ada[:, :, 0:SLAB_COLS]
                for k in range(KT):
                    rows, c = ada[:, :, k * SLAB_COLS:(k + 1) * SLAB_COLS], c_act[:, k:k + 1]
                    if k == 0:
                        ins = dve.tensor_scalar(acc, rows, c, None, ALU.mult)
                    else:
                        ins = dve.scalar_tensor_tensor(acc, rows, c, acc, ALU.mult, ALU.add)
                    ins.then_inc(ada_part, 1)
                    dve.wait_ge(ada_part, KT * i + k + 1)

            def mod_store(m):
                dve.wait_ge(ada_done, m - MOE_AT + 1)
                for j in range(2):
                    at = 4 * (m - MOE_AT) + 2 * j
                    ins = dve.tensor_tensor(mod[:, bass.ds(at, 2)], px[2 + j][:, 0:2], b_ada[:, bass.ds(at, 2)],
                                            ALU.add)
                return ins

            dve.wait_ge(c_silu, 1)
            def experts(g, last_group=False):
                for e in range(PER_GROUP):
                    m = MOE_AT + GROUP_PAIRS * g + e
                    ada_sum(m)
                    dve.wait_ge(moe_act, 4 * g + e + 1)
                    for f in range(2):
                        last = dve.tensor_tensor(T[:, f], T[:, f], T[:, 2], ALU.mult)
                    v(last)
                    dve.wait_ge(slab_done[1], m + 1)
                    for f in range(2):
                        dve.tensor_tensor(T[:, f], T[:, f], pd[2 + f][:], ALU.mult).then_inc(y_val, 1)
                    mod_store(m).then_inc(slab_out[1], 1)
                    for f in range(2):
                        dve.wait_ge(y_hi_ready, Y_MOE + 8 * g + 2 * e + f + 1)
                        dve.tensor_tensor(y_lo[:, 2 * e + f], T[:, f], y_hi[:, 2 * e + f].bitcast(F32),
                                          ALU.subtract).then_inc(y_ready, 1)
                    dve.wait_ge(y_ready, Y_MOE + 8 * g + 2 * e + 2)

                def down(d):
                    m = MOE_AT + GROUP_PAIRS * g + PER_GROUP + d
                    ada_sum(m)
                    add_to_x(dve, v, m, 0, 4 * d)
                    if last_group and d == 1:
                        norm_add(dve, 2, O)
                    dve.wait_ge(slab_done[1], m + 1)
                    for f in range(2):
                        to = xT[:, bass.ds(4 * d + 2 + f, 1)]
                        dve.tensor_tensor(to, pd[2 + f][:].unsqueeze(1), to, ALU.add)
                    mod_store(m).then_inc(slab_out[1], 1)
                    dve.wait_ge(slab_out[1], m + 1)

                if last_group:
                    down(0)
                    down(1)
                else:
                    with inner(dve, 2) as d:
                        down(d)

            with v.loop(GROUPS - 1, PER_GROUP) as g:
                experts(g)
            experts(GROUPS - 1, last_group=True)
            sgn = v1("sign")
            with v.loop(LAYERS, LAYER_VECTOR_STEPS) as l:
                L = LAYERS_AT + LAYER_PAIRS * l
                yb = Y_LAYERS + Y_PER_LAYER * l
                vb = VAL_LAYERS + VAL_PER_LAYER * l
                dve.tensor_copy(lay[:, 0:V2_COLS], v2[:, bass.ds(l, 1)])
                v(dve.tensor_copy(lay[:, MOD:MOD + ADA_COLS], mod[:, bass.ds(ADA_COLS * l, ADA_COLS)]))
                for n in range(2):
                    ins = dve.scalar_tensor_tensor(lay[:, GAIN + 8 * n:GAIN + 8 * n + 8],
                                                   lay[:, MOD + 24 * n + 8:MOD + 24 * n + 16], 1.0,
                                                   lay[:, 8 * n:8 * n + 8], ALU.add, ALU.mult)
                v(ins, lay_ready, l + 1)
                norm_vector(dve, v, 2 + 2 * l, O, lambda k: lv_(GAIN + k), lambda k: lv_(MOD + k))
                dve.wait_ge(tables_loaded, 32 * l + 32)
                v(dve.tensor_scalar(ang, pos.bitcast(I32), v1("inv_freq"), None, ALU.mult))
                v(dve.tensor_scalar(turns, ang, 1.0 / TWO_PI, ROUND, ALU.mult, ALU.add))
                v(dve.tensor_scalar(turns, turns, ROUND, None, ALU.subtract))
                for part in TURN_PARTS:
                    v(dve.scalar_tensor_tensor(ang, turns, -part, ang, ALU.mult, ALU.add))
                v(dve.tensor_scalar(ang, ang, PI_BELOW, -PI_BELOW, ALU.min, ALU.max), angle, l + 1)
                dve.wait_ge(tables_ready, l + 1)
                v(dve.tensor_scalar(sin, sin, sgn, None, ALU.mult))
                for n in range(8):
                    dve.wait_ge(swapped, 8 * l + n + 1)
                    dve.tensor_tensor(T[:, n % 2], px[n % 4][:], sin, ALU.mult)
                    v(dve.tensor_tensor(QK[:, n], QK[:, n], cos, ALU.mult))
                    v(dve.tensor_tensor(QK[:, n], QK[:, n], T[:, n % 2], ALU.add), rotated, 8 * l + n + 1)

                def head_norm(h):
                    dve.wait_ge(ret_root, 4 * l + h + 1)
                    v(dve.reciprocal(T[:, 2], T[:, 2]))
                    for et in range(2):
                        last = dve.tensor_tensor(O[:, 2 * h + et], O[:, 2 * h + et], T[:, 2], ALU.mult)
                    v(last)
                    dve.wait_ge(slab_out[h % 2], L + L_G + h // 2 + 1)
                    for f in range(2):
                        dve.tensor_tensor(O[:, 2 * h + f], O[:, 2 * h + f], QK[:, 4 * f + h],
                                          ALU.mult).then_inc(y_val, 1)
                    remainders(range(2 * h, 2 * h + 2), yb + Y_G)

                def remainders(tiles, y_at, lo=y_lo, hi=y_hi, src=O):
                    for k in tiles:
                        dve.wait_ge(y_hi_ready, y_at + k + 1)
                        dve.tensor_tensor(lo[:, k], src[:, k], hi[:, k].bitcast(F32),
                                          ALU.subtract).then_inc(y_ready, 1)
                    dve.wait_ge(y_ready, y_at + k + 1)

                by_chunk = lambda ap: ap.rearrange("p (c n) -> p c n", c=TB)
                for h in range(HEADS):
                    dec = lambda ap: ap[:, h * P:(h + 1) * P].unsqueeze(1).to_broadcast([P, TB, P])
                    if h:
                        dve.wait_ge(ret_out, 4 * l + h)
                    dve.tensor_tensor(by_chunk(QD), by_chunk(QK[:, h]), dec(decq), ALU.mult)
                    dve.wait_ge(ret_sc, 4 * l + h + 1)
                    dve.tensor_scalar(KD, px[1][:], v1("decay_k", h), None, ALU.mult)
                    v(dve.tensor_tensor(by_chunk(SCT), by_chunk(px[0][:]), dec(decT), ALU.mult),
                      ret_scaled, 4 * l + h + 1)
                    if h:
                        head_norm(h - 1)
                    dve.wait_ge(ret_kv, 4 * l + h + 1)
                    dc = DECAY_CHUNK[h]
                    v(dve.tensor_copy(ST[:, 0:256], px[2][:, 0:256]))
                    v(dve.scalar_tensor_tensor(ST[:, 256:512], ST[:, 0:256], dc, px[2][:, 256:512], ALU.mult, ALU.add))
                    v(dve.scalar_tensor_tensor(ST3[:, 0:256], ST[:, 256:512], dc, px[3][:, 0:256], ALU.mult, ALU.add),
                      ret_state, 4 * l + h + 1)
                head_norm(HEADS - 1)

                def branch_product(at, i, part=None):
                    m = L + at + i
                    dve.wait_ge(slab_out[0], m + 1)
                    dve.wait_ge(slab_done[1], m + 1)
                    for f in range(2):
                        to = MG[:, bass.ds(2 * i + f, 1)]
                        dst = to if part is None else T[:, 2 + f:3 + f]
                        ins = dve.tensor_tensor(dst, T[:, f:f + 1], pd[2 + f][:].unsqueeze(1), ALU.mult)
                    if part is not None:
                        ins.then_inc(branch_part, 1)
                        dve.wait_ge(branch_part, 8 * l + part + 1)
                        for f in range(2):
                            to = MG[:, bass.ds(2 * i + f, 1)]
                            ins = dve.tensor_tensor(to, to, T[:, 2 + f:3 + f], ALU.add)
                    ins.then_inc(slab_out[1], 1)
                    dve.wait_ge(slab_out[1], m + 1)

                branch_product(L_BR0, 0)
                dve.wait_ge(sgu_loaded, 48 * l + 48)
                v(dve.tensor_tensor(by_chunk(w_sgu), by_chunk(w_sgu), tri.unsqueeze(1).to_broadcast([P, TB, P]),
                                    ALU.mult), sgu_w, l + 1)
                dve.wait_ge(vs_root, l + 1)
                v(dve.reciprocal(small2[:, 20:24], small2[:, 16:20]))
                for b in range(TB):
                    last = dve.tensor_scalar(V_tok[:, b], V_tok[:, b], small2[:, 20 + b:21 + b], None, ALU.mult)
                v(last, vs_norm, l + 1)
                with inner(dve, 3) as i:
                    branch_product(L_BR0, 1 + i)
                for k in range(KT):
                    if k % 2 == 0:
                        dve.wait_ge(slab_out[(k // 2) % 2], L + L_U + k // 4 + 1)
                    dve.wait_ge(mixed, 8 * l + k + 1)
                    bias = b_sgu[:, (k // 2) * P:(k // 2 + 1) * P].unsqueeze(1).to_broadcast([P, TB, P])
                    v(dve.scalar_tensor_tensor(by_chunk(T[:, 2 + k % 2]), by_chunk(px[k % 4][:]), lv_(16 + k), bias,
                                               ALU.mult, ALU.add), mixed_out, 8 * l + k + 1)
                    dve.tensor_tensor(O[:, k], O[:, k], T[:, 2 + k % 2], ALU.mult).then_inc(y_val, 1)
                    if k % 4 == 3:
                        remainders(range(k - 3, k + 1), yb + Y_U)
                for j in range(2):
                    dve.wait_ge(slab_out[j], L + L_P + 2)
                for g, w in enumerate(WIN):
                    p = QK[:, 2 * g:2 * g + 2]
                    cur, d, n = p, 1, 0
                    while d < w:
                        nxt = V[:, 4 * (g % 2) + 2 * (n % 2):4 * (g % 2) + 2 * (n % 2) + 2]
                        dve.tensor_tensor(nxt[:, :, d:TOK], cur[:, :, d:TOK], cur[:, :, 0:TOK - d], ALU.add)
                        v(dve.tensor_copy(nxt[:, :, 0:d], cur[:, :, 0:d]))
                        cur, d, n = nxt, 2 * d, n + 1
                    count = vec[:, V1["inv_count"]][:, 16 * g:16 * g + 16].unsqueeze(1).to_broadcast([P, 2, 16])
                    dve.scalar_tensor_tensor(O[:, 2 * g:2 * g + 2, 16:TOK], cur[:, :, 16:TOK], 1.0 / w,
                                             p[:, :, 16:TOK], ALU.mult, ALU.subtract)
                    head = small2[:, 32:64].rearrange("p (a n) -> p a n", a=2)
                    v(dve.tensor_tensor(head, cur[:, :, 0:16], count, ALU.mult))
                    ins = dve.tensor_tensor(O[:, 2 * g:2 * g + 2, 0:16], head, p[:, :, 0:16], ALU.subtract)
                    if g < 3:
                        v(ins)
                    else:
                        v(ins, pooled, l + 1)
                    branch_product(L_BR1, g, g)
                round_vector(dve, O, yb + Y_PIN)
                for j in range(2):
                    for gi in range(2):
                        def scaled_value(tile, f):
                            k = 4 * j + 2 * gi + f
                            return dve.tensor_scalar(tile, tile, lv_(24 + k), lv_(32 + k), ALU.add, ALU.mult)
                        y_vector(dve, v, L + L_POOL, j, scaled_value, 2 * j + gi, yb + Y_POUT, vb + VAL_POUT,
                                 tj=2 * gi, wait=(slab_out[j], L + L_POOL + 1) if gi == 0 else (pool_act, 2 * l + j + 1))
                for i in range(4):
                    if i == 3:
                        remainders(range(6), yb + Y_MG, h_lo, h_hi, MG)
                    branch_product(L_BR2, i, 4 + i)
                remainders(range(6, KT), yb + Y_MG, h_lo, h_hi, MG)
                for n in range(4):
                    add_to_x(dve, v, L + L_WOUT + n // 2, n % 2, 4 * (n // 2), MOD + 16)
                    if n == 2:
                        norm_add(dve, 3 + 2 * l, O)
                norm_vector(dve, v, 3 + 2 * l, O, lambda k: lv_(GAIN + 8 + k), lambda k: lv_(MOD + 24 + k))

                def up_down(q, last_group=False):
                    with inner(dve, 2) as i:
                        for j in range(2):
                            y_vector(dve, v, L + L_FF + 4 * q + i, j,
                                     lambda tile, f: dve.tensor_tensor(tile, tile, tile, ALU.mult),
                                     2 * i + j, yb + Y_FF + 8 * q, vb + VAL_FF + 8 * q)
                    for n in range(4):
                        add_to_x(dve, v, L + L_FF + 4 * q + 2 + n // 2, n % 2, 4 * (n // 2), MOD + 40)
                        if last_group and n == 2:
                            norm_add(dve, 4 + 2 * l, O)

                with inner(dve, FF_GROUPS - 1) as q:
                    up_down(q)
                up_down(FF_GROUPS - 1, last_group=True)
            u = 2 + 2 * LAYERS
            dve.wait_ge(norm_root, u + 1)
            v(dve.reciprocal(T[:, 1], T[:, 0]))
            for k in range(KT):
                dve.scalar_tensor_tensor(O[:, k], xT[:, k], v1("final", k), T[:, 1], ALU.mult,
                                         ALU.mult).then_inc(norm_val, 1)

        rest.close()


def feature_tiles(a):
    return np.ascontiguousarray(np.asarray(a).reshape(-1, P).T)


def slabs_of(w):
    n = w.shape[1] // SLAB_COLS
    return w.reshape(KT, P, n, SLAB_COLS).transpose(2, 1, 0, 3).reshape(n, P, SLAB)


def constants():
    s, q = np.arange(P)[:, None], np.arange(P)[None, :]
    same = s // CH == q // CH
    before, upto = (same & (s < q)).astype(np.float32), (same & (s <= q)).astype(np.float32)
    level = []
    for n in range(INVERSE_LEVELS + 1):
        m = 1 << n
        level.append(((q // (2 * m) == s // (2 * m)) & (q // m % 2 == 1) & (s // m % 2 == 0)).astype(np.float32))
    c1 = {
        "gram": np.concatenate([before, -upto, before, upto], 1), "x0": -level[0].T, "x0t": -level[0],
        "levels": np.concatenate(level[1:], 1), "causal": np.where(q <= s, 0.0, -1e30).astype(np.float32),
        "halves": (np.arange(32)[None, :] == 16 + s // CH).astype(np.float32)}
    f = np.float32
    log_gamma = np.log1p(-np.power(f(2.0), f(-5.0) - np.arange(HEADS, dtype=f)).astype(f)).astype(f)
    pos = np.arange(P, dtype=f)
    rel = pos[None, :] - pos[:, None]
    dec = [np.where(rel >= 0, np.exp(log_gamma[h] * np.maximum(rel, 0)), 0).astype(f) for h in range(HEADS)]
    dec_q = [np.broadcast_to(np.exp(log_gamma[h] * (pos + 1)).astype(f), (P, P)) for h in range(HEADS)]
    dec_k = np.exp(log_gamma[None, :] * (P - 1 - pos[:, None])).astype(f)
    half = P // 2
    inv_freq = np.power(f(10000.0), -np.arange(half, dtype=f) / f(half)).astype(f)
    inv_count = np.concatenate([1.0 / np.minimum(np.arange(1, 17), w) for w in WIN]).astype(f)
    return {
        "c1": c1, "decays": np.stack([np.concatenate(dec, 1), np.concatenate(dec_q, 1)], 1), "decay_k": dec_k,
        "decay_chunk": [float(np.exp(log_gamma[h] * f(P))) for h in range(HEADS)],
        "inv_freq": np.concatenate([inv_freq, inv_freq])[:, None], "sign": np.repeat([[-1.0], [1.0]], half, 0).astype(f),
        "inv_count": np.broadcast_to(inv_count, (P, 64)), "tri": (s <= q).astype(f),
        "swap": (q == (s + half) % P).astype(f), "ident": np.eye(P, dtype=f), "ones": np.ones((P, P), f),
        "blk": same.astype(f)}


ROUND = 12582912.0
TURN_PARTS = (6.28125, 0.0019350051879882812, float(2 * np.pi - 6.28125 - 0.0019350051879882812))
PI_BELOW = 3.1415925
DECAY_CHUNK = constants()["decay_chunk"]
LAYER_VECTOR_STEPS = 52


def lay_out(inputs):
    a = {n: np.asarray(x) for n, x in inputs.items()}
    k = constants()
    f = np.float32
    w_in = a["w_in"][0]
    lru, q_at, f_at, p_at = 512, 512, 2048, 2056
    misc = np.zeros((D, SLAB_COLS), f)
    misc[:, 0:P] = w_in[:, p_at + 768:p_at + 896]
    misc[:, P:P + 8] = w_in[:, f_at:p_at]
    parts = [w_in[:, p_at:p_at + 768], misc, w_in[:, 0:lru], w_in[:, q_at:f_at], a["w_out"][0]]
    slabs = [slabs_of(p) for p in parts]
    for g in range(GROUPS):
        for e in range(g * PER_GROUP, (g + 1) * PER_GROUP):
            slabs += [slabs_of(a["exp_w_gate"][0, e]), slabs_of(a["exp_w_up"][0, e])]
        slabs.append(slabs_of(a["exp_w_down"][0, g * PER_GROUP:(g + 1) * PER_GROUP].reshape(D, D)))
    for l in range(LAYERS):
        w = a["w_in_2"][l]
        cols = {n: slabs_of(w[:, s:e]) for n, s, e in (
            ("q", 0, 512), ("k", 512, 1024), ("v", 1024, 2048), ("g", 2048, 3072), ("u", 3072, 4096),
            ("vs", 4096, 5120), ("p", 5120, 6144))}
        gate = [slabs_of(w[:, 6144 + D * n:6144 + D * (n + 1)]) for n in range(3)]
        br = [slabs_of(a["w_branch_2"][l, n]) for n in range(3)]
        both = [np.stack([gate[n], br[n]], 1).reshape(8, P, SLAB) for n in range(3)]
        pool = np.zeros((2, P, SLAB), f)
        wp = a["w_pool_2"][l].reshape(2, 2, 2, P, SLAB_COLS)
        pool[:, :, 0:SLAB // 2] = wp.transpose(0, 3, 1, 2, 4).reshape(2, P, SLAB // 2)
        slabs += [cols["q"], cols["k"], cols["v"], cols["g"], cols["vs"], both[0], cols["u"], cols["p"],
                  both[1], pool, both[2], slabs_of(a["w_out_2"][l])]
        for n in range(FF_GROUPS):
            slabs += [slabs_of(a["w_ff1_2"][l][:, n * D:(n + 1) * D]), slabs_of(a["w_ff2_2"][l][n * D:(n + 1) * D])]
    slabs.append(np.zeros((1, P, SLAB), f))
    slabs = np.concatenate(slabs)
    assert slabs.shape[0] == 2 * PAIRS + 1, slabs.shape

    vec1 = np.zeros((P, V1_COLS), f)

    def put(name, x):
        vec1[:, V1[name]] = x

    for name, src in (("norm1", "norm1_g"), ("conv_w", "conv_w"), ("conv_b", "conv_b"), ("lru_ba", "lru_ba"),
                      ("lru_bx", "lru_bx"), ("lru_lambda", "lru_lambda"), ("lru_norm", "lru_norm_g"),
                      ("fox_norm", "fox_norm_g"), ("mu", "rwkv_mu"), ("w0", "rwkv_w0"), ("a0", "rwkv_a0"),
                      ("kk", "rwkv_kk"), ("ka", "rwkv_ka"), ("rk", "rwkv_rk"), ("ln_g", "rwkv_ln_g"),
                      ("ln_b", "rwkv_ln_b"), ("norm2", "norm2_g"), ("c", "c_2"), ("final", "final_norm_2")):
        put(name, feature_tiles(a[src]))
    vec1[0:8, V1["fox_fb"]] = a["fox_fb"].reshape(8, 1)
    put("fox_qn", np.concatenate([a["fox_qnorm_g"][0]] * 2)[:, None])
    put("fox_kn", np.concatenate([a["fox_knorm_g"][0]] * 2)[:, None])
    put("router_b", np.broadcast_to(np.concatenate([a["router_gb"][0], a["router_eb"][0]]), (P, 20)))
    rw = np.concatenate([a["router_gw"][0], a["router_ew"][0]], 1)
    put("router_w", rw.reshape(KT, P, 20).transpose(1, 0, 2).reshape(P, 160))
    for name in ("decay_k", "inv_freq", "sign", "inv_count"):
        put(name, k[name])

    c1 = np.zeros((P, C1_COLS), f)
    for name, x in k["c1"].items():
        c1[:, C1[name]] = x
    c1[:, C1["lora"]] = np.concatenate([a["rwkv_w2"][0], a["rwkv_a2"][0], a["rwkv_g2"][0]], 0)
    for name in ("lru_wa", "lru_wx"):
        for h in range(HEADS):
            u, j = h % 2, h // 2
            at = C1[name].start + j * P + 64 * u
            c1[64 * u:64 * u + 64, at:at + 64] = a[name][0, h]

    vec2 = np.zeros((P, LAYERS, V2_COLS), f)
    for l in range(LAYERS):
        for name, src in (("norm1", "norm1_2"), ("norm2", "norm2_2"), ("vnorm", "vnorm_gmlp_2"),
                          ("b_pool", "b_pool_2"), ("pool_scale", "pool_scale_2")):
            vec2[:, l, V2[name]] = feature_tiles(a[src][l])
    return {
        "x": np.ascontiguousarray(a["x"][0].T.reshape(KT, P, TOK).transpose(1, 0, 2)), "slabs": slabs,
        "ada": np.concatenate([slabs_of(a["w_ada_2"][l]) for l in range(LAYERS)]),
        "vec1": vec1, "vec2": vec2, "c1": c1, "b_ada": feature_tiles(a["b_ada_2"]),
        "positions": np.ascontiguousarray(a["positions_2"][0]),
        "w_sgu": np.ascontiguousarray(a["ws_gmlp_2"].transpose(0, 3, 1, 2).reshape(LAYERS, P, 4 * P)),
        "b_sgu": np.ascontiguousarray(a["bs_gmlp_2"].reshape(LAYERS, 4 * P)),
        "decays": k["decays"], "tri": k["tri"], "swap": k["swap"], "ident": k["ident"], "ones": k["ones"],
        "blk": k["blk"]}


def kernel(**inputs):
    import concourse.bacc as bacc
    from concourse.bass_utils import run_bass_kernel_spmd

    nc = bacc.Bacc("TRN2", target_bir_lowering=False, num_devices=1)
    arrays, t = {}, {}
    for name, x in lay_out(inputs).items():
        arrays[f"in_{name}"] = np.ascontiguousarray(x)
        t[name] = nc.dram_tensor(f"in_{name}", x.shape, mybir.dt.from_np(x.dtype), kind="ExternalInput").ap()
    t["out"] = nc.dram_tensor("out_0", (P, KT, TOK), F32, kind="ExternalOutput").ap()
    build(nc, t)
    r = run_bass_kernel_spmd(nc, [arrays], core_ids=[0])
    out = r.results[0]["out_0"]
    return np.ascontiguousarray(out.transpose(2, 1, 0)).reshape(1, TOK, D)
```
